# Optimizing a Trainium2 kernel written in Bass

```python
import math
import jax, jax.numpy as jnp
from jax import lax
import numpy as np

D_MODEL = 1024
BATCH = 1
SEQ = 512
DEPTH = 1
DEC_BATCH = 8
DEC_SEQ = 16
PAST_LEN = 1024

CHUNK = 64
GM_CHUNK = 128
GM_HEADS = 8
GM_HEAD_DIM = 128
GM_WIDTH = GM_HEADS * GM_HEAD_DIM
SSD_HEADS = 16
SSD_HEAD_DIM = 64
SSD_WIDTH = SSD_HEADS * SSD_HEAD_DIM
SSD_GROUPS = 2
SSD_STATE = 128
CONV_W = 4
CONV_DIM = SSD_WIDTH + 2 * SSD_GROUPS * SSD_STATE
D_MIX = GM_WIDTH + SSD_WIDTH
D_IN_PROJ = 2 * GM_WIDTH + SSD_WIDTH + CONV_DIM + SSD_HEADS
D_FF = 2816
N_MOD = 9
EPS = 1e-6

kernel_name = "hymba_gmlp_ssd_macaron_adaln_stream"

def rmsnorm(x, g):
    xf = x.astype(jnp.float32)
    y = xf * lax.rsqrt(jnp.mean(xf * xf, axis=-1, keepdims=True) + EPS)
    return (y * g.astype(jnp.float32)).astype(x.dtype)

def modulate(h, shift, scale):
    return h * (1 + scale[:, None, :]) + shift[:, None, :]

def swiglu(h, w1, w2):
    g, u = jnp.split(h @ w1, 2, axis=-1)
    return (jax.nn.silu(g) * u) @ w2

def chunk_gmlp(u, v, norm_g, ws, bias):
    bsz, t_len, _ = u.shape
    L = min(GM_CHUNK, t_len)
    nc = t_len // L
    u = jax.nn.gelu(u)
    vf = jax.nn.gelu(v).astype(jnp.float32).reshape(bsz, t_len, GM_HEADS, GM_HEAD_DIM)
    mu = jnp.mean(vf, axis=-1, keepdims=True)
    vc = vf - mu
    var = jnp.mean(vc * vc, axis=-1, keepdims=True)
    vn = (vc * lax.rsqrt(var + EPS)).reshape(bsz, t_len, GM_WIDTH)
    vn = (vn * norm_g.astype(jnp.float32)).astype(u.dtype)
    mask = jnp.tril(jnp.ones((L, L), dtype=bool))
    wm = jnp.where(mask, ws[:, :L, :L], 0.0)
    vb = vn.reshape(bsz, nc, L, GM_HEADS, GM_HEAD_DIM)
    mixed = jnp.einsum('hts,bcshd->bcthd', wm, vb) + bias[:, :L].T[:, :, None]
    return u * mixed.reshape(bsz, t_len, GM_WIDTH), vn

def causal_conv(xbc, buf, w, b):
    t_len = xbc.shape[1]
    xp = jnp.concatenate([buf.astype(xbc.dtype), xbc], axis=1)
    y = sum(xp[:, k:k + t_len] * w[k] for k in range(CONV_W)) + b
    return jax.nn.silu(y), xp[:, t_len:]

def ssd_scan(x, dt, a, bm, cm, h0):
    f32 = jnp.float32
    bsz, t_len = x.shape[:2]
    L = min(CHUNK, t_len)
    nc = t_len // L
    hg = SSD_HEADS // SSD_GROUPS
    xr = x.astype(f32).reshape(bsz, nc, L, SSD_GROUPS, hg, SSD_HEAD_DIM)
    dtr = dt.astype(f32).reshape(bsz, nc, L, SSD_GROUPS, hg)
    br = bm.astype(f32).reshape(bsz, nc, L, SSD_GROUPS, SSD_STATE)
    cr = cm.astype(f32).reshape(bsz, nc, L, SSD_GROUPS, SSD_STATE)
    a_cum = jnp.cumsum(dtr * a.astype(f32).reshape(SSD_GROUPS, hg), axis=2)
    xdt = xr * dtr[..., None]
    ac = jnp.transpose(a_cum, (0, 1, 3, 4, 2))
    mask = jnp.tril(jnp.ones((L, L), dtype=bool))
    seg = ac[..., :, None] - ac[..., None, :]
    decay = jnp.exp(jnp.where(mask, seg, -jnp.inf))
    cb = jnp.einsum('bclgn,bcsgn->bcgls', cr, br)
    y_diag = jnp.einsum('bcgls,bcghls,bcsghp->bclghp', cb, decay, xdt)
    decay_states = jnp.exp(a_cum[:, :, -1:] - a_cum)
    states = jnp.einsum('bcsgn,bcsgh,bcsghp->bcghpn', br, decay_states, xdt)
    chunk_decay = jnp.exp(a_cum[:, :, -1])
    h0r = h0.astype(f32).reshape(bsz, SSD_GROUPS, hg, SSD_HEAD_DIM, SSD_STATE)

    def step(h, inp):
        st, dec = inp
        return dec[..., None, None] * h + st, h

    h_final, h_prev = lax.scan(step, h0r, (jnp.swapaxes(states, 0, 1), jnp.swapaxes(chunk_decay, 0, 1)))
    h_prev = jnp.swapaxes(h_prev, 0, 1)
    y_off = jnp.einsum('bclgn,bclgh,bcghpn->bclghp', cr, jnp.exp(a_cum), h_prev)
    y = (y_diag + y_off).reshape(bsz, t_len, SSD_HEADS, SSD_HEAD_DIM)
    return y, h_final.reshape(bsz, SSD_HEADS, SSD_HEAD_DIM, SSD_STATE)

def hybrid_mixer(h, ssm0, conv0, w_in, gm_norm_g, gm_ws, gm_b, conv_w, conv_b,
                 dt_bias, a_log, d_skip, ssd_norm_g, w_out):
    f32 = jnp.float32
    bsz, t_len, _ = h.shape
    proj = h @ w_in
    s1 = GM_WIDTH
    s2 = 2 * GM_WIDTH
    s3 = s2 + SSD_WIDTH
    s4 = s3 + CONV_DIM
    u, v, z, xbc, dt_raw = jnp.split(proj, [s1, s2, s3, s4], axis=-1)
    gm_out, gm_v = chunk_gmlp(u, v, gm_norm_g, gm_ws, gm_b)
    xbc_c, conv_new = causal_conv(xbc, conv0, conv_w, conv_b)
    xs, bm, cm = jnp.split(xbc_c, [SSD_WIDTH, SSD_WIDTH + SSD_GROUPS * SSD_STATE], axis=-1)
    xs = xs.reshape(bsz, t_len, SSD_HEADS, SSD_HEAD_DIM)
    dt = jax.nn.softplus(dt_raw.astype(f32) + dt_bias.astype(f32))
    a = -jnp.exp(a_log.astype(f32))
    y, ssm_new = ssd_scan(xs, dt, a,
                          bm.reshape(bsz, t_len, SSD_GROUPS, SSD_STATE),
                          cm.reshape(bsz, t_len, SSD_GROUPS, SSD_STATE), ssm0)
    y = y + d_skip.astype(f32)[:, None] * xs.astype(f32)
    y = y.reshape(bsz, t_len, SSD_WIDTH) * jax.nn.silu(z.astype(f32))
    y = rmsnorm(y, ssd_norm_g).astype(h.dtype)
    out = jnp.concatenate([gm_out, y], axis=-1) @ w_out
    return out, ssm_new.astype(ssm0.dtype), conv_new, gm_v

def run_trunk(x, c, ssm_init, conv_init, keep_v, w_ada, b_ada, norm_g, ffn_w1, ffn_w2, w_in,
              gm_norm_g, gm_ws, gm_b, conv_w, conv_b, dt_bias, a_log, d_skip, ssd_norm_g,
              w_out, final_norm_g, w_ada_final, b_ada_final):
    sc = jax.nn.silu(c)
    ssm_out, conv_out, v_out = [], [], []
    for l in range(DEPTH):
        mod = sc @ w_ada[l] + b_ada[l]
        sh1, sc1, g1, sh2, sc2, g2, sh3, sc3, g3 = jnp.split(mod, N_MOD, axis=-1)
        hn = modulate(rmsnorm(x, norm_g[l, 0]), sh1, sc1)
        x = x + 0.5 * g1[:, None, :] * swiglu(hn, ffn_w1[l, 0], ffn_w2[l, 0])
        hn = modulate(rmsnorm(x, norm_g[l, 1]), sh2, sc2)
        m, ssm_l, conv_l, v_l = hybrid_mixer(hn, ssm_init[l], conv_init[l], w_in[l], gm_norm_g[l],
                                             gm_ws[l], gm_b[l], conv_w[l], conv_b[l], dt_bias[l],
                                             a_log[l], d_skip[l], ssd_norm_g[l], w_out[l])
        x = x + g2[:, None, :] * m
        hn = modulate(rmsnorm(x, norm_g[l, 2]), sh3, sc3)
        x = x + 0.5 * g3[:, None, :] * swiglu(hn, ffn_w1[l, 1], ffn_w2[l, 1])
        ssm_out.append(ssm_l)
        conv_out.append(conv_l)
        if keep_v:
            v_out.append(v_l)
    shf, scf = jnp.split(sc @ w_ada_final + b_ada_final, 2, axis=-1)
    y = modulate(rmsnorm(x, final_norm_g), shf, scf)
    v_stack = jnp.stack(v_out) if keep_v else None
    return y, jnp.stack(ssm_out), jnp.stack(conv_out), v_stack

def setup_inputs(seed: int = 0) -> dict:
    key = jax.random.key(seed)
    ks = jax.random.split(key, 25)
    f32 = jnp.float32

    def nrm(k, shape, s):
        return jax.random.normal(k, shape, f32) * s

    dt0 = jnp.exp(jax.random.uniform(ks[17], (DEPTH, SSD_HEADS), f32, math.log(1e-3), math.log(1e-1)))
    return {
        "x_prompt": nrm(ks[0], (BATCH, SEQ, D_MODEL), 1.0),
        "x_sample": nrm(ks[1], (DEC_BATCH, DEC_SEQ, D_MODEL), 1.0),
        "state_ssm": nrm(ks[2], (DEPTH, DEC_BATCH, SSD_HEADS, SSD_HEAD_DIM, SSD_STATE), 0.1),
        "state_conv": nrm(ks[3], (DEPTH, DEC_BATCH, CONV_W - 1, CONV_DIM), 0.5),
        "c_prompt": nrm(ks[4], (BATCH, D_MODEL), 1.0),
        "c_sample": nrm(ks[5], (DEC_BATCH, D_MODEL), 1.0),
        "w_ada": nrm(ks[6], (DEPTH, D_MODEL, N_MOD * D_MODEL), 0.5 * D_MODEL ** -0.5),
        "b_ada": nrm(ks[7], (DEPTH, N_MOD * D_MODEL), 0.02),
        "norm_g": 1.0 + nrm(ks[8], (DEPTH, 3, D_MODEL), 0.02),
        "ffn_w1": nrm(ks[9], (DEPTH, 2, D_MODEL, 2 * D_FF), D_MODEL ** -0.5),
        "ffn_w2": nrm(ks[10], (DEPTH, 2, D_FF, D_MODEL), D_FF ** -0.5),
        "w_in": nrm(ks[11], (DEPTH, D_MODEL, D_IN_PROJ), D_MODEL ** -0.5),
        "gm_norm_g": 1.0 + nrm(ks[12], (DEPTH, GM_WIDTH), 0.02),
        "gm_ws": nrm(ks[13], (DEPTH, GM_HEADS, GM_CHUNK, GM_CHUNK), GM_CHUNK ** -0.5),
        "gm_b": 1.0 + nrm(ks[14], (DEPTH, GM_HEADS, GM_CHUNK), 0.02),
        "conv_w": nrm(ks[15], (DEPTH, CONV_W, CONV_DIM), CONV_W ** -0.5),
        "conv_b": nrm(ks[16], (DEPTH, CONV_DIM), 0.02),
        "dt_bias": dt0 + jnp.log(-jnp.expm1(-dt0)),
        "a_log": jnp.log(jax.random.uniform(ks[18], (DEPTH, SSD_HEADS), f32, 1.0, 16.0)),
        "d_skip": 1.0 + nrm(ks[19], (DEPTH, SSD_HEADS), 0.1),
        "ssd_norm_g": 1.0 + nrm(ks[20], (DEPTH, SSD_WIDTH), 0.02),
        "w_out": nrm(ks[21], (DEPTH, D_MIX, D_MODEL), D_MIX ** -0.5),
        "final_norm_g": 1.0 + nrm(ks[22], (D_MODEL,), 0.02),
        "w_ada_final": nrm(ks[23], (D_MODEL, 2 * D_MODEL), 0.5 * D_MODEL ** -0.5),
        "b_ada_final": nrm(ks[24], (2 * D_MODEL,), 0.02),
    }

def reference(x_prompt, x_sample, state_ssm, state_conv, c_prompt, c_sample, w_ada, b_ada, norm_g,
              ffn_w1, ffn_w2, w_in, gm_norm_g, gm_ws, gm_b, conv_w, conv_b, dt_bias, a_log, d_skip,
              ssd_norm_g, w_out, final_norm_g, w_ada_final, b_ada_final):
    params = (w_ada, b_ada, norm_g, ffn_w1, ffn_w2, w_in, gm_norm_g, gm_ws, gm_b, conv_w, conv_b,
              dt_bias, a_log, d_skip, ssd_norm_g, w_out, final_norm_g, w_ada_final, b_ada_final)
    bp = x_prompt.shape[0]
    ssm0 = jnp.zeros((DEPTH, bp, SSD_HEADS, SSD_HEAD_DIM, SSD_STATE), state_ssm.dtype)
    conv0 = jnp.zeros((DEPTH, bp, CONV_W - 1, CONV_DIM), state_conv.dtype)
    y_prompt, ssm_prompt, conv_prompt, _ = run_trunk(x_prompt, c_prompt, ssm0, conv0, False, *params)
    y_sample, ssm_sample, conv_sample, gm_v_sample = run_trunk(x_sample, c_sample, state_ssm, state_conv,
                                                               True, *params)
    return (y_prompt, y_sample, ssm_prompt, conv_prompt, ssm_sample, conv_sample, gm_v_sample)


_drawn_inputs = setup_inputs


def setup_inputs(seed=0):
    import zlib

    import numpy as np

    out = dict(_drawn_inputs(seed))
    spreads = {}
    factors = {'gm_norm_g': 8.398,
     'gm_b': 46.035,
     'd_skip': 5.295,
     'ssd_norm_g': 32.939,
     'final_norm_g': 2.875,
     'b_ada_final': 2.833}
    for name, (base, spread) in spreads.items():
        noise = np.random.default_rng([zlib.crc32(name.encode()), seed]).standard_normal(out[name].shape)
        drawn = base * np.exp(spread * noise) if base else spread * noise
        out[name] = __import__('jax').numpy.asarray(drawn.astype(out[name].dtype))
    for name, factor in factors.items():
        out[name] = (out[name] * factor).astype(out[name].dtype)
    return out
```

```python
import math
from contextlib import ExitStack, contextmanager

import concourse.bass as bass
from concourse import mybir

F32 = mybir.dt.float32
F32R = mybir.dt.float32r
ACT = mybir.ActivationFunctionType
ALU = mybir.AluOpType
AX = mybir.AxisListType

P = 128
D_MODEL = 1024
SEQ = 512
DEC_BATCH = 8
DEC_SEQ = 16
TOK = SEQ + DEC_BATCH * DEC_SEQ
HALF = TOK // 2
BANK = 512
TT = TOK // P
ST = TT - 1
KD = D_MODEL // P
NSTR = 1 + DEC_BATCH
GRP = TOK // DEC_SEQ
D_FF = 2816
FF_TILES = D_FF // P
PARTS = 2
KH = FF_TILES // PARTS
HEADS = 16
HDIM = 64
NSTATE = 128
SSD_G = 2
HG = HEADS // SSD_G
CONV_W = 4
CONV_DIM = D_MODEL + 2 * SSD_G * NSTATE
CT = CONV_DIM // P
XT_ = D_MODEL // P
D_IN = 4 * D_MODEL + 2 * SSD_G * NSTATE + HEADS
COL_U, COL_V, COL_Z, COL_X = 0, D_MODEL, 2 * D_MODEL, 3 * D_MODEL
COL_DT = D_IN - P
N_MOD = 9
MODT = (N_MOD + 2) * KD
EPS = 1e-6
HP = HEADS * HDIM // P
PAD_P = SEQ + CONV_W - 1
PAD_S = DEC_SEQ + CONV_W - 1
PAD = PAD_P + DEC_BATCH * PAD_S
CONV_N = PAD - (CONV_W - 1)
TAIL = NSTR * (CONV_W - 1)

R_NORM, R_FINAL, R_SSDN, R_CW, R_CB = 0, 24, 32, 40, 40 + CONV_W * CT
N_PAR = R_CB + CT

ADA_COLS = 256
ADA_CHUNKS = MODT * P // ADA_COLS
ADA_MAIN = N_MOD * D_MODEL // ADA_COLS
ADA_RING = 4


def trunk_program(nc, x_prompt, x_sample, state_ssm, state_conv, c_prompt, c_sample, w_ada, b_ada, norm_g,
                  ffn_w1, ffn_w2, w_in, gm_norm_g, gm_ws, gm_b, conv_w, conv_b, dt_bias, a_log, d_skip,
                  ssd_norm_g, w_out, final_norm_g, w_ada_final, b_ada_final,
                  y_prompt, y_sample, ssm_prompt, conv_prompt, ssm_sample, conv_sample, gm_v_sample):
    top = ExitStack()

    def sb(name, shape, dt=F32, stack=None):
        return (stack or top).enter_context(nc.sbuf_tensor(name, shape, dt))

    def ps(name, cols):
        return top.enter_context(nc.psum_tensor(name, [P, cols], F32))

    def sem(name):
        return top.enter_context(nc.semaphore(name))

    xT = sb("xT", [P, KD * TOK])
    hn_hi = sb("hn_hi", [P, KD * TOK], F32R)
    hn_lo = sb("hn_lo", [P, KD * TOK], F32R)
    wraw = [sb(f"wraw{i}", [P, KH * P]) for i in range(2)]
    whi = [sb(f"whi{i}", [P, KH * P], F32R) for i in range(2)]
    wlo = [sb(f"wlo{i}", [P, KH * P], F32R) for i in range(2)]
    modc = sb("modc", [P, MODT, NSTR])
    gate = sb("gate", [P, 3, KD * GRP])
    par = sb("par", [P, N_PAR])
    ident = sb("ident", [P, P])
    ones_mean = sb("ones_mean", [P, P])
    ones = sb("ones", [P, P])
    upto = sb("upto", [P, 2, P])
    after = sb("after", [P, 2, P])
    stream_of = sb("stream_of", [P, DEC_BATCH])
    rT = sb("rT", [P, TOK])
    ssum = sb("ssum", [P, TOK])
    sq = sb("sq", [P, TOK])
    tmp = [sb(f"tmp{i}", [P, TOK]) for i in range(2)]
    tms = [sb(f"tms{i}", [P, P]) for i in range(2)]
    xadd = sb("xadd", [P, TOK])
    eps_t = sb("eps_t", [P, 1])
    vecs = sb("vecs", [P, 3, HEADS])

    reg = ExitStack()
    ada_raw = [sb(f"ada_raw{i}", [P, KD * ADA_COLS], stack=reg) for i in range(ADA_RING)]
    ada_hi = [sb(f"ada_hi{i}", [P, KD * ADA_COLS], F32R, reg) for i in range(2)]
    ada_lo = [sb(f"ada_lo{i}", [P, KD * ADA_COLS], F32R, reg) for i in range(2)]
    c_row = sb("c_row", [NSTR, D_MODEL], stack=reg)
    c_sil = sb("c_sil", [NSTR, D_MODEL], stack=reg)
    c_hl = sb("c_hl", [P, KD, 2 * NSTR], F32R, reg)
    b_row = sb("b_row", [MODT, P], stack=reg)
    b_col = sb("b_col", [P, MODT], stack=reg)
    p_row = sb("p_row", [N_PAR, P], stack=reg)
    x_row = [sb(f"x_row{i}", [P, D_MODEL], stack=reg) for i in range(2)]
    reg.close()
    reg = ExitStack()
    hid_hi = sb("hid_hi", [P, KH * TOK], F32R, reg)
    hid_lo = sb("hid_lo", [P, KH * TOK], F32R, reg)
    silg = sb("silg", [P, TOK], stack=reg)
    hidp = sb("hidp", [P, TOK], stack=reg)
    reg.close()
    reg = ExitStack()
    ytm = sb("ytm", [P, TT * D_MODEL], stack=reg)
    sub = ExitStack()
    bcf = sb("bcf", [P, 4, TOK], stack=sub)
    btm = sb("btm", [P, TT, SSD_G * NSTATE], stack=sub)
    dt_z = sb("dt_z", [P, TT * HEADS], stack=sub)
    dt_e = sb("dt_e", [P, TT * HEADS], stack=sub)
    dt_v = sb("dt_v", [P, TT * HEADS], stack=sub)
    dt_a = sb("dt_a", [P, TT * HEADS], stack=sub)
    expo = sb("expo", [P, 3, TT * HEADS], stack=sub)
    conv_mem = ExitStack()
    tails = sb("tails", [P, CT, TAIL], stack=conv_mem)
    stT = sb("stT", [P, CT, TAIL - 3], stack=conv_mem)
    st_row = sb("st_row", [TAIL - 3, CONV_DIM], stack=conv_mem)
    tail_row = sb("tail_row", [TAIL, CONV_DIM], stack=conv_mem)
    xpad = [sb(f"xpad{i}", [P, PAD], stack=conv_mem) for i in range(2)]
    cacc = sb("cacc", [P, PAD], stack=conv_mem)
    conv_mem.close()
    hst = sb("hst", [P, HEADS * HDIM], stack=sub)
    wd = sb("wd", [P, HG, P], stack=sub)
    gd = sb("gd", [P, HG, P], stack=sub)
    cbm = sb("cbm", [P, P], stack=sub)
    xdt = sb("xdt", [P, HG * HDIM], stack=sub)
    xds = sb("xds", [P, HG * HDIM], stack=sub)
    yt1 = sb("yt1", [P, HG * HDIM], stack=sub)
    yt2 = sb("yt2", [P, HG * HDIM], stack=sub)
    h0s = [sb(f"h0s{i}", [P, DEC_BATCH, NSTATE], stack=sub) for i in range(2)]
    h0T = sb("h0T", [P, DEC_BATCH, P], stack=sub)
    decs = sb("decs", [P, HP, DEC_BATCH], stack=sub)
    yoT = sb("yoT", [P, P], stack=sub)
    sub.close()
    sub = ExitStack()
    gm_hi = sb("gm_hi", [P, KD * TOK], F32R, sub)
    gm_lo = sb("gm_lo", [P, KD * TOK], F32R, sub)
    wmT = sb("wmT", [P, 2, 8 * P], stack=sub)
    wst = sb("wst", [P, 8, P], stack=sub)
    gm_g = sb("gm_g", [P, D_MODEL], stack=sub)
    gm_bias = sb("gm_bias", [P, 8 * P], stack=sub)
    stat = sb("stat", [P, 4, TT], stack=sub)
    gu = sb("gu", [P, TOK], stack=sub)
    gmp = sb("gmp", [P, TOK], stack=sub)
    sub.close()
    reg.close()
    reg = ExitStack()
    y_row = sb("y_row", [P, TT, D_MODEL], stack=reg)
    y_fm = [sb(f"y_fm{i}", [P, TOK], stack=reg) for i in range(2)]
    reg.close()

    acc = [ps("acc0", 2 * BANK), ps("acc1", 2 * BANK)]
    pB = ps("pB", 2 * BANK)
    pC = ps("pC", 2 * BANK)

    setup_in = sem("setup_in")
    vecs_in = sem("vecs_in")
    x_in = [sem(f"x_in{i}") for i in range(2)]
    masks_done = sem("masks_done")
    pool_step, act_step, dve_step = sem("pool_step"), sem("act_step"), sem("dve_step")
    c_silu = sem("c_silu")
    c_tr, c_used, c_split = sem("c_tr"), sem("c_used"), sem("c_split")
    par_tr, par_done = sem("par_tr"), sem("par_done")
    xt_tr, xt_done = sem("xt_tr"), sem("xt_done")
    ada_in = [sem(f"ada_in{i}") for i in range(ADA_RING)]
    ada_hi_done, ada_lo_done = sem("ada_hi_done"), sem("ada_lo_done")
    ada_mm, ada_used = sem("ada_mm"), sem("ada_used")
    mod_ready = sem("mod_ready")
    w_in_sb = [sem(f"w_in_sb{i}") for i in range(2)]
    whi_done, wlo_done = sem("whi_done"), sem("wlo_done")
    unit_done = sem("unit_done")
    acc_free = [sem(f"acc_free{i}") for i in range(2)]
    sq_ready, sq_added = sem("sq_ready"), sem("sq_added")
    x_ready = sem("x_ready")
    rms_mm, rms_sqrt, rinv_ready = sem("rms_mm"), sem("rms_sqrt"), sem("rinv_ready")
    prod_ready, tms_ready, nhi_ready, hn_ready = sem("prod_ready"), sem("tms_ready"), sem("nhi_ready"), sem("hn_ready")
    silg_ready, hidp_ready, hhi_ready, hid_ready = sem("silg_ready"), sem("hidp_ready"), sem("hhi_ready"), sem("hid_ready")
    st_in, st_tr, st_done = sem("st_in"), sem("st_tr"), sem("st_done")
    dt_row_ready, dt_tr, dt_z_ready, dt_e_ready, dta_ready = (
        sem("dt_row_ready"), sem("dt_tr"), sem("dt_z_ready"), sem("dt_e_ready"), sem("dta_ready"))
    sums_mm, expo_ready = sem("sums_mm"), sem("expo_ready")
    pad0_ready, xpad_ready, conv_done, xcv_ready = sem("pad0_ready"), sem("xpad_ready"), sem("conv_done"), sem("xcv_ready")
    conv_tr, conv_tr_used = sem("conv_tr"), sem("conv_tr_used")
    tail_tr, tail_done, tail_out = sem("tail_tr"), sem("tail_done"), sem("tail_out")
    wd_ready, seg_done, cb_done, gexp_done, cbm_done = (
        sem("wd_ready"), sem("seg_done"), sem("cb_done"), sem("gexp_done"), sem("cbm_done"))
    g_ready, y_mm, st_mm, y_done = sem("g_ready"), sem("y_mm"), sem("st_mm"), sem("y_done")
    hst_ready = sem("hst_ready")
    hout_tr, hout_ready, hout_out = sem("hout_tr"), sem("hout_ready"), sem("hout_out")
    h0_in = [sem(f"h0_in{i}") for i in range(2)]
    h0_tr, h0T_ready, yo_mm, yoT_ready, yo_tr, h1_mm, h1_ready = (
        sem("h0_tr"), sem("h0T_ready"), sem("yo_mm"), sem("yoT_ready"), sem("yo_tr"), sem("h1_mm"), sem("h1_ready"))
    h1_out = [sem(f"h1_out{i}") for i in range(2)]
    bblk_ready = sem("bblk_ready")
    ssd_over = sem("ssd_over")
    ws_zero, ws_in, ws_blk_in, gm_vec_in = sem("ws_zero"), sem("ws_in"), sem("ws_blk_in"), sem("gm_vec_in")
    ws_tr, wm_ready = sem("ws_tr"), sem("wm_ready")
    gv_ready, vt_tr, vc_ready, vsq_ready, vvar_ready, vstd_ready, vn_ready, v_out = (
        sem("gv_ready"), sem("vt_tr"), sem("vc_ready"), sem("vsq_ready"), sem("vvar_ready"), sem("vstd_ready"),
        sem("vn_ready"), sem("v_out"))
    mix_mm, mix_used, gu_ready, gmp_ready, gmhi_ready, gm_ready = (
        sem("mix_mm"), sem("mix_used"), sem("gu_ready"), sem("gmp_ready"), sem("gmhi_ready"), sem("gm_ready"))
    _unused_sz, yt_tr, yz_ready = sem("sz_ready"), sem("yt_tr"), sem("yz_ready")
    yp_ready, yhi_ready, yfm_split = sem("yp_ready"), sem("yhi_ready"), sem("yfm_split")
    of_ready, of_tr, of_done, y_out = sem("of_ready"), sem("of_tr"), sem("of_done"), sem("y_out")

    def halves(t):
        return t[:, :].rearrange("p (h x) -> p h x", h=2)[:, :, 0:HALF]

    def split2(ap):
        return ap.rearrange("p (h x) -> p h x", h=2)

    def tile(t, f):
        return t[:, bass.ds(f * TOK, TOK)]

    def kxn(w, k, n):
        return w[:, 0:k * n].rearrange("p (k n) -> p k n", n=n)

    def mod40(q, f):
        g = gate[:, q, bass.ds(f * GRP, GRP)]
        return g.rearrange("p (h g) -> p h g", h=2).unsqueeze(3).broadcast_to([P, 2, GRP // 2, DEC_SEQ])

    def by_group(ap3):
        return ap3.rearrange("p h (g t) -> p h g t", t=DEC_SEQ)

    def by_stream(ap, n=DEC_SEQ):
        return ap.rearrange("p (b t) -> p b t", t=n)

    ytm3 = ytm[:, :].rearrange("p (c n) -> p c n", c=TT)
    w1 = ffn_w1[0].rearrange("a (k p) n -> a p k n", p=P)
    w2 = ffn_w2[0].rearrange("a (k p) n -> a p k n", p=P)
    win = w_in[0].rearrange("(k p) n -> p k n", p=P)
    wout = w_out[0].rearrange("(k p) n -> p k n", p=P)
    wada = w_ada[0].rearrange("(k p) n -> p k n", p=P)
    wadaf = w_ada_final.rearrange("(k p) n -> p k n", p=P)
    ws_t = gm_ws[0].rearrange("h t s -> t h s")
    h0_d = state_ssm[0].rearrange("b (j h) p n -> j (h p) b n", h=2)
    h1_d = ssm_sample[0].rearrange("b (j h) p n -> j (h p) b n", h=2)
    hp_d = ssm_prompt[0, 0].rearrange("(j h) p n -> (h p) j n", h=2)

    ffn_units = PARTS * (2 * KH + KD)
    U_F0 = 0
    U_DT = ffn_units
    U_X = U_DT + 1
    U_V = U_X + CT
    U_Z = U_V + 2 * KD
    U_OG = U_Z + KD
    U_OY = U_OG + KD
    U_F1 = U_OY + KD
    U_END = U_F1 + ffn_units

    def unit_tiles(n, i=0):
        n += 2 * i if isinstance(i, int) else 0
        for base in (U_F0, U_F1):
            if base <= n < base + ffn_units and (n - base) % (2 * KH + KD) >= 2 * KH:
                return KH
        return KD

    class Steps:

        def __init__(self, eng, s):
            self.eng, self.s, self.n, self.i, self.start, self.per = eng, s, 0, None, 0, 0

        def done(self, ins):
            ins.then_inc(self.s, 1)
            self.n += 1
            v = self.n if self.i is None else self.i * self.per + (self.n - self.start * self.per)
            self.eng.wait_ge(self.s, v)

    def repeat(eng, steps, per, start, stop, body):
        if stop - start == 1:
            body(start)
            return
        with eng.Fori(start, stop) as i:
            n0 = steps.n if steps else 0
            if steps:
                steps.i, steps.start, steps.per = i, start, per
            body(i)
            if steps:
                assert steps.n - n0 == per, (steps.n - n0, per)
                steps.n = n0 + per * (stop - start)
                steps.i = None

    def after_first(i):
        return not isinstance(i, int) or i > 0

    def repeat_peeled(eng, stop, body, n):
        if n == 0:
            body(0)
        repeat(eng, None, 0, int(n == 0), stop, body)

    def evacuated(eng, n, i=0):
        eng.wait_ge(acc_free[n % 2], i + (n // 2 + 1))

    def all_evacuated(eng, p, n):
        eng.wait_ge(acc_free[p], (n + 1 - p) // 2)

    def wait(eng, s, v):
        if not isinstance(v, int) or v > 0:
            eng.wait_ge(s, v)

    block = top.enter_context(nc.Block())

    @block.sync
    def _(sp):
        def first_col(col):
            return col if isinstance(col, int) else sp.snap(col)

        def load_unit(n, i, rows, col):
            col = first_col(col)
            wait(sp, wlo_done, n - 1 + i * 2)
            k = unit_tiles(n, i)
            sp.dma_start(kxn(wraw[n % 2], k, P), rows[:, :, bass.ds(col, P)]).then_inc(w_in_sb[n % 2], 16)

        def load_ffn(u0, a):
            for part in range(PARTS):
                n = u0 + part * (2 * KH + KD)

                def pair(i, n=n, part=part):
                    load_unit(n, i, w1[a], i * P + part * KH * P)
                    load_unit(n + 1, i, w1[a], i * P + (D_FF + part * KH * P))
                repeat_peeled(sp, KH, pair, n)
                n += 2 * KH

                def down(i, n=n, part=part):
                    for d in range(2):
                        load_unit(n + d, i, w2[a, :, part * KH:(part + 1) * KH, :], i * (2 * P) + d * P)
                repeat(sp, None, 0, 0, KD // 2, down)

        def load_two(n, src, col):
            def two(i):
                for d in range(2):
                    load_unit(n + d, i, src, i * (2 * P) + (col + d * P))
            return two

        sp.dma_start(c_row[0:1, :], c_prompt).then_inc(setup_in, 16)
        sp.dma_start(c_row[1:NSTR, :], c_sample).then_inc(setup_in, 16)
        sp.dma_start(b_row[0:N_MOD * KD, :], b_ada[0].rearrange("(r c) -> r c", c=P)).then_inc(setup_in, 16)
        sp.dma_start(b_row[N_MOD * KD:MODT, :], b_ada_final.rearrange("(r c) -> r c", c=P)).then_inc(setup_in, 16)
        for r, src in ((R_NORM, norm_g[0].rearrange("a (r c) -> (a r) c", c=P)),
                       (R_FINAL, final_norm_g.rearrange("(r c) -> r c", c=P)),
                       (R_SSDN, ssd_norm_g[0].rearrange("(r c) -> r c", c=P)),
                       (R_CW, conv_w[0].rearrange("a (r c) -> (a r) c", c=P)),
                       (R_CB, conv_b[0].rearrange("(r c) -> r c", c=P))):
            sp.dma_start(p_row[r:r + src.shape[0], :], src).then_inc(setup_in, 16)
        for q, src in enumerate((dt_bias, a_log, d_skip)):
            sp.dma_start(vecs[:, q, :], src[0].partition_broadcast(P)).then_inc(vecs_in, 16)
        for c in range(TT):
            wait(sp, xt_tr, c - 1)
            src = x_prompt[0, c * P:(c + 1) * P, :] if c < ST else x_sample.rearrange("b t d -> (b t) d")
            sp.dma_start(x_row[c % 2][:, :], src).then_inc(x_in[c % 2], 16)

        def ada_body(src, first):
            def body(i):
                for s in range(ADA_RING):
                    col = first_col(i * (ADA_RING * ADA_COLS) + s * ADA_COLS)
                    wait(sp, ada_lo_done, i * ADA_RING + (first + s + 1 - ADA_RING))
                    sp.dma_start(kxn(ada_raw[s], KD, ADA_COLS),
                                 src[:, :, bass.ds(col, ADA_COLS)]
                                 ).then_inc(ada_in[s], 16)
            return body
        ada_body(wada, 0)(0)
        repeat(sp, None, 0, 1, ADA_MAIN // ADA_RING, ada_body(wada, 0))
        repeat(sp, None, 0, 0, (ADA_CHUNKS - ADA_MAIN) // ADA_RING, ada_body(wadaf, ADA_MAIN))

        load_ffn(U_F0, 0)
        load_unit(U_DT, 0, win, COL_DT)
        sp.wait_ge(unit_done, U_DT)
        sp.dma_start(st_row[:, :], state_conv[0].rearrange("b k c -> (b k) c")).then_inc(st_in, 16)
        repeat(sp, None, 0, 0, CT // 2, load_two(U_X, win, COL_X))
        for d, col in ((0, COL_V), (1, COL_U)):
            load_unit(U_V + d, 0, win, col)

        sp.wait_ge(ssd_over, 1)
        sp.wait_ge(hout_out, 16)
        for b in range(2):
            sp.wait_ge(h1_out[b], 16 * HP // 2)
        sp.dma_start(wst[:, :, :], ws_t).then_inc(ws_in, 16)
        sp.dma_start(gm_g[:, :], gm_norm_g[0].partition_broadcast(P)).then_inc(gm_vec_in, 16)
        sp.dma_start(gm_bias[:, :], gm_b[0].rearrange("h t -> (h t)").partition_broadcast(P)).then_inc(gm_vec_in, 16)
        sp.wait_ge(ws_zero, 1)
        for b in range(DEC_BATCH):
            r = slice(b * DEC_SEQ, (b + 1) * DEC_SEQ)
            sp.dma_start(wst[r, :, r], ws_t[0:DEC_SEQ, :, 0:DEC_SEQ]).then_inc(ws_blk_in, 16)

        def vu(i):
            load_unit(U_V + 2, i, win, i * P + (COL_V + P))
            load_unit(U_V + 3, i, win, i * P + (COL_U + P))
        repeat(sp, None, 0, 0, KD - 1, vu)
        repeat(sp, None, 0, 0, KD // 2, load_two(U_Z, win, COL_Z))
        repeat(sp, None, 0, 0, KD // 2, load_two(U_OG, wout[:, 0:KD, :], 0))
        repeat(sp, None, 0, 0, KD // 2, load_two(U_OY, wout[:, KD:2 * KD, :], 0))
        load_ffn(U_F1, 1)

    @block.gpsimd
    def _(pool):
        st = Steps(pool, pool_step)

        def select(t, pattern, mult, base):
            st.done(nc.gpsimd.affine_select(out=t, in_=t, pattern=pattern, compare_op=ALU.is_ge, fill=0.0,
                                            base=base, channel_multiplier=mult))
        st.done(nc.gpsimd.memset(ident[:, :], 0.0))
        st.done(nc.gpsimd.affine_select(out=ident[:, :], in_=ident[:, :], pattern=[[-1, P]],
                                        compare_op=ALU.not_equal, fill=1.0, base=0, channel_multiplier=1))
        nc.gpsimd.memset(ones[:, :], 1.0)
        nc.gpsimd.memset(ones_mean[:, :], 1.0 / D_MODEL)
        nc.gpsimd.memset(eps_t[:, :], EPS)
        nc.gpsimd.memset(upto[:, :, :], 1.0)
        nc.gpsimd.memset(after[:, :, :], 1.0)
        st.done(nc.gpsimd.memset(stream_of[:, :], 1.0))
        select(upto[:, :, :], [[0, 2], [1, P]], -1, 0)
        select(after[:, :, :], [[0, 2], [-1, P]], 1, -1)
        for t in (upto, after):
            v = t[:, 1, :].rearrange("p (b t) -> p b t", t=DEC_SEQ)
            select(v, [[-DEC_SEQ, DEC_BATCH], [0, DEC_SEQ]], 1, 0)
            select(v, [[DEC_SEQ, DEC_BATCH], [0, DEC_SEQ]], -1, DEC_SEQ - 1)
        select(stream_of[:, :], [[-DEC_SEQ, DEC_BATCH]], 1, 0)
        select(stream_of[:, :], [[DEC_SEQ, DEC_BATCH]], -1, DEC_SEQ - 1)
        nc.gpsimd.memset(ident[0:1, 0:1], 1.0).then_inc(masks_done, 1)

        def norm_samples(m, used0, shift, scale):
            pool.wait_ge(rinv_ready, m + 1)
            pool.wait_ge(mod_ready, 1)
            for f in range(KD):
                t = tms[f % 2]
                if f >= 2:
                    used0(f - 2)
                tv = by_stream(t[:, :])
                st.done(nc.gpsimd.tensor_tensor(out=t[:, :], in0=xT[:, f * TOK + SEQ:(f + 1) * TOK],
                                                in1=rT[:, SEQ:TOK], op=ALU.mult))
                for op, q in ((ALU.mult, scale), (ALU.add, shift)):
                    v = modc[:, q + f, 1:NSTR].unsqueeze(2).broadcast_to([P, DEC_BATCH, DEC_SEQ])
                    ins = nc.gpsimd.tensor_tensor(out=tv, in0=tv, in1=v, op=op)
                    if op == ALU.mult:
                        st.done(ins)
                ins.then_inc(tms_ready, 1)

        norm_samples(0, lambda f: pool.wait_ge(hn_ready, f + 1), 0, KD)
        pool.wait_ge(unit_done, U_DT)
        for i in range(2):
            nc.gpsimd.memset(xpad[i][:, 0:CONV_W - 1], 0.0).then_inc(pad0_ready, 1)
        norm_samples(1, lambda f: pool.wait_ge(hn_ready, KD + f + 1), 3 * KD, 4 * KD)

        pool.wait_ge(tail_done, 1)
        pool.dma_start(conv_prompt[0, 0], tail_row[0:CONV_W - 1, :]).then_inc(tail_out, 16)
        pool.dma_start(conv_sample[0].rearrange("b k c -> (b k) c"), tail_row[CONV_W - 1:TAIL, :]).then_inc(tail_out, 16)
        pool.wait_ge(tail_out, 32)
        for j in range(2):
            pool.dma_start(h0s[j][:, :, :], h0_d[j]).then_inc(h0_in[j], 16)
        pool.wait_ge(hout_ready, 1)
        pool.dma_start(hp_d, h0T[:, :, :]).then_inc(hout_out, 16)
        for j in range(HP):
            pool.wait_ge(h1_ready, j + 1)
            pool.dma_start(h1_d[j], h0s[j % 2][:, :, :]).then_inc(h1_out[j % 2], 16)
            if j + 2 < HP:
                pool.wait_ge(h1_out[j % 2], 16 * (j // 2 + 1))
                pool.dma_start(h0s[j % 2][:, :, :], h0_d[j + 2]).then_inc(h0_in[j % 2], 16)
        def v_store(i):
            pool.wait_ge(vn_ready, i + 1)
            pool.dma_start(gm_v_sample[0].rearrange("b t d -> (b t) d")[:, bass.ds(i * P, P)],
                           xadd[:, ST * P:TT * P]).then_inc(v_out, 16)
        repeat(pool, None, 0, 0, KD, v_store)
        pool.wait_ge(v_out, 16 * KD)
        norm_samples(3, lambda f: pool.wait_ge(hn_ready, 2 * KD + f + 1), 6 * KD, 7 * KD)
        norm_samples(4, lambda f: pool.wait_ge(of_ready, f + 1), 9 * KD, 10 * KD)
        for f in range(KD):
            pool.wait_ge(of_done, f + 1)
            cols = slice(f * P, (f + 1) * P)
            pool.dma_start(y_prompt[0].rearrange("(c p) d -> p c d", p=P)[:, :, cols],
                           y_row[:, 0:ST, cols]).then_inc(y_out, 16)
            pool.dma_start(y_sample.rearrange("b t d -> (b t) d")[:, cols], y_row[:, ST, cols]).then_inc(y_out, 16)
        pool.wait_ge(y_out, 2 * 16 * KD)

    @block.tensor
    def _(pe):
        mm = nc.tensor.matmul

        def unit(n, i, hi, lo, k_ready):
            p, kt = n % 2, unit_tiles(n, i)
            wh, wl = kxn(whi[p], kt, P), kxn(wlo[p], kt, P)
            pe.wait_ge(wlo_done, i * 2 + (n + 1))
            wait(pe, acc_free[p], i + n // 2)
            for k in range(kt):
                k_ready(k)
                for t, (w, a) in enumerate(((wh, hi), (wh, lo), (wl, hi))):
                    for h in range(2):
                        last = mm(acc[p][:, h * BANK:h * BANK + HALF], w[:, k, :],
                                  a[:, k * TOK + h * HALF:k * TOK + (h + 1) * HALF],
                                  start=(k == 0 and t == 0), stop=(k == kt - 1 and t == 2))
            last.then_inc(unit_done, 1)

        def hn_wait(m):
            return lambda k: pe.wait_ge(hn_ready, m * KD + k + 1)

        def rms(m):
            pe.wait_ge(sq_added, (m + 1) * KD)
            for h in range(2):
                last = mm(pC[:, h * BANK:h * BANK + HALF], ones_mean[:, :], ssum[:, h * HALF:(h + 1) * HALF],
                          start=True, stop=True)
            last.then_inc(rms_mm, 1)

        def to_tokens(out, src, used, v):
            wait(pe, used, v)
            for c in range(TT):
                last = nc.tensor.transpose(out[:, c * P:(c + 1) * P], src[:, c * P:(c + 1) * P], ident[:, :])
            return last

        pe.wait_ge(masks_done, 1)
        pe.wait_ge(c_silu, 1)
        for k in range(KD):
            last = mm(pB[:, k * NSTR:(k + 1) * NSTR], c_sil[0:NSTR, k * P:(k + 1) * P], ident[0:NSTR, 0:NSTR],
                      start=True, stop=True)
        last.then_inc(c_tr, 1)
        mm(pB[:, BANK:BANK + MODT], b_row[0:MODT, :], ident[0:MODT, 0:MODT], start=True, stop=True)
        mm(pB[:, BANK + P:BANK + P + N_PAR], p_row[0:N_PAR, :], ident[0:N_PAR, 0:N_PAR],
           start=True, stop=True).then_inc(par_tr, 1)
        for c in range(TT):
            pe.wait_ge(x_in[c % 2], 16 * (c // 2 + 1))
            wait(pe, xt_done, c - 1)
            for f in range(KD):
                last = nc.tensor.transpose(acc[c % 2][:, f * P:(f + 1) * P], x_row[c % 2][:, f * P:(f + 1) * P],
                                           ident[:, :])
            last.then_inc(xt_tr, 1)

        pe.wait_ge(c_split, 1)

        def ada(i, s):
            pe.wait_ge(ada_lo_done, i * ADA_RING + (s + 1))
            wait(pe, ada_used, i * ADA_RING + (s - 1))
            wh, wl = kxn(ada_hi[s % 2], KD, ADA_COLS), kxn(ada_lo[s % 2], KD, ADA_COLS)
            for ft in range(ADA_COLS // P):
                o = (s % 2) * BANK + ft * 2 * NSTR
                for k in range(KD):
                    for t, w in enumerate((wh, wl)):
                        last = mm(pC[:, o:o + 2 * NSTR], w[:, k, ft * P:(ft + 1) * P], c_hl[:, k, :],
                                  start=(k == 0 and t == 0), stop=(k == KD - 1 and t == 1))
            last.then_inc(ada_mm, 1)

        def ada_ring(i):
            for s in range(ADA_RING):
                ada(i, s)
        ada_ring(0)
        repeat(pe, None, 0, 1, ADA_CHUNKS // ADA_RING, ada_ring)
        pe.wait_ge(ada_used, ADA_CHUNKS)

        def ffn(u0, m, part0):
            for part in range(PARTS):
                n = u0 + part * (2 * KH + KD)

                def pair(i, n=n):
                    unit(n, i, hn_hi, hn_lo, hn_wait(m))
                    unit(n + 1, i, hn_hi, hn_lo, lambda k: None)
                repeat_peeled(pe, KH, pair, n)

                def hid_wait(k, have=(part0 + part) * KH):
                    if k in (0, KH - 1):
                        pe.wait_ge(hid_ready, have + (KH if k else KH - 1))

                def down(i, n=n + 2 * KH):
                    for d in range(2):
                        unit(n + d, i, hid_hi, hid_lo, hid_wait)
                repeat(pe, None, 0, 0, KD // 2, down)

        rms(0)
        ffn(U_F0, 0, 0)
        rms(1)

        unit(U_DT, 0, hn_hi, hn_lo, hn_wait(1))
        pe.wait_ge(st_in, 16)
        for j in range(CT):
            last = mm(pB[:, j * 24:(j + 1) * 24], st_row[0:24, j * P:(j + 1) * P], ident[0:24, 0:24],
                      start=True, stop=True)
        last.then_inc(st_tr, 1)
        pe.wait_ge(st_done, 1)

        def conv_tr_tile(p, i, j, src=None):
            pe.wait_ge(xcv_ready, i * 2 + (j + 1))
            to_tokens(pB, tmp[p] if src is None else src, conv_tr_used, i * 2 + j).then_inc(conv_tr, 1)

        def x_pair(i):
            if after_first(i):
                unit(U_X, i, hn_hi, hn_lo, lambda k: None)
                conv_tr_tile(1, i, -1)
            else:
                unit(U_X, i, hn_hi, hn_lo, lambda k: None)
            unit(U_X + 1, i, hn_hi, hn_lo, lambda k: None)
            conv_tr_tile(0, i, 0)
        x_pair(0)
        evacuated(pe, U_DT)
        for c in range(TT):
            last = mm(pC[:, c * 32:(c + 1) * 32], sq[96:P, c * P:(c + 1) * P], ident[96:P, 96:P],
                      start=True, stop=True)
        last.then_inc(dt_tr, 1)
        repeat(pe, None, 0, 1, XT_ // 2, x_pair)
        for j in range(XT_, CT):
            unit(U_X + j, 0, hn_hi, hn_lo, lambda k: None)
            if j - 1 < XT_:
                conv_tr_tile((j - 1) % 2, 0, j - 1)
            elif j - 1 < XT_ + SSD_G:
                conv_tr_tile(0, 0, j - 1, bcf[:, j - 1 - XT_, :])
        pe.wait_ge(conv_done, CT)
        all_evacuated(pe, 1, U_V)
        pe.wait_ge(dt_z_ready, 1)
        for j in range(CT):
            dst = (acc[1][0:TAIL, j * P:(j + 1) * P] if j < 8 else pC[0:TAIL, (j - 8) * P:(j - 7) * P])
            last = mm(dst, tails[:, j, :], ident[:, :], start=True, stop=True)
        last.then_inc(tail_tr, 1)

        pe.wait_ge(wd_ready, 1)
        pe.wait_ge(tail_done, 1)
        nh = TT * HEADS
        np_ = ST * HEADS
        for q, mask in enumerate((upto, after)):
            mm(pC[:, q * nh:q * nh + np_], mask[:, 0, :], dt_a[:, 0:np_], start=True, stop=True)
            mm(pC[:, q * nh + np_:(q + 1) * nh], mask[:, 1, :], dt_a[:, np_:nh], start=True, stop=True)
        mm(pC[:, 2 * nh:3 * nh], ones[:, :], dt_a[:, :], start=True, stop=True)
        for j in range(HP):
            last = mm(pC[:, 3 * nh + j * DEC_BATCH:3 * nh + (j + 1) * DEC_BATCH],
                      wd[:, :, :].rearrange("p a b -> p (a b)")[:, j * P:(j + 1) * P], stream_of[:, :],
                      start=True, stop=True)
        last.then_inc(sums_mm, 1)

        for s in range(TT * SSD_G):
            c, g = divmod(s, SSD_G)
            kind = int(c == ST)
            tok = slice(c * P, (c + 1) * P)
            pe.wait_ge(wd_ready, s + 2)
            if s == 0:
                pe.wait_ge(expo_ready, 1)
                pe.wait_ge(conv_tr_used, XT_ + SSD_G)
            wait(pe, gexp_done, s)
            for q in range(2):
                last = mm(pB[:, q * BANK:(q + 1) * BANK], after[:, kind, :],
                          wd[:, 4 * q:4 * q + 4, :].rearrange("p a b -> p (a b)"), start=True, stop=True)
            last.then_inc(seg_done, 1)
            wait(pe, y_done, s)
            if s == 0:
                all_evacuated(pe, 0, U_V)
            mm(pC[:, BANK:BANK + P], bcf[:, g, tok], bcf[:, SSD_G + g, tok], start=True, stop=True).then_inc(cb_done, 1)
            if not kind:
                if c:
                    pe.wait_ge(hst_ready, s - 1)
                    mm(acc[0][:, 0:BANK], bcf[:, SSD_G + g, tok], hst[:, g * BANK:(g + 1) * BANK],
                       start=True, stop=True)
                pe.wait_ge(g_ready, s + 1)
                mm(acc[0][:, BANK:2 * BANK], btm[:, c, g * P:(g + 1) * P], xds[:, :],
                   start=True, stop=True).then_inc(st_mm, 1)
            else:
                pe.wait_ge(g_ready, s + 1)
                for jj in range(HP // SSD_G):
                    j = g * (HP // SSD_G) + jj
                    pe.wait_ge(h0_in[j % 2], 16 * (j // 2 + 1))
                    wait(pe, h1_ready, j)
                    for b in range(DEC_BATCH):
                        last = nc.tensor.transpose(acc[1][:, b * P:(b + 1) * P], h0s[j % 2][:, b, :], ident[:, :])
                    last.then_inc(h0_tr, 1)
                    pe.wait_ge(h0T_ready, j + 1)
                    wait(pe, yoT_ready, j)
                    for b in range(DEC_BATCH):
                        t0 = c * P + b * DEC_SEQ
                        last = mm(pC[:, BANK + P + b * DEC_SEQ:BANK + P + (b + 1) * DEC_SEQ], h0T[:, b, :],
                                  bcf[:, SSD_G + g, t0:t0 + DEC_SEQ], start=True, stop=True)
                    last.then_inc(yo_mm, 1)
                    if jj == 0:
                        pe.wait_ge(bblk_ready, g + 1)
                    for q in range(2):
                        last = mm(acc[1][:, q * BANK:(q + 1) * BANK], xds[:, jj * P:(jj + 1) * P],
                                  wd[:, 4 * q:4 * q + 4, :].rearrange("p a b -> p (a b)"), start=True, stop=True)
                    last.then_inc(h1_mm, 1)
                    pe.wait_ge(yoT_ready, j + 1)
                    nc.tensor.transpose(acc[0][:, jj * P:(jj + 1) * P], yoT[:, :], ident[:, :]).then_inc(yo_tr, 1)
            for h in range(HG):
                last = mm(pC[:, h * HDIM:(h + 1) * HDIM], gd[:, h, :], xdt[:, h * HDIM:(h + 1) * HDIM],
                          start=True, stop=True)
            last.then_inc(y_mm, 1)
            if s == ST * SSD_G - 1:
                pe.wait_ge(hst_ready, ST * SSD_G)
                for j in range(HP):
                    last = nc.tensor.transpose(acc[1][:, j * P:(j + 1) * P], hst[:, j * P:(j + 1) * P], ident[:, :])
                last.then_inc(hout_tr, 1)
                pe.wait_ge(hout_ready, 1)

        pe.wait_ge(y_done, TT * SSD_G)
        pe.wait_ge(h1_ready, HP)
        for kind, s_in, v in ((0, ws_in, 16), (1, ws_blk_in, 16 * DEC_BATCH)):
            pe.wait_ge(s_in, v)
            wait(pe, wm_ready, kind)
            for h in range(8):
                last = nc.tensor.transpose(pB[:, h * P:(h + 1) * P], wst[:, h, :], ident[:, :])
            last.then_inc(ws_tr, 1)
        pe.wait_ge(wm_ready, 2)

        def mix(h):
            pe.wait_ge(vn_ready, h + 1)
            wait(pe, mix_used, h)
            for c in range(TT):
                last = mm(pC[:, c * P:(c + 1) * P], xadd[:, c * P:(c + 1) * P],
                          wmT[:, int(c == ST), bass.ds(h * P, P)], start=True, stop=True)
            last.then_inc(mix_mm, 1)

        def vu(i):
            unit(U_V, i, hn_hi, hn_lo, lambda k: None)
            if after_first(i):
                mix(i - 1)
            unit(U_V + 1, i, hn_hi, hn_lo, lambda k: None)
            evacuated(pe, U_V, i)
            to_tokens(pB, tmp[0], vc_ready, i).then_inc(vt_tr, 1)
        vu(0)
        vu(1)
        repeat(pe, None, 0, 2, KD, vu)
        for j in range(KD):
            unit(U_Z + j, 0, hn_hi, hn_lo, lambda k: None)
            if j == 0:
                mix(KD - 1)
                pe.wait_ge(vc_ready, KD)
            wait(pe, yz_ready, j)
            for c in range(TT):
                last = nc.tensor.transpose(pB[:, c * P:(c + 1) * P], ytm3[:, c, j * P:(j + 1) * P], ident[:, :])
            last.then_inc(yt_tr, 1)

        pe.wait_ge(gm_ready, KD)
        unit(U_OG, 0, gm_hi, gm_lo, lambda k: None)
        rms(2)
        unit(U_OG + 1, 0, gm_hi, gm_lo, lambda k: None)

        def og(i):
            for d in range(2):
                unit(U_OG + d, i, gm_hi, gm_lo, lambda k: None)
        repeat(pe, None, 0, 1, KD // 2, og)

        def oy(i):
            for d in range(2):
                unit(U_OY + d, i, hn_hi, hn_lo, lambda k: pe.wait_ge(yfm_split, k + 1))
        repeat(pe, None, 0, 0, KD // 2, oy)

        rms(3)
        ffn(U_F1, 2, PARTS)
        rms(4)
        for f in range(KD):
            if f < 2:
                all_evacuated(pe, f, U_END)
            pe.wait_ge(of_ready, f + 1)
            to_tokens(acc[f % 2], y_fm[f % 2], of_done, f - 1).then_inc(of_tr, 1)

    @block.scalar
    def _(act):
        st = Steps(act, act_step)
        A = nc.scalar.activation

        def hi(n, i=0):
            if isinstance(i, int) and n + 2 * i >= U_END:
                return
            p, w = n % 2, unit_tiles(n, i) * P
            act.wait_ge(w_in_sb[p], i * 16 + 16 * (n // 2 + 1))
            wait(act, unit_done, i * 2 + (n - 1))
            A(whi[p][:, 0:w], wraw[p][:, 0:w], ACT.Copy).then_inc(whi_done, 1)

        def done(n, i=0):
            act.wait_ge(unit_done, i * 2 + (n + 1))

        def rms_root(m):
            act.wait_ge(rms_mm, m + 1)
            A(split2(rT[:, :]), halves(pC), ACT.Sqrt, bias=eps_t[:, 0:1]).then_inc(rms_sqrt, 1)

        def norm(m, hn0, shift, dst=None):
            for f in range(KD):
                b = modc[:, shift + f, 0:1]
                if dst is None:
                    act.wait_ge(prod_ready, prod0[0] + f + 1)
                    A(hn_hi[:, f * TOK:f * TOK + SEQ], tmp[f % 2][:, 0:SEQ], ACT.Identity, bias=b)
                    act.wait_ge(tms_ready, tms0[0] + f + 1)
                    A(hn_hi[:, f * TOK + SEQ:(f + 1) * TOK], tms[f % 2][:, :], ACT.Copy).then_inc(nhi_ready, 1)
                else:
                    act.wait_ge(prod_ready, prod0[0] + f + 1)
                    wait(act, of_tr, f - 1)
                    A(dst[f % 2][:, 0:SEQ], tmp[f % 2][:, 0:SEQ], ACT.Identity, bias=b)
                    act.wait_ge(tms_ready, tms0[0] + f + 1)
                    A(dst[f % 2][:, SEQ:TOK], tms[f % 2][:, :], ACT.Copy).then_inc(of_ready, 1)
            prod0[0] += KD
            tms0[0] += KD
        prod0, tms0 = [0], [0]

        act.wait_ge(setup_in, 16 * 9)
        A(c_sil[:, :], c_row[:, :], ACT.Silu).then_inc(c_silu, 1)
        act.wait_ge(vecs_in, 48)
        st.done(A(vecs[:, 1, :], vecs[:, 1, :], ACT.Exp))
        act.wait_ge(c_tr, 1)
        A(c_hl[:, :, 0:NSTR], pB[:, 0:KD * NSTR].rearrange("p (k c) -> p k c", c=NSTR), ACT.Copy).then_inc(c_used, 1)
        for c in range(TT):
            act.wait_ge(xt_tr, c + 1)
            A(xT[:, :].rearrange("p (f t) -> p f t", t=TOK)[:, :, c * P:(c + 1) * P],
              acc[c % 2][:, :].rearrange("p (f t) -> p f t", t=P), ACT.Copy).then_inc(xt_done, 1)
        act.wait_ge(xt_done, TT)
        for f in range(KD):
            wait(act, sq_added, f)
            A(sq[:, :], tile(xT, f), ACT.Square).then_inc(sq_ready, 1)

        def ada_ring(i):
            for s in range(ADA_RING):
                act.wait_ge(ada_in[s], i * 16 + 16)
                wait(act, ada_mm, i * ADA_RING + (s - 1))
                A(ada_hi[s % 2][:, :], ada_raw[s][:, :], ACT.Copy).then_inc(ada_hi_done, 1)
        ada_ring(0)
        repeat(act, None, 0, 1, ADA_CHUNKS // ADA_RING, ada_ring)

        def ffn(u0, p0, squares):
            for part in range(PARTS):
                n = u0 + part * (2 * KH + KD)
                h0 = (p0 + part) * KH

                def pair(i, n=n, h0=h0):
                    hi(n + 1, i)
                    done(n, i)
                    wait(act, hid_ready, i + h0)
                    A(split2(silg[:, :]), halves(acc[n % 2]), ACT.Silu).then_inc(acc_free[n % 2], 1)
                    hi(n + 2, i)
                    evacuated(act, n + 1, i)
                    A(tile(hid_hi, i), hidp[:, :], ACT.Copy).then_inc(hhi_ready, 1)
                repeat_peeled(act, KH - 1, pair, n)
                pair(KH - 1)
                n += 2 * KH
                sq0 = (sq_of[0] * KD)

                def down(i, n=n, sq0=sq0, last=(part == PARTS - 1)):
                    for d in range(2):
                        hi(n + d + 1, i)
                        if last:
                            act.wait_ge(x_ready, i * 2 + (x0[0] + d + 1))
                            wait(act, sq_added, i * 2 + (sq0 + d))
                            A(sq[:, :], tile(xT, i * 2 + d), ACT.Square).then_inc(sq_ready, 1)
                repeat(act, None, 0, 0, KD // 2 - 1, down)
                down(KD // 2 - 1)
            sq_of[0] += 1
            x0[0] += KD
        sq_of, x0 = [1], [0]

        hi(U_F0)
        rms_root(0)
        act.wait_ge(mod_ready, 1)
        norm(0, 0, 0)
        ffn(U_F0, 0, 0)
        rms_root(1)
        norm(1, 0, 3 * KD)

        hi(U_DT + 1)
        done(U_DT)
        A(sq[96:P, :].rearrange("p (h x) -> p h x", h=2), halves(acc[U_DT % 2])[96:P], ACT.Copy
          ).then_inc(acc_free[U_DT % 2], 1)
        act.wait_ge(st_tr, 1)
        A(stT[:, :, :], pB[:, 0:CT * 24].rearrange("p (j r) -> p j r", r=24), ACT.Copy).then_inc(st_done, 1)

        def xbc(n, i, j, last=False):
            p = n % 2
            b = j % 2
            hi(n + 1, i)
            done(n, i)
            wait(act, conv_done, i * 2 + (j - 1))
            A(xpad[b][:, 3:3 + HALF], acc[p][:, 0:HALF], ACT.Copy)
            A(xpad[b][:, 3 + HALF:PAD_P], acc[p][:, BANK:BANK + SEQ - HALF], ACT.Copy)
            A(by_stream(xpad[b][:, PAD_P:PAD], PAD_S)[:, :, 3:PAD_S],
              by_stream(acc[p][:, BANK + SEQ - HALF:BANK + HALF]), ACT.Copy).then_inc(acc_free[p], 1)
            act.wait_ge(conv_done, i * 2 + (j + 1))
            if j < XT_:
                dst = tmp[b]
                wait(act, conv_tr, i * 2 + (j - 1))
            else:
                dst = bcf[:, j - XT_, :]
            A(dst[:, 0:SEQ], cacc[:, 0:SEQ], ACT.Silu)
            A(by_stream(dst[:, SEQ:TOK]), by_stream(cacc[:, PAD_P:PAD], PAD_S)[:, :, 0:DEC_SEQ],
              ACT.Silu).then_inc(xcv_ready, 1)

        def conv_out(i, j):
            act.wait_ge(conv_tr, i * 2 + (j + 1))
            if j < XT_:
                dst = ytm3[:, :, bass.ds(i * 2 * P + j * P, P)]
            else:
                dst = btm[:, :, (j - XT_) * P:(j - XT_ + 1) * P]
            A(dst, pB[:, 0:TOK].rearrange("p (c n) -> p c n", c=TT), ACT.Copy).then_inc(conv_tr_used, 1)

        def x_pair(i):
            xbc(U_X, i, 0)
            if after_first(i):
                conv_out(i, -1)
            xbc(U_X + 1, i, 1)
            conv_out(i, 0)
        x_pair(0)
        repeat(act, None, 0, 1, XT_ // 2, x_pair)
        for j in range(XT_, CT):
            xbc(U_X + j, 0, j)
            if j - 1 < XT_ + SSD_G:
                conv_out(0, j - 1)
        act.wait_ge(dt_z_ready, 1)
        st.done(A(dt_e[:, :], dt_z[:, :], ACT.Abs))
        st.done(A(dt_e[:, :], dt_e[:, :], ACT.Exp, scale=-1.0))
        A(dt_e[:, :], dt_e[:, :], ACT.Ln, bias=1.0).then_inc(dt_e_ready, 1)
        act.wait_ge(tail_tr, 1)
        A(tail_row[:, 0:2 * BANK], acc[1][0:TAIL, :], ACT.Copy)
        A(tail_row[:, 2 * BANK:CONV_DIM], pC[0:TAIL, 0:CONV_DIM - 2 * BANK], ACT.Copy).then_inc(tail_done, 1)

        nh = TT * HEADS
        act.wait_ge(sums_mm, 1)
        A(expo[:, :, :].rearrange("p a b -> p (a b)"), pC[:, 0:3 * nh], ACT.Exp)
        act.wait_ge(tail_out, 32)
        A(decs[:, :, :].rearrange("p a b -> p (a b)"), pC[:, 3 * nh:3 * nh + HP * DEC_BATCH], ACT.Exp
          ).then_inc(expo_ready, 1)
        for s in range(TT * SSD_G):
            c, g = divmod(s, SSD_G)
            act.wait_ge(seg_done, s + 1)
            wait(act, y_mm, s)
            A(gd[:, :, :].rearrange("p a b -> p (a b)"), pB[:, :], ACT.Exp).then_inc(gexp_done, 1)
            if c == ST:
                for jj in range(HP // SSD_G):
                    j = g * (HP // SSD_G) + jj
                    act.wait_ge(h0_tr, j + 1)
                    wait(act, yo_mm, j)
                    A(h0T[:, :, :].rearrange("p a b -> p (a b)"), acc[1][:, :], ACT.Copy).then_inc(h0T_ready, 1)
                    act.wait_ge(yo_mm, j + 1)
                    wait(act, yo_tr, j)
                    A(yoT[:, :], pC[:, BANK + P:BANK + 2 * P], ACT.Copy).then_inc(yoT_ready, 1)
            if s == ST * SSD_G - 1:
                act.wait_ge(hout_tr, 1)
                A(h0T[:, :, :].rearrange("p a b -> p (a b)"), acc[1][:, :], ACT.Copy).then_inc(hout_ready, 1)
                act.wait_ge(hout_out, 16)

        def v_stats(h):
            act.wait_ge(vc_ready, h + 1)
            A(sq[:, :], tmp[1][:, :], ACT.Square).then_inc(vsq_ready, 1)
            act.wait_ge(vvar_ready, h + 1)
            A(stat[:, 3, :], stat[:, 2, :], ACT.Sqrt, bias=eps_t[:, 0:1], scale=1.0 / P).then_inc(vstd_ready, 1)

        def gm_hi_part(h):
            act.wait_ge(gmp_ready, h + 1)
            A(tile(gm_hi, h), gmp[:, :], ACT.Copy).then_inc(gmhi_ready, 1)

        def vu(i):
            first = not after_first(i)
            hi(U_V + 1, i)
            if not first:
                v_stats(i - 1)
            done(U_V, i)
            wait(act, vt_tr, i)
            A(split2(tmp[0][:, :]), halves(acc[U_V % 2]), ACT.Gelu_apprx_tanh).then_inc(acc_free[U_V % 2], 1)
            hi(U_V + 2, i)
            if not first:
                gm_hi_part(i - 1)
            done(U_V + 1, i)
            A(split2(gu[:, :]), halves(acc[(U_V + 1) % 2]), ACT.Gelu_apprx_tanh).then_inc(acc_free[(U_V + 1) % 2], 1)
        vu(0)
        vu(1)
        repeat(act, None, 0, 2, KD, vu)
        for j in range(KD):
            hi(U_Z + j + 1)
            if j == 0:
                v_stats(KD - 1)
                gm_hi_part(KD - 1)
            n = U_Z + j
            done(n)
            wait(act, yz_ready, j - 1)
            if j == 1:
                act.wait_ge(vn_ready, KD)
            A(split2(tmp[j % 2][:, :]), halves(acc[n % 2]), ACT.Silu).then_inc(acc_free[n % 2], 1)
            act.wait_ge(yz_ready, j + 1)
            wait(act, sq_added, 2 * KD + j)
            A(sq[:, :].rearrange("p (c n) -> p c n", c=TT), ytm3[:, :, j * P:(j + 1) * P], ACT.Square
              ).then_inc(sq_ready, 1)

        hi(U_OG + 1)
        rms_root(2)
        hi(U_OG + 2)
        for f in range(KD):
            act.wait_ge(yp_ready, f + 1)
            A(tile(hn_hi, f), tmp[f % 2][:, :], ACT.Copy).then_inc(yhi_ready, 1)
            if f + 2 < KD:
                hi(U_OG + f + 3)
        hi(U_OY + 1)
        for f in range(KD):
            if f:
                hi(U_OY + f + 1)
            act.wait_ge(x_ready, x0[0] + f + 1)
            wait(act, sq_added, 3 * KD + f)
            A(sq[:, :], tile(xT, f), ACT.Square).then_inc(sq_ready, 1)
        x0[0] += KD
        sq_of[0] = 4
        rms_root(3)
        norm(3, 0, 6 * KD)
        ffn(U_F1, PARTS, 0)
        rms_root(4)
        norm(4, 0, 9 * KD, y_fm)

    @block.vector
    def _(dve):
        V = nc.vector
        st = Steps(dve, dve_step)

        def lo(n, i=0):
            if isinstance(i, int) and n + 2 * i >= U_END:
                return
            p, w = n % 2, unit_tiles(n, i) * P
            dve.wait_ge(whi_done, i * 2 + (n + 1))
            V.tensor_tensor(out=wlo[p][:, 0:w], in0=wraw[p][:, 0:w], in1=whi[p][:, 0:w].bitcast(F32),
                            op=ALU.subtract).then_inc(wlo_done, 1)

        def done(n, i=0):
            dve.wait_ge(unit_done, i * 2 + (n + 1))

        def add_gated(n, i, f, q, count_x):
            done(n, i)
            g = by_group(split2(xadd[:, :]))
            V.tensor_tensor(out=g, in0=by_group(halves(acc[n % 2])), in1=mod40(q, f), op=ALU.mult
                            ).then_inc(acc_free[n % 2], 1)
            evacuated(dve, n, i)
            x = tile(xT, f)
            ins = V.tensor_tensor(out=x, in0=x, in1=xadd[:, :], op=ALU.add)
            if count_x:
                ins.then_inc(x_ready, 1)
            else:
                st.done(ins)

        def add_square(k, fresh=False):
            dve.wait_ge(sq_ready, k + 1)
            V.tensor_tensor(out=ssum[:, :], in0=ssum[:, :], in1=sq[:, :], op=ALU.add).then_inc(sq_added, 1)

        def r_of(m):
            dve.wait_ge(rms_sqrt, m + 1)
            V.reciprocal(out=rT[:, :], in_=rT[:, :]).then_inc(rinv_ready, 1)
            st.done(V.memset(ssum[:, :], 0.0))
            dve.wait_ge(rinv_ready, m + 1)

        def norm(shift, scale, to_hn=True):
            def prod(f):
                V.scalar_tensor_tensor(out=tmp[f % 2][:, 0:SEQ], in0=xT[:, f * TOK:f * TOK + SEQ],
                                       scalar=modc[:, scale + f, 0:1], in1=rT[:, 0:SEQ],
                                       op0=ALU.mult, op1=ALU.mult).then_inc(prod_ready, 1)
            prod(0)
            for f in range(KD):
                if f + 1 < KD:
                    if f >= 1:
                        dve.wait_ge(*((hn_ready, nhi0[0] + f) if to_hn else (of_ready, f)))
                    prod(f + 1)
                if not to_hn and f:
                    result(f - 1)
                if not to_hn:
                    continue
                dve.wait_ge(nhi_ready, nhi0[0] + f + 1)
                a, b, c = f * TOK, f * TOK + SEQ, (f + 1) * TOK
                V.scalar_tensor_tensor(out=hn_lo[:, a:b], in0=tmp[f % 2][:, 0:SEQ], scalar=modc[:, shift + f, 0:1],
                                       in1=hn_hi[:, a:b].bitcast(F32), op0=ALU.add, op1=ALU.subtract)
                V.tensor_tensor(out=hn_lo[:, b:c], in0=tms[f % 2][:, :], in1=hn_hi[:, b:c].bitcast(F32),
                                op=ALU.subtract).then_inc(hn_ready, 1)
            nhi0[0] += KD
        nhi0 = [0]

        dve.wait_ge(c_used, 1)
        V.tensor_tensor(out=c_hl[:, :, NSTR:2 * NSTR], in0=pB[:, 0:KD * NSTR].rearrange("p (k c) -> p k c", c=NSTR),
                        in1=c_hl[:, :, 0:NSTR].bitcast(F32), op=ALU.subtract).then_inc(c_split, 1)
        dve.wait_ge(par_tr, 1)
        V.tensor_copy(b_col[:, :], pB[:, BANK:BANK + MODT])
        st.done(V.tensor_copy(par[:, :], pB[:, BANK + P:BANK + P + N_PAR]))
        st.done(V.memset(ssum[:, :], 0.0))
        for f in range(KD):
            add_square(f)

        def ada_ring(i):
            for s in range(ADA_RING):
                dve.wait_ge(ada_hi_done, i * ADA_RING + (s + 1))
                V.tensor_tensor(out=ada_lo[s % 2][:, :], in0=ada_raw[s][:, :], in1=ada_hi[s % 2][:, :].bitcast(F32),
                                op=ALU.subtract).then_inc(ada_lo_done, 1)
                dve.wait_ge(ada_mm, i * ADA_RING + (s + 1))
                ft = ADA_COLS // P
                o = (s % 2) * BANK
                V.tensor_reduce(out=modc[:, bass.ds(i * (ADA_RING * ft) + s * ft, ft), :],
                                in_=pC[:, o:o + ft * 2 * NSTR].rearrange("p (f a c) -> p f c a", a=2, c=NSTR),
                                axis=AX.X, op=ALU.add).then_inc(ada_used, 1)
        repeat(dve, None, 0, 0, ADA_CHUNKS // ADA_RING, ada_ring)
        dve.wait_ge(ada_used, ADA_CHUNKS)
        st.done(V.tensor_tensor(out=modc[:, :, :], in0=modc[:, :, :],
                                in1=b_col[:, :].unsqueeze(2).broadcast_to([P, MODT, NSTR]), op=ALU.add))
        for row, scale in ((R_NORM, KD), (R_NORM + KD, 4 * KD), (R_NORM + 2 * KD, 7 * KD), (R_FINAL, 10 * KD)):
            g = par[:, row:row + KD].unsqueeze(2).broadcast_to([P, KD, NSTR])
            v = modc[:, scale:scale + KD, :]
            st.done(V.scalar_tensor_tensor(out=v, in0=v, scalar=1.0, in1=g, op0=ALU.add, op1=ALU.mult))
        for q, factor in ((0, 0.5), (1, 1.0), (2, 0.5)):
            v = modc[:, (3 * q + 2) * KD:(3 * q + 3) * KD, :]
            g = gate[:, q, :].rearrange("p (f g) -> p f g", f=KD)
            V.tensor_scalar(out=g[:, :, 0:GRP - DEC_BATCH],
                            in0=v[:, :, 0:1].broadcast_to([P, KD, GRP - DEC_BATCH]),
                            scalar1=factor, scalar2=None, op0=ALU.mult)
            st.done(V.tensor_scalar(out=g[:, :, GRP - DEC_BATCH:GRP], in0=v[:, :, 1:NSTR],
                                    scalar1=factor, scalar2=None, op0=ALU.mult))
        V.tensor_copy(b_col[:, 0:1], par[:, 0:1]).then_inc(mod_ready, 1)

        def ffn(u0, q, part0, sq0):
            for part in range(PARTS):
                n = u0 + part * (2 * KH + KD)
                h0 = (part0 + part) * KH

                def pair(i, n=n, h0=h0):
                    lo(n + 1, i)
                    lo(n + 2, i)
                    done(n + 1, i)
                    evacuated(dve, n, i)
                    wait(dve, hid_ready, i + h0)
                    V.tensor_tensor(out=split2(hidp[:, :]), in0=split2(silg[:, :]), in1=halves(acc[(n + 1) % 2]),
                                    op=ALU.mult).then_inc(acc_free[(n + 1) % 2], 1)
                    dve.wait_ge(hhi_ready, i + (h0 + 1))
                    V.tensor_tensor(out=tile(hid_lo, i), in0=hidp[:, :], in1=tile(hid_hi, i).bitcast(F32),
                                    op=ALU.subtract).then_inc(hid_ready, 1)
                repeat_peeled(dve, KH - 1, pair, n)
                pair(KH - 1)
                n += 2 * KH
                last = part == PARTS - 1

                def down(i, n=n, last=last):
                    for d in range(2):
                        lo(n + d + 1, i)
                        add_gated(n + d, i, i * 2 + d, q, last)
                        if last:
                            add_square(i * 2 + (sq0 + d))
                repeat(dve, st, 0 if last else 2, 0, KD // 2 - 1, down)
                down(KD // 2 - 1)

        lo(U_F0)
        r_of(0)
        norm(0, KD)
        ffn(U_F0, 0, 0, KD)
        r_of(1)
        norm(3 * KD, 4 * KD)

        lo(U_DT + 1)
        dve.wait_ge(st_done, 1)

        def xbc(n, i, j):
            b = j % 2
            lo(n + 1, i)
            V.tensor_copy(by_stream(xpad[b][:, PAD_P:PAD], PAD_S)[:, :, 0:3],
                          stT[:, bass.ds(i * 2 + j, 1), :].rearrange("p a (b k) -> p (a b) k", k=3))
            evacuated(dve, n, i)
            t = tails[:, bass.ds(i * 2 + j, 1), :].rearrange("p a r -> p (a r)")
            V.tensor_copy(t[:, 0:3], xpad[b][:, SEQ:PAD_P])
            st.done(V.tensor_copy(t[:, 3:TAIL].rearrange("p (b k) -> p b k", k=3),
                                  by_stream(xpad[b][:, PAD_P:PAD], PAD_S)[:, :, DEC_SEQ:PAD_S]))
            wait(dve, xcv_ready, i * 2 + j)
            w = [par[:, bass.ds(i * 2 + (R_CW + k * CT + j), 1)] for k in range(CONV_W)]
            st.done(V.tensor_scalar(out=cacc[:, 0:CONV_N], in0=xpad[b][:, 0:CONV_N], scalar1=w[0],
                                    scalar2=par[:, bass.ds(i * 2 + (R_CB + j), 1)], op0=ALU.mult, op1=ALU.add))
            for k in range(1, CONV_W):
                ins = V.scalar_tensor_tensor(out=cacc[:, 0:CONV_N], in0=xpad[b][:, k:k + CONV_N], scalar=w[k],
                                             in1=cacc[:, 0:CONV_N], op0=ALU.mult, op1=ALU.add)
                if k + 1 < CONV_W:
                    st.done(ins)
            ins.then_inc(conv_done, 1)

        def x_pair(i):
            xbc(U_X, i, 0)
            xbc(U_X + 1, i, 1)
        dve.wait_ge(pad0_ready, 2)
        st.done(V.memset(cacc[:, CONV_N:PAD], 0.0))
        x_pair(0)
        repeat(dve, st, 8, 1, XT_ // 2, x_pair)
        for j in range(XT_, CT):
            xbc(U_X + j, 0, j)
        dve.wait_ge(dt_tr, 1)
        per_head = [vecs[:, q, :].unsqueeze(1).broadcast_to([P, TT, HEADS]) for q in range(3)]
        by_tile = lambda t: t[:, :].rearrange("p (c h) -> p c h", h=HEADS)
        V.tensor_tensor(out=by_tile(dt_z), in0=pC[:, 0:TT * 32].rearrange("p (c h) -> p c h", h=32)[:, :, 16:32],
                        in1=per_head[0], op=ALU.add).then_inc(dt_z_ready, 1)
        st.done(V.tensor_scalar(out=vecs[:, 1, :], in0=vecs[:, 1, :], scalar1=-1.0, scalar2=None, op0=ALU.mult))
        dve.wait_ge(dt_e_ready, 1)
        st.done(V.scalar_tensor_tensor(out=dt_v[:, :], in0=dt_z[:, :], scalar=0.0, in1=dt_e[:, :],
                                       op0=ALU.max, op1=ALU.add))
        st.done(V.tensor_tensor(out=by_tile(dt_a), in0=by_tile(dt_v), in1=per_head[1], op=ALU.mult))

        dve.wait_ge(tail_out, 32)
        V.tensor_copy(wd[:, :, :].rearrange("p a (b x) -> p (a b) x", x=HDIM),
                      dt_a[:, ST * HEADS:TT * HEADS].unsqueeze(2).broadcast_to([P, HEADS, HDIM])
                      ).then_inc(wd_ready, 1)
        dve.wait_ge(expo_ready, 1)
        for s in range(TT * SSD_G):
            c, g = divmod(s, SSD_G)
            kind = int(c == ST)
            h0 = c * HEADS + g * HG
            x = ytm3[:, c, g * BANK:(g + 1) * BANK]
            heads = lambda ap: ap.rearrange("p (h x) -> p h x", x=HDIM)
            wide = lambda ap: ap.unsqueeze(2).broadcast_to([P, HG, HDIM])
            if s > ST * SSD_G:
                dve.wait_ge(h1_mm, (s - ST * SSD_G) * (HP // SSD_G))
            elif s:
                dve.wait_ge(seg_done, s)
            V.tensor_tensor(out=wd[:, :, :], in0=upto[:, kind, :].unsqueeze(1).broadcast_to([P, HG, P]),
                            in1=dt_a[:, h0:h0 + HG].unsqueeze(2).broadcast_to([P, HG, P]), op=ALU.mult
                            ).then_inc(wd_ready, 1)
            wait(dve, y_mm, s)
            st.done(V.tensor_tensor(out=heads(xdt[:, :]), in0=heads(x), in1=wide(dt_v[:, h0:h0 + HG]), op=ALU.mult))
            V.tensor_tensor(out=heads(xds[:, :]), in0=heads(xdt[:, :]), in1=wide(expo[:, 1, h0:h0 + HG]), op=ALU.mult)
            dve.wait_ge(cb_done, s + 1)
            V.tensor_tensor(out=cbm[:, :], in0=pC[:, BANK:BANK + P], in1=upto[:, kind, :], op=ALU.mult
                            ).then_inc(cbm_done, 1)
            if kind:
                dve.wait_ge(seg_done, s + 1)
                V.tensor_tensor(out=wd[:, :, :], in0=btm[:, c, g * P:(g + 1) * P].unsqueeze(1).broadcast_to([P, HG, P]),
                                in1=stream_of[:, :].unsqueeze(2).broadcast_to([P, DEC_BATCH, NSTATE]), op=ALU.mult
                                ).then_inc(bblk_ready, 1)
            dve.wait_ge(cbm_done, s + 1)
            dve.wait_ge(gexp_done, s + 1)
            V.tensor_tensor(out=gd[:, :, :], in0=gd[:, :, :], in1=cbm[:, :].unsqueeze(1).broadcast_to([P, HG, P]),
                            op=ALU.mult).then_inc(g_ready, 1)
            V.tensor_tensor(out=heads(yt2[:, :]), in0=heads(x), in1=wide(vecs[:, 2, g * HG:(g + 1) * HG]), op=ALU.mult)
            if kind:
                for jj in range(HP // SSD_G):
                    j = g * (HP // SSD_G) + jj
                    dve.wait_ge(h1_mm, j + 1)
                    h = h0s[j % 2][:, :, :]
                    st.done(V.tensor_tensor(out=h, in0=h, in1=decs[:, j, :].unsqueeze(2).broadcast_to([P, DEC_BATCH, NSTATE]),
                                            op=ALU.mult))
                    V.tensor_tensor(out=h, in0=h, in1=acc[1][:, :].rearrange("p (b n) -> p b n", n=NSTATE), op=ALU.add
                                    ).then_inc(h1_ready, 1)
                dve.wait_ge(yo_tr, (g + 1) * (HP // SSD_G))
            dve.wait_ge(y_mm, s + 1)
            if c:
                st.done(V.tensor_tensor(out=heads(yt1[:, :]), in0=heads(acc[0][:, 0:BANK]),
                                        in1=wide(expo[:, 0, h0:h0 + HG]), op=ALU.mult))
                st.done(V.tensor_tensor(out=yt2[:, :], in0=yt2[:, :], in1=yt1[:, :], op=ALU.add))
            else:
                st.done(V.tensor_copy(cbm[:, 0:1], cbm[:, 0:1]))
            V.tensor_tensor(out=x, in0=yt2[:, :], in1=pC[:, 0:BANK], op=ALU.add).then_inc(y_done, 1)
            if not kind:
                hs = hst[:, g * BANK:(g + 1) * BANK]
                dve.wait_ge(st_mm, s + 1)
                if c:
                    st.done(V.tensor_tensor(out=heads(hs), in0=heads(hs), in1=wide(expo[:, 2, h0:h0 + HG]), op=ALU.mult))
                    V.tensor_tensor(out=hs, in0=hs, in1=acc[0][:, BANK:2 * BANK], op=ALU.add).then_inc(hst_ready, 1)
                else:
                    V.tensor_copy(hs, acc[0][:, BANK:2 * BANK]).then_inc(hst_ready, 1)
        dve.wait_ge(y_done, TT * SSD_G)
        dve.wait_ge(h1_ready, HP)
        V.tensor_copy(dt_z[:, 0:1], dt_e[:, 0:1]).then_inc(ssd_over, 1)

        for kind in range(2):
            dve.wait_ge(ws_tr, kind + 1)
            if kind == 0:
                V.memset(wst[:, :, :], 0.0).then_inc(ws_zero, 1)
            V.tensor_tensor(out=wmT[:, kind, :].rearrange("p (h t) -> p h t", t=P),
                            in0=pB[:, :].rearrange("p (h t) -> p h t", t=P),
                            in1=upto[:, kind, :].unsqueeze(1).broadcast_to([P, 8, P]), op=ALU.mult
                            ).then_inc(wm_ready, 1)
        dve.wait_ge(gm_vec_in, 32)

        def v_norm(h):
            pv = pB[:, 0:TOK].rearrange("p (c n) -> p c n", c=TT)
            vc = tmp[1][:, :].rearrange("p (c n) -> p c n", c=TT)
            vn = xadd[:, :].rearrange("p (c n) -> p c n", c=TT)
            dve.wait_ge(vt_tr, h + 1)
            st.done(V.tensor_reduce(out=stat[:, 0, :], in_=pv, axis=AX.X, op=ALU.add))
            st.done(V.tensor_scalar(out=stat[:, 1, :], in0=stat[:, 0, :], scalar1=-1.0 / P, scalar2=None, op0=ALU.mult))
            V.tensor_tensor(out=vc, in0=pv, in1=stat[:, 1, :].unsqueeze(2).broadcast_to([P, TT, P]), op=ALU.add
                            ).then_inc(vc_ready, 1)
            dve.wait_ge(vsq_ready, h + 1)
            V.tensor_reduce(out=stat[:, 2, :], in_=sq[:, :].rearrange("p (c n) -> p c n", c=TT), axis=AX.X, op=ALU.add
                            ).then_inc(vvar_ready, 1)
            dve.wait_ge(vstd_ready, h + 1)
            st.done(V.reciprocal(out=stat[:, 0, :], in_=stat[:, 3, :]))
            wait(dve, v_out, h * 16)
            wait(dve, mix_mm, h)
            st.done(V.tensor_tensor(out=vn, in0=vc, in1=stat[:, 0, :].unsqueeze(2).broadcast_to([P, TT, P]), op=ALU.mult))
            V.tensor_tensor(out=vn, in0=vn, in1=gm_g[:, bass.ds(h * P, P)].unsqueeze(1).broadcast_to([P, TT, P]),
                            op=ALU.mult).then_inc(vn_ready, 1)

        def gm_out(h):
            bias = gm_bias[:, bass.ds(h * P, P)]
            dve.wait_ge(mix_mm, h + 1)
            V.tensor_tensor(out=gmp[:, 0:SEQ].rearrange("p (c t) -> p c t", c=ST),
                            in0=pC[:, 0:SEQ].rearrange("p (c t) -> p c t", c=ST),
                            in1=bias.unsqueeze(1).broadcast_to([P, ST, P]), op=ALU.add)
            V.tensor_tensor(out=by_stream(gmp[:, SEQ:TOK]), in0=by_stream(pC[:, SEQ:TOK]),
                            in1=bias[:, 0:DEC_SEQ].unsqueeze(1).broadcast_to([P, DEC_BATCH, DEC_SEQ]), op=ALU.add
                            ).then_inc(mix_used, 1)
            dve.wait_ge(mix_used, h + 1)
            evacuated(dve, U_V + 1, h)
            V.tensor_tensor(out=gmp[:, :], in0=gmp[:, :], in1=gu[:, :], op=ALU.mult).then_inc(gmp_ready, 1)
            dve.wait_ge(gmhi_ready, h + 1)
            V.tensor_tensor(out=tile(gm_lo, h), in0=gmp[:, :], in1=tile(gm_hi, h).bitcast(F32), op=ALU.subtract
                            ).then_inc(gm_ready, 1)

        def vu(i):
            lo(U_V + 1, i)
            if after_first(i):
                v_norm(i - 1)
            lo(U_V + 2, i)
            if after_first(i):
                gm_out(i - 1)
        vu(0)
        vu(1)
        repeat(dve, st, 4, 2, KD, vu)
        for j in range(KD):
            n = U_Z + j
            lo(n + 1)
            if j == 0:
                v_norm(KD - 1)
                gm_out(KD - 1)
            dve.wait_ge(yt_tr, j + 1)
            evacuated(dve, n)
            V.tensor_tensor(out=ytm3[:, :, j * P:(j + 1) * P], in0=pB[:, 0:TOK].rearrange("p (c n) -> p c n", c=TT),
                            in1=tmp[j % 2][:, :].rearrange("p (c n) -> p c n", c=TT), op=ALU.mult
                            ).then_inc(yz_ready, 1)
            add_square(2 * KD + j)

        lo(U_OG + 1)
        dve.wait_ge(v_out, 16 * KD)
        add_gated(U_OG, 0, 0, 1, False)
        r_of(2)
        lo(U_OG + 2)
        for f in range(KD):
            if f >= 1:
                add_gated(U_OG + f, 0, f, 1, False)
            v3 = tmp[f % 2][:, :].rearrange("p (c n) -> p c n", c=TT)
            V.scalar_tensor_tensor(out=v3, in0=ytm3[:, :, f * P:(f + 1) * P], scalar=par[:, R_SSDN + f:R_SSDN + f + 1],
                                   in1=rT[:, :].rearrange("p (c n) -> p c n", c=TT), op0=ALU.mult, op1=ALU.mult
                                   ).then_inc(yp_ready, 1)
            dve.wait_ge(yhi_ready, f + 1)
            V.tensor_tensor(out=tile(hn_lo, f), in0=tmp[f % 2][:, :], in1=tile(hn_hi, f).bitcast(F32), op=ALU.subtract
                            ).then_inc(yfm_split, 1)
            if f + 2 < KD:
                lo(U_OG + f + 3)
        lo(U_OY + 1)
        for f in range(KD):
            if f:
                lo(U_OY + f + 1)
            add_gated(U_OY + f, 0, f, 1, True)
            add_square(3 * KD + f)
        r_of(3)
        norm(6 * KD, 7 * KD)
        ffn(U_F1, 2, PARTS, 4 * KD)
        r_of(4)

        def result(f):
            dve.wait_ge(of_tr, f + 1)
            V.tensor_copy(y_row[:, :, f * P:(f + 1) * P], acc[f % 2][:, 0:TOK].rearrange("p (c n) -> p c n", c=TT)
                          ).then_inc(of_done, 1)
        norm(9 * KD, 10 * KD, to_hn=False)
        result(KD - 1)

    top.close()


_INPUTS = ("x_prompt", "x_sample", "state_ssm", "state_conv", "c_prompt", "c_sample", "w_ada", "b_ada", "norm_g",
           "ffn_w1", "ffn_w2", "w_in", "gm_norm_g", "gm_ws", "gm_b", "conv_w", "conv_b", "dt_bias", "a_log",
           "d_skip", "ssd_norm_g", "w_out", "final_norm_g", "w_ada_final", "b_ada_final")
_OUTPUTS = (("y_prompt", (1, SEQ, D_MODEL)), ("y_sample", (DEC_BATCH, DEC_SEQ, D_MODEL)),
            ("ssm_prompt", (1, 1, HEADS, HDIM, NSTATE)), ("conv_prompt", (1, 1, CONV_W - 1, CONV_DIM)),
            ("ssm_sample", (1, DEC_BATCH, HEADS, HDIM, NSTATE)),
            ("conv_sample", (1, DEC_BATCH, CONV_W - 1, CONV_DIM)),
            ("gm_v_sample", (1, DEC_BATCH, DEC_SEQ, D_MODEL)))


def kernel(**inputs):
    import numpy as np
    import concourse.bacc as bacc
    from concourse.bass_utils import run_bass_kernel_spmd

    nc = bacc.Bacc("TRN2", target_bir_lowering=False, num_devices=1)
    arrays, args = {}, []
    for name in _INPUTS:
        a = np.ascontiguousarray(inputs[name])
        arrays[f"in_{name}"] = a
        args.append(nc.dram_tensor(f"in_{name}", a.shape, mybir.dt.from_np(a.dtype), kind="ExternalInput").ap())
    for name, shape in _OUTPUTS:
        args.append(nc.dram_tensor(f"out_{name}", shape, F32, kind="ExternalOutput").ap())
    trunk_program(nc, *args)
    r = run_bass_kernel_spmd(nc, [arrays], core_ids=[0])
    return tuple(r.results[0][f"out_{name}"] for name, _ in _OUTPUTS)
```

```python
import math
from contextlib import ExitStack, contextmanager

import concourse.bass as bass
from concourse import mybir

F32 = mybir.dt.float32
F32R = mybir.dt.float32r
ACT = mybir.ActivationFunctionType
ALU = mybir.AluOpType
AX = mybir.AxisListType

P = 128
D_MODEL = 1024
SEQ = 512
DEC_BATCH = 8
DEC_SEQ = 16
TOK = SEQ + DEC_BATCH * DEC_SEQ
HALF = TOK // 2
BANK = 512
TT = TOK // P
ST = TT - 1
KD = D_MODEL // P
NSTR = 1 + DEC_BATCH
GRP = TOK // DEC_SEQ
D_FF = 2816
FF_TILES = D_FF // P
PARTS = (KD, KD, FF_TILES - 2 * KD)
PART0 = (0, KD, 2 * KD)
HEADS = 16
HDIM = 64
NSTATE = 128
SSD_G = 2
HG = HEADS // SSD_G
CONV_W = 4
CONV_DIM = D_MODEL + 2 * SSD_G * NSTATE
CT = CONV_DIM // P
XT_ = D_MODEL // P
D_IN = 4 * D_MODEL + 2 * SSD_G * NSTATE + HEADS
COL_U, COL_V, COL_Z, COL_X = 0, D_MODEL, 2 * D_MODEL, 3 * D_MODEL
COL_DT = D_IN - P
N_MOD = 9
MODT = (N_MOD + 2) * KD
EPS = 1e-6
HP = HEADS * HDIM // P
PAD_P = SEQ + CONV_W - 1
PAD_S = DEC_SEQ + CONV_W - 1
PAD = PAD_P + DEC_BATCH * PAD_S
CONV_N = PAD - (CONV_W - 1)
TAIL = NSTR * (CONV_W - 1)

R_NORM, R_FINAL, R_SSDN, R_CW, R_CB = 0, 24, 32, 40, 40 + CONV_W * CT
N_PAR = R_CB + CT

H0_RING = 4

ADA_COLS = 2 * P
ADA_FIRST = 2 * D_MODEL // ADA_COLS
ADA_RING = 4
ADA_MAIN = N_MOD * D_MODEL // ADA_COLS
ADA_ALL = (N_MOD + 2) * D_MODEL // ADA_COLS
CH_PAIR = (ADA_FIRST, ADA_FIRST + PARTS[0] + KD // 2, ADA_FIRST + PARTS[0] + PARTS[1] + KD)
CH_DOWN = (CH_PAIR[0] + PARTS[0], CH_PAIR[1] + PARTS[1])
CH_LAST = ADA_MAIN - CH_PAIR[2]


def trunk_program(nc, x_prompt, x_sample, state_ssm, state_conv, c_prompt, c_sample, w_ada, b_ada, norm_g,
                  ffn_w1, ffn_w2, w_in, gm_norm_g, gm_ws, gm_b, conv_w, conv_b, dt_bias, a_log, d_skip,
                  ssd_norm_g, w_out, final_norm_g, w_ada_final, b_ada_final,
                  y_prompt, y_sample, ssm_prompt, conv_prompt, ssm_sample, conv_sample, gm_v_sample):
    top = ExitStack()

    def sb(name, shape, dt=F32, stack=None):
        return (stack or top).enter_context(nc.sbuf_tensor(name, shape, dt))

    def ps(name, cols):
        return top.enter_context(nc.psum_tensor(name, [P, cols], F32))

    def sem(name):
        return top.enter_context(nc.semaphore(name))

    xT = sb("xT", [P, KD * TOK])
    hn_hi = sb("hn_hi", [P, KD * TOK], F32R)
    hn_lo = sb("hn_lo", [P, KD * TOK], F32R)
    wraw = [sb(f"wraw{i}", [P, KD * P]) for i in range(2)]
    whi = [sb(f"whi{i}", [P, KD * P], F32R) for i in range(2)]
    wlo = [sb(f"wlo{i}", [P, KD * P], F32R) for i in range(2)]
    modc = sb("modc", [P, MODT, NSTR])
    gate = sb("gate", [P, 3, KD * GRP])
    par = sb("par", [P, N_PAR])
    ident = sb("ident", [P, P])
    ones_mean = sb("ones_mean", [P, P])
    ones = sb("ones", [P, P])
    upto = sb("upto", [P, 2, P])
    after = sb("after", [P, 2, P])
    stream_of = sb("stream_of", [P, DEC_BATCH])
    rT = sb("rT", [P, TOK])
    ssum = sb("ssum", [P, TOK])
    sq = sb("sq", [P, TOK])
    tmp = [sb(f"tmp{i}", [P, TOK]) for i in range(2)]
    tms = [sb(f"tms{i}", [P, P]) for i in range(2)]
    xadd = sb("xadd", [P, TOK])
    eps_t = sb("eps_t", [P, 1])
    c_hl = sb("c_hl", [P, KD, 2 * NSTR], F32R)
    b_col = sb("b_col", [P, MODT])
    pairsum = sb("pairsum", [2 * NSTR, NSTR])
    vecs = sb("vecs", [P, 3, HEADS])

    reg = ExitStack()
    ada_raw = [sb(f"ada_raw{i}", [P, KD * ADA_COLS], stack=reg) for i in range(ADA_RING)]
    ada_hi = [sb(f"ada_hi{i}", [P, KD * ADA_COLS], F32R, reg) for i in range(2)]
    ada_lo = [sb(f"ada_lo{i}", [P, KD * ADA_COLS], F32R, reg) for i in range(2)]
    ada_row = [sb(f"ada_row{i}", [2 * NSTR, ADA_COLS], stack=reg) for i in range(2)]
    c_row = sb("c_row", [NSTR, D_MODEL], stack=reg)
    c_sil = sb("c_sil", [NSTR, D_MODEL], stack=reg)
    b_row = sb("b_row", [MODT, P], stack=reg)
    p_row = sb("p_row", [N_PAR, P], stack=reg)
    x_row = [sb(f"x_row{i}", [P, D_MODEL], stack=reg) for i in range(TT)]
    reg.close()
    reg = ExitStack()
    hid_hi = sb("hid_hi", [P, KD * TOK], F32R, reg)
    hid_lo = sb("hid_lo", [P, KD * TOK], F32R, reg)
    silg = sb("silg", [P, TOK], stack=reg)
    hidp = sb("hidp", [P, TOK], stack=reg)
    sraw = sb("sraw", [P, KD * ADA_COLS], stack=reg)
    shi = sb("shi", [P, KD * ADA_COLS], F32R, reg)
    slo = sb("slo", [P, KD * ADA_COLS], F32R, reg)
    srow = sb("srow", [2 * NSTR, ADA_COLS], stack=reg)
    reg.close()
    reg = ExitStack()
    ytm = sb("ytm", [P, TT * D_MODEL], stack=reg)
    sub = ExitStack()
    bcf = sb("bcf", [P, 4, TOK], stack=sub)
    btm = sb("btm", [P, TT, SSD_G * NSTATE], stack=sub)
    dt_z = sb("dt_z", [P, TT * HEADS], stack=sub)
    dt_e = sb("dt_e", [P, TT * HEADS], stack=sub)
    dt_v = sb("dt_v", [P, TT * HEADS], stack=sub)
    dt_a = sb("dt_a", [P, TT * HEADS], stack=sub)
    expo = sb("expo", [P, 3, TT * HEADS], stack=sub)
    decs = sb("decs", [P, HP, DEC_BATCH], stack=sub)
    conv_mem = ExitStack()
    tails = sb("tails", [P, CT, TAIL], stack=conv_mem)
    stT = sb("stT", [P, CT, TAIL - 3], stack=conv_mem)
    st_row = sb("st_row", [TAIL - 3, CONV_DIM], stack=conv_mem)
    tail_row = sb("tail_row", [TAIL, CONV_DIM], stack=conv_mem)
    xpad = [sb(f"xpad{i}", [P, PAD], stack=conv_mem) for i in range(2)]
    cacc = sb("cacc", [P, PAD], stack=conv_mem)
    conv_mem.close()
    h0s = [sb(f"h0s{i}", [P, DEC_BATCH, NSTATE], stack=sub) for i in range(H0_RING)]
    h0T = sb("h0T", [P, DEC_BATCH, P], stack=sub)
    hst = sb("hst", [P, HEADS * HDIM], stack=sub)
    wd = sb("wd", [P, HG, P], stack=sub)
    gd = sb("gd", [P, HG, P], stack=sub)
    cbm = sb("cbm", [P, TT * SSD_G, P], stack=sub)
    zs = sb("zs", [P, KD * TOK], stack=sub)
    sub.close()
    sub = ExitStack()
    wst = sb("wst", [P, 8, P], stack=sub)
    wsb = sb("wsb", [P, 8, P], stack=sub)
    gm_g = sb("gm_g", [P, D_MODEL], stack=sub)
    gm_bias = sb("gm_bias", [P, 8 * P], stack=sub)
    wmT = sb("wmT", [P, 2, 8 * P], stack=sub)
    stat = sb("stat", [P, 4, TT], stack=sub)
    gu = sb("gu", [P, TOK], stack=sub)
    gmp = sb("gmp", [P, TOK], stack=sub)
    gm_hi = sb("gm_hi", [P, KD * TOK], F32R, sub)
    gm_lo = sb("gm_lo", [P, KD * TOK], F32R, sub)
    sub.close()
    reg.close()
    reg = ExitStack()
    y_row = sb("y_row", [P, TT, D_MODEL], stack=reg)
    y_fm = [sb(f"y_fm{i}", [P, TOK], stack=reg) for i in range(2)]
    reg.close()

    acc = [ps("acc0", 2 * BANK), ps("acc1", 2 * BANK)]
    pB = ps("pB", 2 * BANK)
    pC = ps("pC", 2 * BANK)

    setup_in = sem("setup_in")
    vecs_in = sem("vecs_in")
    x_in = [sem(f"x_in{i}") for i in range(TT)]
    masks_done = sem("masks_done")
    pool_step, act_step, dve_step = sem("pool_step"), sem("act_step"), sem("dve_step")
    c_silu = sem("c_silu")
    c_tr, c_used, c_split = sem("c_tr"), sem("c_used"), sem("c_split")
    par_tr, par_done = sem("par_tr"), sem("par_done")
    xt_tr, xt_done = sem("xt_tr"), sem("xt_done")
    ada_in = [sem(f"ada_in{i}") for i in range(ADA_RING)]
    s_in = sem("s_in")
    ch_hi, ch_lo = sem("ch_hi"), sem("ch_lo")
    ch_mm, ch_row, ch_tr, ch_sum = sem("ch_mm"), sem("ch_row"), sem("ch_tr"), sem("ch_sum")
    mod_ready = sem("mod_ready")
    w_in_sb = [sem(f"w_in_sb{i}") for i in range(2)]
    whi_done, wlo_done = sem("whi_done"), sem("wlo_done")
    unit_done = sem("unit_done")
    acc_free = [sem(f"acc_free{i}") for i in range(2)]
    sq_ready, sq_added = sem("sq_ready"), sem("sq_added")
    x_ready = sem("x_ready")
    rms_mm, rms_sqrt, rinv_ready = sem("rms_mm"), sem("rms_sqrt"), sem("rinv_ready")
    prod_ready, tms_ready, nhi_ready, hn_ready = sem("prod_ready"), sem("tms_ready"), sem("nhi_ready"), sem("hn_ready")
    silg_ready, hidp_ready, hhi_ready, hid_ready = sem("silg_ready"), sem("hidp_ready"), sem("hhi_ready"), sem("hid_ready")
    st_in, st_tr, st_done = sem("st_in"), sem("st_tr"), sem("st_done")
    dt_row_ready, dt_tr, dt_z_ready, dt_e_ready, dta_ready = (
        sem("dt_row_ready"), sem("dt_tr"), sem("dt_z_ready"), sem("dt_e_ready"), sem("dta_ready"))
    sums_mm, expo_ready = sem("sums_mm"), sem("expo_ready")
    pad0_ready, xpad_ready, conv_done, xcv_ready = sem("pad0_ready"), sem("xpad_ready"), sem("conv_done"), sem("xcv_ready")
    conv_tr, conv_tr_used = sem("conv_tr"), sem("conv_tr_used")
    tail_tr, tail_done, tail_out = sem("tail_tr"), sem("tail_done"), sem("tail_out")
    wd_ready, seg_done, gexp_done, cb_done, cbm_done = (
        sem("wd_ready"), sem("seg_done"), sem("gexp_done"), sem("cb_done"), sem("cbm_done"))
    g_ready, y_mm, yo_mm, yo_used, st_mm, y_done = (
        sem("g_ready"), sem("y_mm"), sem("yo_mm"), sem("yo_used"), sem("st_mm"), sem("y_done"))
    hst_ready = sem("hst_ready")
    hout_tr, hout_ready, hout_out = sem("hout_tr"), sem("hout_ready"), sem("hout_out")
    h0_in = [sem(f"h0_in{i}") for i in range(H0_RING)]
    h0_tr, h0T_ready, ys_mm, h1_mm, h1_ready = (
        sem("h0_tr"), sem("h0T_ready"), sem("ys_mm"), sem("h1_mm"), sem("h1_ready"))
    h1_out = [sem(f"h1_out{i}") for i in range(H0_RING)]
    bblk_ready, cblk_ready = sem("bblk_ready"), sem("cblk_ready")
    ssd_over = sem("ssd_over")
    ws_zero, ws_in, ws_blk_in, gm_vec_in = sem("ws_zero"), sem("ws_in"), sem("ws_blk_in"), sem("gm_vec_in")
    ws_tr, wm_ready = sem("ws_tr"), sem("wm_ready")
    gv_ready, vt_tr, vc_ready, vsq_ready, vvar_ready, vstd_ready, vn_ready, v_out = (
        sem("gv_ready"), sem("vt_tr"), sem("vc_ready"), sem("vsq_ready"), sem("vvar_ready"), sem("vstd_ready"),
        sem("vn_ready"), sem("v_out"))
    mix_mm, mix_used, gu_ready, gmp_ready, gmhi_ready, gm_ready = (
        sem("mix_mm"), sem("mix_used"), sem("gu_ready"), sem("gmp_ready"), sem("gmhi_ready"), sem("gm_ready"))
    yt_tr, yz_ready = sem("yt_tr"), sem("yz_ready")
    yp_ready, yhi_ready, yfm_split = sem("yp_ready"), sem("yhi_ready"), sem("yfm_split")
    of_ready, of_tr, of_done, y_out = sem("of_ready"), sem("of_tr"), sem("of_done"), sem("y_out")

    def halves(t):
        return t[:, :].rearrange("p (h x) -> p h x", h=2)[:, :, 0:HALF]

    def split2(ap):
        return ap.rearrange("p (h x) -> p h x", h=2)

    def tile(t, f):
        return t[:, bass.ds(f * TOK, TOK)]

    def kxn(w, k, n):
        return w[:, 0:k * n].rearrange("p (k n) -> p k n", n=n)

    def mod40(q, f):
        g = gate[:, q, bass.ds(f * GRP, GRP)]
        return g.rearrange("p (h g) -> p h g", h=2).unsqueeze(3).broadcast_to([P, 2, GRP // 2, DEC_SEQ])

    def by_group(ap3):
        return ap3.rearrange("p h (g t) -> p h g t", t=DEC_SEQ)

    def by_stream(ap, n=DEC_SEQ):
        return ap.rearrange("p (b t) -> p b t", t=n)

    ch_rows = [pC[0:2 * NSTR, i * BANK:i * BANK + ADA_COLS] for i in range(2)]
    ch_cols = [pB[:, i * BANK:i * BANK + 2 * NSTR] for i in range(2)]

    xdt, xds = sq[:, 0:HG * HDIM], xadd[:, 0:HG * HDIM]
    yt1, yt2 = tmp[0][:, 0:HG * HDIM], tmp[1][:, 0:HG * HDIM]
    hout = [rT[:, 0:BANK], ssum[:, 0:BANK]]
    bblk = btm[:, 0:ST, :].rearrange("p c n -> p (c n)")
    zs3 = zs[:, :].rearrange("p (f c n) -> p f c n", c=TT, n=P)
    ytm3 = ytm[:, :].rearrange("p (c n) -> p c n", c=TT)
    w1 = ffn_w1[0].rearrange("a (k p) n -> a p k n", p=P)
    w2 = ffn_w2[0].rearrange("a (k p) n -> a p k n", p=P)
    win = w_in[0].rearrange("(k p) n -> p k n", p=P)
    wout = w_out[0].rearrange("(k p) n -> p k n", p=P)
    wada = w_ada[0].rearrange("(k p) n -> p k n", p=P)
    wadaf = w_ada_final.rearrange("(k p) n -> p k n", p=P)
    ws_t = gm_ws[0].rearrange("h t s -> t h s")
    h0_d = state_ssm[0].rearrange("b (j h) p n -> j (h p) b n", h=2)
    h1_d = ssm_sample[0].rearrange("b (j h) p n -> j (h p) b n", h=2)
    hp_d = ssm_prompt[0, 0].rearrange("(j h) p n -> (h p) j n", h=2)

    ffn_units = sum(2 * kh + KD for kh in PARTS)
    U_F0 = 0
    U_DT = ffn_units
    U_X = U_DT + 1
    U_Z = U_X + CT
    U_V = U_Z + KD
    U_OG = U_V + 2 * KD
    U_OY = U_OG + KD
    U_F1 = U_OY + KD
    U_END = U_F1 + ffn_units

    acc_h0, acc_h1 = acc[U_V % 2], acc[(U_V + 1) % 2]

    def unit_tiles(n, i=0):
        n += 2 * i if isinstance(i, int) else 0
        for base in (U_F0, U_F1):
            for kh in PARTS:
                base += 2 * kh
                if base <= n < base + KD:
                    return kh
                base += KD
        return KD

    def part_unit(u0, part):
        return u0 + sum(2 * kh + KD for kh in PARTS[:part])

    def chunks_of(u0, part):
        if u0 == U_F0:
            return (CH_LAST if part == 2 else PARTS[part]), CH_PAIR[part]
        return (PARTS[0], ADA_MAIN) if part == 0 else (0, None)

    class Steps:

        def __init__(self, eng, s):
            self.eng, self.s, self.n, self.i, self.start, self.per = eng, s, 0, None, 0, 0

        def done(self, ins):
            ins.then_inc(self.s, 1)
            self.n += 1
            v = self.n if self.i is None else self.i * self.per + (self.n - self.start * self.per)
            self.eng.wait_ge(self.s, v)

    def repeat(eng, steps, per, start, stop, body):
        if stop - start == 1:
            body(start)
            return
        with eng.Fori(start, stop) as i:
            n0 = steps.n if steps else 0
            if steps:
                steps.i, steps.start, steps.per = i, start, per
            body(i)
            if steps:
                assert steps.n - n0 == per, (steps.n - n0, per)
                steps.n = n0 + per * (stop - start)
                steps.i = None

    def after_first(i):
        return not isinstance(i, int) or i > 0

    def repeat_peeled(eng, stop, body, n):
        if n == 0:
            body(0)
        repeat(eng, None, 0, int(n == 0), stop, body)

    def evacuated(eng, n, i=0):
        eng.wait_ge(acc_free[n % 2], i + (n // 2 + 1))

    def all_evacuated(eng, p, n):
        eng.wait_ge(acc_free[p], (n + 1 - p) // 2)

    def wait(eng, s, v):
        if not isinstance(v, int) or v > 0:
            eng.wait_ge(s, v)

    block = top.enter_context(nc.Block())

    @block.sync
    def _(sp):
        def first_col(col):
            return col if isinstance(col, int) else sp.snap(col)

        def load_unit(n, i, rows, col):
            col = first_col(col)
            wait(sp, wlo_done, n - 1 + i * 2)
            k = unit_tiles(n, i)
            sp.dma_start(kxn(wraw[n % 2], k, P), rows[:, :, bass.ds(col, P)]).then_inc(w_in_sb[n % 2], 16)

        def load_chunk(i, m, src, m0):
            col = first_col(i * ADA_COLS + (m - m0) * ADA_COLS)
            sp.wait_ge(ch_lo, i + m)
            sp.dma_start(kxn(sraw, KD, ADA_COLS), src[:, :, bass.ds(col, ADA_COLS)]).then_inc(s_in, 16)

        def load_ffn(u0, a):
            for part, kh in enumerate(PARTS):
                n, h0 = part_unit(u0, part), PART0[part]

                def pair(i, n=n, h0=h0, part=part, chunk=None, src=wada, m0=0):
                    if not isinstance(i, int) or n + i > U_F0:
                        load_unit(n, i, w1[a], i * P + h0 * P)
                    load_unit(n + 1, i, w1[a], i * P + (D_FF + h0 * P))
                    if chunk is not None:
                        load_chunk(i, chunk, src, m0)
                have = 0
                if u0 == U_F0:
                    have = CH_LAST if part == 2 else kh
                    if part == 0:
                        pair(0, chunk=CH_PAIR[0])
                    repeat(sp, None, 0, int(part == 0), have, lambda i: pair(i, chunk=CH_PAIR[part]))
                elif part == 0:
                    have = kh
                    repeat(sp, None, 0, 0, kh, lambda i: pair(i, chunk=ADA_MAIN, src=wadaf, m0=ADA_MAIN))
                if have < kh:
                    repeat(sp, None, 0, have, kh, pair)
                n += 2 * kh

                def down(i, n=n, h0=h0, kh=kh, part=part):
                    for d in range(2):
                        load_unit(n + d, i, w2[a, :, h0:h0 + kh, :], i * (2 * P) + d * P)
                    if u0 == U_F0 and part < 2:
                        load_chunk(i, CH_DOWN[part], wada, 0)
                repeat(sp, None, 0, 0, KD // 2, down)

        def load_two(n, src, col):
            def two(i):
                for d in range(2):
                    load_unit(n + d, i, src, i * (2 * P) + (col + d * P))
            return two

        def load_first(m):
            sp.dma_start(kxn(ada_raw[m % ADA_RING], KD, ADA_COLS),
                         wada[:, :, m * ADA_COLS:(m + 1) * ADA_COLS]).then_inc(ada_in[m % ADA_RING], 16)
        sp.dma_start(c_row[0:1, :], c_prompt).then_inc(setup_in, 16)
        sp.dma_start(c_row[1:NSTR, :], c_sample).then_inc(setup_in, 16)
        sp.dma_start(b_row[0:N_MOD * KD, :], b_ada[0].rearrange("(r c) -> r c", c=P)).then_inc(setup_in, 16)
        sp.dma_start(b_row[N_MOD * KD:MODT, :], b_ada_final.rearrange("(r c) -> r c", c=P)).then_inc(setup_in, 16)
        for r, src in ((R_NORM, norm_g[0].rearrange("a (r c) -> (a r) c", c=P)),
                       (R_FINAL, final_norm_g.rearrange("(r c) -> r c", c=P)),
                       (R_SSDN, ssd_norm_g[0].rearrange("(r c) -> r c", c=P)),
                       (R_CW, conv_w[0].rearrange("a (r c) -> (a r) c", c=P)),
                       (R_CB, conv_b[0].rearrange("(r c) -> r c", c=P))):
            sp.dma_start(p_row[r:r + src.shape[0], :], src).then_inc(setup_in, 16)
        for q, src in enumerate((dt_bias, a_log, d_skip)):
            sp.dma_start(vecs[:, q, :], src[0].partition_broadcast(P)).then_inc(vecs_in, 16)
        for c in range(TT):
            src = x_prompt[0, c * P:(c + 1) * P, :] if c < ST else x_sample.rearrange("b t d -> (b t) d")
            sp.dma_start(x_row[c][:, :], src).then_inc(x_in[c], 16)
        for m in range(ADA_RING):
            load_first(m)
        for m in range(ADA_RING, ADA_FIRST):
            sp.wait_ge(ch_lo, m + 1 - ADA_RING)
            load_first(m)
        load_unit(U_F0, 0, w1[0], 0)
        sp.wait_ge(ch_tr, ADA_FIRST)
        sp.wait_ge(xt_tr, TT)
        load_ffn(U_F0, 0)
        load_unit(U_DT, 0, win, COL_DT)
        sp.wait_ge(unit_done, U_DT)
        sp.dma_start(st_row[:, :], state_conv[0].rearrange("b k c -> (b k) c")).then_inc(st_in, 16)
        repeat(sp, None, 0, 0, CT // 2, load_two(U_X, win, COL_X))
        load_two(U_Z, win, COL_Z)(0)
        sp.wait_ge(tail_out, 32)
        for j in range(H0_RING):
            sp.dma_start(h0s[j][:, :, :], h0_d[j]).then_inc(h0_in[j], 16)
        repeat(sp, None, 0, 1, KD // 2, load_two(U_Z, win, COL_Z))
        for d, col in ((0, COL_V), (1, COL_U)):
            load_unit(U_V + d, 0, win, col)
        for j in range(H0_RING, HP):
            sp.wait_ge(h1_out[j % H0_RING], 16 * (j // H0_RING))
            sp.dma_start(h0s[j % H0_RING][:, :, :], h0_d[j]).then_inc(h0_in[j % H0_RING], 16)

        sp.wait_ge(ssd_over, 1)
        sp.dma_start(wst[:, :, :], ws_t).then_inc(ws_in, 16)
        sp.wait_ge(ws_zero, 1)
        for b in range(DEC_BATCH):
            r = slice(b * DEC_SEQ, (b + 1) * DEC_SEQ)
            sp.dma_start(wsb[r, :, r], ws_t[0:DEC_SEQ, :, 0:DEC_SEQ]).then_inc(ws_blk_in, 16)
        sp.dma_start(gm_g[:, :], gm_norm_g[0].partition_broadcast(P)).then_inc(gm_vec_in, 16)
        sp.dma_start(gm_bias[:, :], gm_b[0].rearrange("h t -> (h t)").partition_broadcast(P)).then_inc(gm_vec_in, 16)

        def vu(i):
            load_unit(U_V + 2, i, win, i * P + (COL_V + P))
            load_unit(U_V + 3, i, win, i * P + (COL_U + P))
        repeat(sp, None, 0, 0, KD - 1, vu)
        repeat(sp, None, 0, 0, KD // 2, load_two(U_OG, wout[:, 0:KD, :], 0))
        repeat(sp, None, 0, 0, KD // 2, load_two(U_OY, wout[:, KD:2 * KD, :], 0))
        load_ffn(U_F1, 1)

    @block.gpsimd
    def _(pool):
        st = Steps(pool, pool_step)

        def select(t, pattern, mult, base):
            st.done(nc.gpsimd.affine_select(out=t, in_=t, pattern=pattern, compare_op=ALU.is_ge, fill=0.0,
                                            base=base, channel_multiplier=mult))
        st.done(nc.gpsimd.memset(ident[:, :], 0.0))
        st.done(nc.gpsimd.affine_select(out=ident[:, :], in_=ident[:, :], pattern=[[-1, P]],
                                        compare_op=ALU.not_equal, fill=1.0, base=0, channel_multiplier=1))
        nc.gpsimd.memset(ones[:, :], 1.0)
        nc.gpsimd.memset(ones_mean[:, :], 1.0 / D_MODEL)
        nc.gpsimd.memset(eps_t[:, :], EPS)
        nc.gpsimd.memset(upto[:, :, :], 1.0)
        nc.gpsimd.memset(after[:, :, :], 1.0)
        st.done(nc.gpsimd.memset(stream_of[:, :], 1.0))
        select(upto[:, :, :], [[0, 2], [1, P]], -1, 0)
        select(after[:, :, :], [[0, 2], [-1, P]], 1, -1)
        for t in (upto, after):
            v = t[:, 1, :].rearrange("p (b t) -> p b t", t=DEC_SEQ)
            select(v, [[-DEC_SEQ, DEC_BATCH], [0, DEC_SEQ]], 1, 0)
            select(v, [[DEC_SEQ, DEC_BATCH], [0, DEC_SEQ]], -1, DEC_SEQ - 1)
        select(stream_of[:, :], [[-DEC_SEQ, DEC_BATCH]], 1, 0)
        select(stream_of[:, :], [[DEC_SEQ, DEC_BATCH]], -1, DEC_SEQ - 1)
        nc.gpsimd.tensor_tensor(out=pairsum[:, :], in0=ident[0:2 * NSTR, 0:NSTR],
                                in1=ident[0:2 * NSTR, NSTR:2 * NSTR], op=ALU.add).then_inc(masks_done, 1)

        def norm_samples(m, used0, shift, scale):
            pool.wait_ge(rinv_ready, m + 1)
            pool.wait_ge(mod_ready, (1, 2, 2, 2, 3)[m])
            for f in range(KD):
                t = tms[f % 2]
                if f >= 2:
                    used0(f - 2)
                tv = by_stream(t[:, :])
                st.done(nc.gpsimd.tensor_tensor(out=t[:, :], in0=xT[:, f * TOK + SEQ:(f + 1) * TOK],
                                                in1=rT[:, SEQ:TOK], op=ALU.mult))
                for op, q in ((ALU.mult, scale), (ALU.add, shift)):
                    v = modc[:, q + f, 1:NSTR].unsqueeze(2).broadcast_to([P, DEC_BATCH, DEC_SEQ])
                    ins = nc.gpsimd.tensor_tensor(out=tv, in0=tv, in1=v, op=op)
                    if op == ALU.mult:
                        st.done(ins)
                ins.then_inc(tms_ready, 1)

        norm_samples(0, lambda f: pool.wait_ge(hn_ready, f + 1), 0, KD)
        pool.wait_ge(unit_done, U_DT)
        for i in range(2):
            nc.gpsimd.memset(xpad[i][:, 0:CONV_W - 1], 0.0).then_inc(pad0_ready, 1)
        norm_samples(1, lambda f: pool.wait_ge(hn_ready, KD + f + 1), 3 * KD, 4 * KD)

        pool.wait_ge(tail_done, 1)
        pool.dma_start(conv_prompt[0, 0], tail_row[0:CONV_W - 1, :]).then_inc(tail_out, 16)
        pool.dma_start(conv_sample[0].rearrange("b k c -> (b k) c"), tail_row[CONV_W - 1:TAIL, :]).then_inc(tail_out, 16)
        for q in range(2):
            pool.wait_ge(hout_ready, q + 1)
            pool.dma_start(hp_d[:, q * HP // 2:(q + 1) * HP // 2, :], hout[q].rearrange("p (j n) -> p j n", n=NSTATE)
                           ).then_inc(hout_out, 16)
        for j in range(HP):
            pool.wait_ge(h1_ready, j + 1)
            pool.dma_start(h1_d[j], h0s[j % H0_RING][:, :, :]).then_inc(h1_out[j % H0_RING], 16)
        def v_store(i):
            pool.wait_ge(vn_ready, i + 1)
            pool.dma_start(gm_v_sample[0].rearrange("b t d -> (b t) d")[:, bass.ds(i * P, P)],
                           xadd[:, ST * P:TT * P]).then_inc(v_out, 16)
        repeat(pool, None, 0, 0, KD, v_store)
        pool.wait_ge(v_out, 16 * KD)
        norm_samples(3, lambda f: pool.wait_ge(hn_ready, 2 * KD + f + 1), 6 * KD, 7 * KD)
        norm_samples(4, lambda f: pool.wait_ge(of_ready, f + 1), 9 * KD, 10 * KD)
        for f in range(KD):
            pool.wait_ge(of_done, f + 1)
            cols = slice(f * P, (f + 1) * P)
            pool.dma_start(y_prompt[0].rearrange("(c p) d -> p c d", p=P)[:, :, cols],
                           y_row[:, 0:ST, cols]).then_inc(y_out, 16)
            pool.dma_start(y_sample.rearrange("b t d -> (b t) d")[:, cols], y_row[:, ST, cols]).then_inc(y_out, 16)
        pool.wait_ge(y_out, 2 * 16 * KD)

    @block.tensor
    def _(pe):
        mm = nc.tensor.matmul

        def unit(n, i, hi, lo, k_ready, ks=None):
            p, kt = n % 2, unit_tiles(n, i)
            wh, wl = kxn(whi[p], kt, P), kxn(wlo[p], kt, P)
            ks = range(kt) if ks is None else ks
            if ks[0] == 0:
                pe.wait_ge(wlo_done, i * 2 + (n + 1))
                wait(pe, acc_free[p], i + n // 2)
            for k in ks:
                k_ready(k)
                for t, (w, a) in enumerate(((wh, hi), (wh, lo), (wl, hi))):
                    for h in range(2):
                        last = mm(acc[p][:, h * BANK:h * BANK + HALF], w[:, k, :],
                                  a[:, k * TOK + h * HALF:k * TOK + (h + 1) * HALF],
                                  start=(k == 0 and t == 0), stop=(k == kt - 1 and t == 2))
            if ks[-1] == kt - 1:
                last.then_inc(unit_done, 1)

        def hn_wait(m):
            return lambda k: pe.wait_ge(hn_ready, m * KD + k + 1)

        def rms(m):
            pe.wait_ge(sq_added, (m + 1) * KD)
            for h in range(2):
                last = mm(pC[:, h * BANK:h * BANK + HALF], ones_mean[:, :], ssum[:, h * HALF:(h + 1) * HALF],
                          start=True, stop=True)
            last.then_inc(rms_mm, 1)

        def to_tokens(out, src, used, v):
            wait(pe, used, v)
            for c in range(TT):
                last = nc.tensor.transpose(out[:, c * P:(c + 1) * P], src[:, c * P:(c + 1) * P], ident[:, :])
            return last

        pe.wait_ge(masks_done, 1)
        pe.wait_ge(c_silu, 1)
        for k in range(KD):
            last = mm(pB[:, k * NSTR:(k + 1) * NSTR], c_sil[0:NSTR, k * P:(k + 1) * P], ident[0:NSTR, 0:NSTR],
                      start=True, stop=True)
        last.then_inc(c_tr, 1)
        mm(pB[:, BANK:BANK + MODT], b_row[0:MODT, :], ident[0:MODT, 0:MODT], start=True, stop=True)
        mm(pB[:, BANK + P:BANK + P + N_PAR], p_row[0:N_PAR, :], ident[0:N_PAR, 0:N_PAR],
           start=True, stop=True).then_inc(par_tr, 1)
        for c in range(TT):
            pe.wait_ge(x_in[c], 16)
            wait(pe, xt_done, c - 1)
            for f in range(KD):
                last = nc.tensor.transpose(acc[c % 2][:, f * P:(f + 1) * P], x_row[c][:, f * P:(f + 1) * P],
                                           ident[:, :])
            last.then_inc(xt_tr, 1)

        pe.wait_ge(c_split, 1)

        def chunk_rows(i, m, bank, wh, wl):
            pe.wait_ge(ch_lo, i + (m + 1))
            for k in range(KD):
                for t, w in enumerate((wh, wl)):
                    last = mm(ch_rows[bank], c_hl[:, k, :], kxn(w, KD, ADA_COLS)[:, k, :],
                              start=(k == 0 and t == 0), stop=(k == KD - 1 and t == 1))
            last.then_inc(ch_mm, 1)

        def chunk_cols(i, m, bank, row):
            pe.wait_ge(ch_row, i + (m + 1))
            for f in range(2):
                last = mm(ch_cols[bank][:, f * NSTR:(f + 1) * NSTR], row[:, f * P:(f + 1) * P], pairsum[:, :],
                          start=True, stop=True)
            last.then_inc(ch_tr, 1)

        for m in range(ADA_FIRST + 1):
            if m < ADA_FIRST:
                wait(pe, ch_row, m - 1)
                chunk_rows(0, m, m % 2, ada_hi[m % 2], ada_lo[m % 2])
            if m:
                wait(pe, ch_sum, m - 2)
                chunk_cols(0, m - 1, (m - 1) % 2, ada_row[(m - 1) % 2])

        def ffn(u0, m, t0):
            first_one = u0 == U_F0
            for part, kh in enumerate(PARTS):
                n = part_unit(u0, part)

                def pair(i, n=n, chunk=None):
                    unit(n, i, hn_hi, hn_lo, hn_wait(m))
                    if chunk is not None:
                        chunk_rows(i, chunk, 0, shi, slo)
                    unit(n + 1, i, hn_hi, hn_lo, lambda k: None)
                    if chunk is not None:
                        pe.wait_ge(ch_sum, i + chunk)
                        chunk_cols(i, chunk, 0, srow)
                have, chunk = chunks_of(u0, part)
                if have:
                    repeat_peeled(pe, have, lambda i: pair(i, chunk=chunk), n)
                if have < kh:
                    repeat(pe, None, 0, have, kh, pair)

                def hid_wait(k, have=t0 + PART0[part], kh=kh):
                    if k in (0, kh - 1):
                        pe.wait_ge(hid_ready, have + (kh if k else kh - 1))

                def down(i, n=n + 2 * kh, part=part):
                    chunk = CH_DOWN[part] if first_one and part < 2 else None
                    unit(n, i, hid_hi, hid_lo, hid_wait)
                    if chunk is not None:
                        chunk_rows(i, chunk, 0, shi, slo)
                    unit(n + 1, i, hid_hi, hid_lo, hid_wait)
                    if chunk is not None:
                        pe.wait_ge(ch_sum, i + chunk)
                        chunk_cols(i, chunk, 0, srow)
                repeat(pe, None, 0, 0, KD // 2, down)

        rms(0)
        ffn(U_F0, 0, 0)
        rms(1)

        unit(U_DT, 0, hn_hi, hn_lo, hn_wait(1))
        pe.wait_ge(st_in, 16)
        for j in range(CT):
            last = mm(pB[:, j * 24:(j + 1) * 24], st_row[0:24, j * P:(j + 1) * P], ident[0:24, 0:24],
                      start=True, stop=True)
        last.then_inc(st_tr, 1)
        pe.wait_ge(st_done, 1)

        def conv_tr_tile(p, i, j, src=None):
            pe.wait_ge(xcv_ready, i * 2 + (j + 1))
            to_tokens(pB, tmp[p] if src is None else src, conv_tr_used, i * 2 + j).then_inc(conv_tr, 1)

        def x_pair(i):
            if after_first(i):
                unit(U_X, i, hn_hi, hn_lo, lambda k: None)
                conv_tr_tile(1, i, -1)
            else:
                unit(U_X, i, hn_hi, hn_lo, lambda k: None)
            unit(U_X + 1, i, hn_hi, hn_lo, lambda k: None)
            conv_tr_tile(0, i, 0)
        x_pair(0)
        evacuated(pe, U_DT)
        for c in range(TT):
            last = mm(pC[:, c * 32:(c + 1) * 32], sq[96:P, c * P:(c + 1) * P], ident[96:P, 96:P],
                      start=True, stop=True)
        last.then_inc(dt_tr, 1)
        repeat(pe, None, 0, 1, XT_ // 2, x_pair)
        for j in range(XT_, CT):
            unit(U_X + j, 0, hn_hi, hn_lo, lambda k: None)
            if j - 1 < XT_:
                conv_tr_tile((j - 1) % 2, 0, j - 1)
            elif j - 1 < XT_ + SSD_G:
                conv_tr_tile(0, 0, j - 1, bcf[:, j - 1 - XT_, :])
        pe.wait_ge(conv_done, CT)
        all_evacuated(pe, 1, U_Z)
        pe.wait_ge(dt_z_ready, 1)
        for j in range(CT):
            dst = (acc[1][0:TAIL, j * P:(j + 1) * P] if j < 8 else pC[0:TAIL, (j - 8) * P:(j - 7) * P])
            last = mm(dst, tails[:, j, :], ident[:, :], start=True, stop=True)
        last.then_inc(tail_tr, 1)
        pe.wait_ge(xcv_ready, CT)
        pe.wait_ge(conv_tr_used, XT_ + SSD_G)
        for s in range(TT * SSD_G):
            c, g = divmod(s, SSD_G)
            tok = slice(c * P, (c + 1) * P)
            dst = pB[:, s * P:(s + 1) * P] if c < ST else pC[:, BANK + g * P:BANK + (g + 1) * P]
            last = mm(dst, bcf[:, g, tok], bcf[:, SSD_G + g, tok], start=True, stop=True)
        last.then_inc(cb_done, 1)

        pe.wait_ge(wd_ready, 1)
        pe.wait_ge(tail_done, 1)
        nh = TT * HEADS
        np_ = ST * HEADS
        for q, mask in enumerate((upto, after)):
            mm(pC[:, q * nh:q * nh + np_], mask[:, 0, :], dt_a[:, 0:np_], start=True, stop=True)
            mm(pC[:, q * nh + np_:(q + 1) * nh], mask[:, 1, :], dt_a[:, np_:nh], start=True, stop=True)
        mm(pC[:, 2 * nh:3 * nh], ones[:, :], dt_a[:, :], start=True, stop=True)
        for j in range(HP):
            last = mm(pC[:, 3 * nh + j * DEC_BATCH:3 * nh + (j + 1) * DEC_BATCH],
                      wd[:, :, :].rearrange("p a b -> p (a b)")[:, j * P:(j + 1) * P], stream_of[:, :],
                      start=True, stop=True)
        last.then_inc(sums_mm, 1)

        def seg(s):
            pe.wait_ge(wd_ready, s + 2)
            wait(pe, gexp_done, s)
            for q in range(2):
                last = mm(pB[:, q * BANK:(q + 1) * BANK], after[:, int(s >= ST * SSD_G), :],
                          wd[:, 4 * q:4 * q + 4, :].rearrange("p a b -> p (a b)"), start=True, stop=True)
            last.then_inc(seg_done, 1)

        def within(s):
            pe.wait_ge(g_ready, s + 1)
            wait(pe, y_done, s)
            for h in range(HG):
                last = mm(pC[:, h * HDIM:(h + 1) * HDIM], gd[:, h, :], xdt[:, h * HDIM:(h + 1) * HDIM],
                          start=True, stop=True)
            last.then_inc(y_mm, 1)

        pe.wait_ge(cbm_done, 2)
        for s in range(ST * SSD_G):
            c, g = divmod(s, SSD_G)
            seg(s)
            if c:
                pe.wait_ge(hst_ready, s)
                mm(pC[:, BANK:2 * BANK], bcf[:, SSD_G + g, c * P:(c + 1) * P], hst[:, g * BANK:(g + 1) * BANK],
                   start=True, stop=True).then_inc(yo_mm, 1)

            def inner(k, s=s, c=c, g=g):
                if k == KD // 2:
                    within(s)
                    if c:
                        pe.wait_ge(yo_used, s + 1 - SSD_G)
                    else:
                        wait(pe, hst_ready, s)
                    mm(pC[:, BANK:2 * BANK], btm[:, c, g * P:(g + 1) * P], xds, start=True, stop=True
                       ).then_inc(st_mm, 1)
            unit(U_Z + s, 0, hn_hi, hn_lo, inner)

        pe.wait_ge(hst_ready, ST * SSD_G)
        pe.wait_ge(gexp_done, ST * SSD_G)
        for j in range(HP):
            last = nc.tensor.transpose(pB[:, j * P:(j + 1) * P], hst[:, j * P:(j + 1) * P], ident[:, :])
        last.then_inc(hout_tr, 1)

        def state_tr(j):
            pe.wait_ge(h0_in[j % H0_RING], 16 * (j // H0_RING + 1))
            wait(pe, h0T_ready, j)
            for b in range(DEC_BATCH):
                last = nc.tensor.transpose(acc_h0[:, b * P:(b + 1) * P], h0s[j % H0_RING][:, b, :], ident[:, :])
            last.then_inc(h0_tr, 1)

        all_evacuated(pe, U_V % 2, U_V)
        state_tr(0)
        pe.wait_ge(hout_ready, 2)
        seg(ST * SSD_G)
        all_evacuated(pe, (U_V + 1) % 2, U_V)
        for j in range(HP):
            g, jj = divmod(j, HP // SSD_G)
            pe.wait_ge(bblk_ready, g + 1)
            wait(pe, h1_ready, j)
            for q in range(2):
                last = mm(acc_h1[:, q * BANK:(q + 1) * BANK], xds[:, jj * P:(jj + 1) * P],
                          bblk[:, q * BANK:(q + 1) * BANK], start=True, stop=True)
            last.then_inc(h1_mm, 1)
            if j + 1 < HP:
                state_tr(j + 1)
            pe.wait_ge(h0T_ready, j + 1)
            pe.wait_ge(cblk_ready, g + 1)
            if jj == 0 and g:
                pe.wait_ge(y_done, ST * SSD_G + g)
            for b in range(DEC_BATCH):
                last = mm(pC[:, BANK + jj * P:BANK + (jj + 1) * P], hst[:, b * P:(b + 1) * P], h0T[:, b, :],
                          start=(b == 0), stop=(b == DEC_BATCH - 1))
            last.then_inc(ys_mm, 1)
            if jj == 0:
                within(ST * SSD_G + g)
                if g == 0:
                    seg(ST * SSD_G + 1)

        def y_tile(k):
            if k == 0:
                pe.wait_ge(y_done, TT * SSD_G)
                pe.wait_ge(gexp_done, TT * SSD_G)
            dst = (pB, pC)[k % 2]
            wait(pe, yz_ready, k - 1)
            for c in range(TT):
                last = nc.tensor.transpose(dst[:, c * P:(c + 1) * P], ytm3[:, c, k * P:(k + 1) * P], ident[:, :])
            last.then_inc(yt_tr, 1)

        def ws_tile(h):
            if h == 0:
                pe.wait_ge(yz_ready, KD)
                pe.wait_ge(ws_in, 16)
                pe.wait_ge(ws_blk_in, 16 * DEC_BATCH)
            for dst, src in ((pB, wst), (pC, wsb)):
                last = nc.tensor.transpose(dst[:, h * P:(h + 1) * P], src[:, h, :], ident[:, :])
            if h == 7:
                last.then_inc(ws_tr, 1)

        def mix(h):
            pe.wait_ge(vn_ready, h + 1)
            wait(pe, mix_used, h)
            for c in range(TT):
                last = mm(pC[:, c * P:(c + 1) * P], xadd[:, c * P:(c + 1) * P],
                          wmT[:, int(c == ST), bass.ds(h * P, P)], start=True, stop=True)
            last.then_inc(mix_mm, 1)

        def vu(i):
            unit(U_V, i, hn_hi, hn_lo, lambda k: None)
            mix(i - 1)
            unit(U_V + 1, i, hn_hi, hn_lo, lambda k: None)
            evacuated(pe, U_V, i)
            to_tokens(pB, tmp[0], vc_ready, i).then_inc(vt_tr, 1)
        pe.wait_ge(h0T_ready, HP)
        unit(U_V, 0, hn_hi, hn_lo, lambda k: y_tile(k - 1) if k else None)
        y_tile(KD - 1)
        pe.wait_ge(h1_ready, HP)
        unit(U_V + 1, 0, hn_hi, hn_lo, lambda k: ws_tile(k - 1) if k else None)
        ws_tile(KD - 1)
        evacuated(pe, U_V)
        pe.wait_ge(wm_ready, 2)
        to_tokens(pB, tmp[0], vc_ready, 0).then_inc(vt_tr, 1)
        vu(1)
        repeat(pe, None, 0, 2, KD, vu)

        for d in range(2):
            unit(U_OG + d, 0, gm_hi, gm_lo, lambda k: pe.wait_ge(gm_ready, KD - 1), ks=range(KD - 1))
            if d == 0:
                mix(KD - 1)
        pe.wait_ge(gm_ready, KD)
        for d in range(2):
            unit(U_OG + d, 0, gm_hi, gm_lo, lambda k: None, ks=(KD - 1,))
        rms(2)

        def og(i):
            for d in range(2):
                unit(U_OG + d, i, gm_hi, gm_lo, lambda k: None)
        repeat(pe, None, 0, 1, KD // 2, og)

        def oy(i):
            for d in range(2):
                unit(U_OY + d, i, hn_hi, hn_lo, lambda k: pe.wait_ge(yfm_split, k + 1))
        repeat(pe, None, 0, 0, KD // 2, oy)

        rms(3)
        ffn(U_F1, 2, FF_TILES)
        rms(4)
        for f in range(KD):
            if f < 2:
                all_evacuated(pe, f, U_END)
            pe.wait_ge(of_ready, f + 1)
            to_tokens(acc[f % 2], y_fm[f % 2], of_done, f - 1).then_inc(of_tr, 1)

    @block.scalar
    def _(act):
        st = Steps(act, act_step)
        A = nc.scalar.activation

        def hi(n, i=0):
            if isinstance(i, int) and n + 2 * i >= U_END:
                return
            p, w = n % 2, unit_tiles(n, i) * P
            act.wait_ge(w_in_sb[p], i * 16 + 16 * (n // 2 + 1))
            wait(act, unit_done, i * 2 + (n - 1))
            A(whi[p][:, 0:w], wraw[p][:, 0:w], ACT.Copy).then_inc(whi_done, 1)

        def done(n, i=0):
            act.wait_ge(unit_done, i * 2 + (n + 1))

        def rms_root(m):
            act.wait_ge(rms_mm, m + 1)
            A(split2(rT[:, :]), halves(pC), ACT.Sqrt, bias=eps_t[:, 0:1]).then_inc(rms_sqrt, 1)

        def norm(m, hn0, shift, dst=None):
            for f in range(KD):
                b = modc[:, shift + f, 0:1]
                if dst is None:
                    act.wait_ge(prod_ready, prod0[0] + f + 1)
                    A(hn_hi[:, f * TOK:f * TOK + SEQ], tmp[f % 2][:, 0:SEQ], ACT.Identity, bias=b)
                    act.wait_ge(tms_ready, tms0[0] + f + 1)
                    A(hn_hi[:, f * TOK + SEQ:(f + 1) * TOK], tms[f % 2][:, :], ACT.Copy).then_inc(nhi_ready, 1)
                else:
                    act.wait_ge(prod_ready, prod0[0] + f + 1)
                    wait(act, of_tr, f - 1)
                    A(dst[f % 2][:, 0:SEQ], tmp[f % 2][:, 0:SEQ], ACT.Identity, bias=b)
                    act.wait_ge(tms_ready, tms0[0] + f + 1)
                    A(dst[f % 2][:, SEQ:TOK], tms[f % 2][:, :], ACT.Copy).then_inc(of_ready, 1)
            prod0[0] += KD
            tms0[0] += KD
        prod0, tms0 = [0], [0]

        act.wait_ge(setup_in, 16 * 9)
        A(c_sil[:, :], c_row[:, :], ACT.Silu).then_inc(c_silu, 1)
        act.wait_ge(vecs_in, 48)
        st.done(A(vecs[:, 1, :], vecs[:, 1, :], ACT.Exp))
        act.wait_ge(c_tr, 1)
        A(c_hl[:, :, 0:NSTR], pB[:, 0:KD * NSTR].rearrange("p (k c) -> p k c", c=NSTR), ACT.Copy).then_inc(c_used, 1)
        def copy_x(c):
            act.wait_ge(xt_tr, c + 1)
            A(xT[:, :].rearrange("p (f t) -> p f t", t=TOK)[:, :, c * P:(c + 1) * P],
              acc[c % 2][:, :].rearrange("p (f t) -> p f t", t=P), ACT.Copy).then_inc(xt_done, 1)

        def chunk_hi(i, m, dst, src):
            A(dst[:, :], src[:, :], ACT.Copy).then_inc(ch_hi, 1)

        def chunk_row(i, m, bank, row):
            act.wait_ge(ch_mm, i + (m + 1))
            A(row[:, :], ch_rows[bank], ACT.Copy).then_inc(ch_row, 1)

        for c in range(TT):
            copy_x(c)
        act.wait_ge(xt_done, TT)
        for m in range(ADA_FIRST):
            act.wait_ge(ada_in[m % ADA_RING], 16 * (m // ADA_RING + 1))
            wait(act, ch_mm, m - 1)
            chunk_hi(0, m, ada_hi[m % 2], ada_raw[m % ADA_RING])
            wait(act, sq_added, m)
            A(sq[:, :], tile(xT, m), ACT.Square).then_inc(sq_ready, 1)
            if m:
                wait(act, ch_tr, m - 2)
                chunk_row(0, m - 1, (m - 1) % 2, ada_row[(m - 1) % 2])
        act.wait_ge(ch_tr, ADA_FIRST - 2)
        chunk_row(0, ADA_FIRST - 1, (ADA_FIRST - 1) % 2, ada_row[(ADA_FIRST - 1) % 2])

        def stream_hi(i, m):
            act.wait_ge(s_in, i * 16 + 16 * (m - ADA_FIRST + 1))
            if not (isinstance(i, int) and m == ADA_FIRST):
                act.wait_ge(ch_mm, i + m)
            chunk_hi(i, m, shi, sraw)

        def stream_row(i, m):
            if not (isinstance(i, int) and m == ADA_FIRST):
                act.wait_ge(ch_tr, i + m)
            chunk_row(i, m, 0, srow)

        def ffn(u0, t0, squares):
            first_one = u0 == U_F0
            for part, kh in enumerate(PARTS):
                n = part_unit(u0, part)
                h0 = t0 + PART0[part]

                def pair(i, n=n, h0=h0, chunk=None):
                    if chunk is not None:
                        stream_hi(i, chunk)
                    hi(n + 1, i)
                    done(n, i)
                    wait(act, hid_ready, i + h0)
                    A(split2(silg[:, :]), halves(acc[n % 2]), ACT.Silu).then_inc(acc_free[n % 2], 1)
                    hi(n + 2, i)
                    if chunk is not None:
                        stream_row(i, chunk)
                    evacuated(act, n + 1, i)
                    A(tile(hid_hi, i), hidp[:, :], ACT.Copy).then_inc(hhi_ready, 1)
                have, chunk = chunks_of(u0, part)
                if have:
                    repeat_peeled(act, min(have, kh - 1), lambda i: pair(i, chunk=chunk), n)
                if have < kh - 1:
                    repeat(act, None, 0, have, kh - 1, pair)
                pair(kh - 1, chunk=chunk if have == kh else None)
                n += 2 * kh

                def down(i, n=n, last=(part == 2), part=part):
                    chunk = CH_DOWN[part] if first_one and part < 2 else None
                    if chunk is not None:
                        stream_hi(i, chunk)
                    for d in range(2):
                        hi(n + d + 1, i)
                        if d == 0 and chunk is not None:
                            stream_row(i, chunk)
                        if last:
                            act.wait_ge(x_ready, i * 2 + (x0[0] + d + 1))
                            act.wait_ge(sq_added, i * 2 + (squares + d))
                            A(sq[:, :], tile(xT, i * 2 + d), ACT.Square).then_inc(sq_ready, 1)
                repeat(act, None, 0, 0, KD // 2 - 1, down)
                down(KD // 2 - 1)
            x0[0] += KD
        x0 = [0]

        hi(U_F0)
        rms_root(0)
        act.wait_ge(mod_ready, 1)
        norm(0, 0, 0)
        ffn(U_F0, 0, KD)
        rms_root(1)
        act.wait_ge(mod_ready, 2)
        norm(1, 0, 3 * KD)

        hi(U_DT + 1)
        done(U_DT)
        A(sq[96:P, :].rearrange("p (h x) -> p h x", h=2), halves(acc[U_DT % 2])[96:P], ACT.Copy
          ).then_inc(acc_free[U_DT % 2], 1)
        act.wait_ge(st_tr, 1)
        A(stT[:, :, :], pB[:, 0:CT * 24].rearrange("p (j r) -> p j r", r=24), ACT.Copy).then_inc(st_done, 1)

        def xbc(n, i, j, last=False):
            p = n % 2
            b = j % 2
            hi(n + 1, i)
            done(n, i)
            wait(act, conv_done, i * 2 + (j - 1))
            A(xpad[b][:, 3:3 + HALF], acc[p][:, 0:HALF], ACT.Copy)
            A(xpad[b][:, 3 + HALF:PAD_P], acc[p][:, BANK:BANK + SEQ - HALF], ACT.Copy)
            A(by_stream(xpad[b][:, PAD_P:PAD], PAD_S)[:, :, 3:PAD_S],
              by_stream(acc[p][:, BANK + SEQ - HALF:BANK + HALF]), ACT.Copy).then_inc(acc_free[p], 1)
            act.wait_ge(conv_done, i * 2 + (j + 1))
            if j < XT_:
                dst = tmp[b]
                wait(act, conv_tr, i * 2 + (j - 1))
            else:
                dst = bcf[:, j - XT_, :]
            A(dst[:, 0:SEQ], cacc[:, 0:SEQ], ACT.Silu)
            A(by_stream(dst[:, SEQ:TOK]), by_stream(cacc[:, PAD_P:PAD], PAD_S)[:, :, 0:DEC_SEQ],
              ACT.Silu).then_inc(xcv_ready, 1)

        def conv_out(i, j):
            act.wait_ge(conv_tr, i * 2 + (j + 1))
            if j < XT_:
                dst = ytm3[:, :, bass.ds(i * 2 * P + j * P, P)]
            else:
                dst = btm[:, :, (j - XT_) * P:(j - XT_ + 1) * P]
            A(dst, pB[:, 0:TOK].rearrange("p (c n) -> p c n", c=TT), ACT.Copy).then_inc(conv_tr_used, 1)

        def x_pair(i):
            xbc(U_X, i, 0)
            if after_first(i):
                conv_out(i, -1)
            xbc(U_X + 1, i, 1)
            conv_out(i, 0)
        x_pair(0)
        repeat(act, None, 0, 1, XT_ // 2, x_pair)
        for j in range(XT_, CT):
            xbc(U_X + j, 0, j)
            if j - 1 < XT_ + SSD_G:
                conv_out(0, j - 1)
        act.wait_ge(dt_z_ready, 1)
        st.done(A(dt_e[:, :], dt_z[:, :], ACT.Abs))
        st.done(A(dt_e[:, :], dt_e[:, :], ACT.Exp, scale=-1.0))
        A(dt_e[:, :], dt_e[:, :], ACT.Ln, bias=1.0).then_inc(dt_e_ready, 1)
        act.wait_ge(tail_tr, 1)
        A(tail_row[:, 0:2 * BANK], acc[1][0:TAIL, :], ACT.Copy)
        A(tail_row[:, 2 * BANK:CONV_DIM], pC[0:TAIL, 0:CONV_DIM - 2 * BANK], ACT.Copy).then_inc(tail_done, 1)

        nh = TT * HEADS
        act.wait_ge(sums_mm, 1)
        A(expo[:, :, :].rearrange("p a b -> p (a b)"), pC[:, 0:3 * nh], ACT.Exp)
        A(decs[:, :, :].rearrange("p a b -> p (a b)"), pC[:, 3 * nh:3 * nh + HP * DEC_BATCH], ACT.Exp
          ).then_inc(expo_ready, 1)

        def decay(s):
            act.wait_ge(seg_done, s + 1)
            wait(act, y_mm, s)
            A(gd[:, :, :].rearrange("p a b -> p (a b)"), pB[:, :], ACT.Exp).then_inc(gexp_done, 1)

        def silu_z(j):
            n = U_Z + j
            done(n)
            A(split2(tile(zs, j)), halves(acc[n % 2]), ACT.Silu).then_inc(acc_free[n % 2], 1)
        for s in range(ST * SSD_G):
            decay(s)
            hi(U_Z + s + 1)
            if s:
                silu_z(s - 1)
        silu_z(KD - 1)
        act.wait_ge(hout_tr, 1)
        for q in range(2):
            A(hout[q], pB[:, q * BANK:(q + 1) * BANK], ACT.Copy).then_inc(hout_ready, 1)
        for j in range(HP):
            act.wait_ge(h0_tr, j + 1)
            wait(act, ys_mm, j)
            A(h0T[:, :, :].rearrange("p a b -> p (a b)"), acc_h0[:, :], ACT.Copy).then_inc(h0T_ready, 1)
            if j < SSD_G:
                decay(ST * SSD_G + j)

        def v_stats(h):
            act.wait_ge(vc_ready, h + 1)
            A(sq[:, :], tmp[1][:, :], ACT.Square).then_inc(vsq_ready, 1)
            act.wait_ge(vvar_ready, h + 1)
            A(stat[:, 3, :], stat[:, 2, :], ACT.Sqrt, bias=eps_t[:, 0:1], scale=1.0 / P).then_inc(vstd_ready, 1)

        def gm_hi_part(h):
            act.wait_ge(gmp_ready, h + 1)
            A(tile(gm_hi, h), gmp[:, :], ACT.Copy).then_inc(gmhi_ready, 1)

        def vu(i):
            first = not after_first(i)
            hi(U_V + 1, i)
            if first:
                for j in range(KD):
                    act.wait_ge(yz_ready, j + 1)
                    wait(act, sq_added, 2 * KD + j)
                    A(sq[:, :].rearrange("p (c n) -> p c n", c=TT), ytm3[:, :, j * P:(j + 1) * P], ACT.Square
                      ).then_inc(sq_ready, 1)
            else:
                v_stats(i - 1)
            done(U_V, i)
            wait(act, vt_tr, i)
            A(split2(tmp[0][:, :]), halves(acc[U_V % 2]), ACT.Gelu_apprx_tanh).then_inc(acc_free[U_V % 2], 1)
            hi(U_V + 2, i)
            if not first:
                gm_hi_part(i - 1)
            if first:
                for j in range(H0_RING):
                    act.wait_ge(h1_out[j], 16 * (HP // H0_RING))
            done(U_V + 1, i)
            A(split2(gu[:, :]), halves(acc[(U_V + 1) % 2]), ACT.Gelu_apprx_tanh).then_inc(acc_free[(U_V + 1) % 2], 1)
        vu(0)
        vu(1)
        repeat(act, None, 0, 2, KD, vu)

        hi(U_OG + 1)
        v_stats(KD - 1)
        gm_hi_part(KD - 1)
        hi(U_OG + 2)
        hi(U_OG + 3)
        rms_root(2)
        for f in range(KD):
            act.wait_ge(yp_ready, f + 1)
            A(tile(hn_hi, f), tmp[f % 2][:, :], ACT.Copy).then_inc(yhi_ready, 1)
            if f + 2 < KD:
                hi(U_OG + f + 4)
        for f in range(KD):
            if f:
                hi(U_OY + f + 1)
            act.wait_ge(x_ready, x0[0] + f + 1)
            wait(act, sq_added, 3 * KD + f)
            A(sq[:, :], tile(xT, f), ACT.Square).then_inc(sq_ready, 1)
        x0[0] += KD
        rms_root(3)
        norm(3, 0, 6 * KD)
        ffn(U_F1, FF_TILES, 4 * KD)
        rms_root(4)
        act.wait_ge(mod_ready, 3)
        norm(4, 0, 9 * KD, y_fm)

    @block.vector
    def _(dve):
        V = nc.vector
        st = Steps(dve, dve_step)

        def lo(n, i=0):
            if isinstance(i, int) and n + 2 * i >= U_END:
                return
            p, w = n % 2, unit_tiles(n, i) * P
            dve.wait_ge(whi_done, i * 2 + (n + 1))
            V.tensor_tensor(out=wlo[p][:, 0:w], in0=wraw[p][:, 0:w], in1=whi[p][:, 0:w].bitcast(F32),
                            op=ALU.subtract).then_inc(wlo_done, 1)

        def done(n, i=0):
            dve.wait_ge(unit_done, i * 2 + (n + 1))

        def add_gated(n, i, f, q, count_x):
            done(n, i)
            g = by_group(split2(xadd[:, :]))
            V.tensor_tensor(out=g, in0=by_group(halves(acc[n % 2])), in1=mod40(q, f), op=ALU.mult
                            ).then_inc(acc_free[n % 2], 1)
            evacuated(dve, n, i)
            x = tile(xT, f)
            ins = V.tensor_tensor(out=x, in0=x, in1=xadd[:, :], op=ALU.add)
            if count_x:
                ins.then_inc(x_ready, 1)
            else:
                st.done(ins)

        def add_square(k, fresh=False):
            dve.wait_ge(sq_ready, k + 1)
            V.tensor_tensor(out=ssum[:, :], in0=ssum[:, :], in1=sq[:, :], op=ALU.add).then_inc(sq_added, 1)

        def r_of(m):
            dve.wait_ge(rms_sqrt, m + 1)
            V.reciprocal(out=rT[:, :], in_=rT[:, :]).then_inc(rinv_ready, 1)
            st.done(V.memset(ssum[:, :], 0.0))
            dve.wait_ge(rinv_ready, m + 1)

        def norm(shift, scale, to_hn=True):
            def prod(f):
                V.scalar_tensor_tensor(out=tmp[f % 2][:, 0:SEQ], in0=xT[:, f * TOK:f * TOK + SEQ],
                                       scalar=modc[:, scale + f, 0:1], in1=rT[:, 0:SEQ],
                                       op0=ALU.mult, op1=ALU.mult).then_inc(prod_ready, 1)
            prod(0)
            for f in range(KD):
                if f + 1 < KD:
                    if f >= 1:
                        dve.wait_ge(*((hn_ready, nhi0[0] + f) if to_hn else (of_ready, f)))
                    prod(f + 1)
                if not to_hn and f:
                    result(f - 1)
                if not to_hn:
                    continue
                dve.wait_ge(nhi_ready, nhi0[0] + f + 1)
                a, b, c = f * TOK, f * TOK + SEQ, (f + 1) * TOK
                V.scalar_tensor_tensor(out=hn_lo[:, a:b], in0=tmp[f % 2][:, 0:SEQ], scalar=modc[:, shift + f, 0:1],
                                       in1=hn_hi[:, a:b].bitcast(F32), op0=ALU.add, op1=ALU.subtract)
                V.tensor_tensor(out=hn_lo[:, b:c], in0=tms[f % 2][:, :], in1=hn_hi[:, b:c].bitcast(F32),
                                op=ALU.subtract).then_inc(hn_ready, 1)
            nhi0[0] += KD
        nhi0 = [0]

        dve.wait_ge(c_used, 1)
        V.tensor_tensor(out=c_hl[:, :, NSTR:2 * NSTR], in0=pB[:, 0:KD * NSTR].rearrange("p (k c) -> p k c", c=NSTR),
                        in1=c_hl[:, :, 0:NSTR].bitcast(F32), op=ALU.subtract).then_inc(c_split, 1)
        dve.wait_ge(par_tr, 1)
        V.tensor_copy(b_col[:, :], pB[:, BANK:BANK + MODT])
        st.done(V.tensor_copy(par[:, :], pB[:, BANK + P:BANK + P + N_PAR]))
        st.done(V.memset(ssum[:, :], 0.0))

        def chunk_lo(i, m, dst, raw, hi_half):
            dve.wait_ge(ch_hi, i + (m + 1))
            V.tensor_tensor(out=dst[:, :], in0=raw[:, :], in1=hi_half[:, :].bitcast(F32), op=ALU.subtract
                            ).then_inc(ch_lo, 1)

        def chunk_sum(i, m, bank):
            dve.wait_ge(ch_tr, i + (m + 1))
            b = b_col[:, bass.ds(i * 2 + 2 * m, 2)].unsqueeze(2).broadcast_to([P, 2, NSTR])
            V.tensor_tensor(out=modc[:, bass.ds(i * 2 + 2 * m, 2), :],
                            in0=ch_cols[bank].rearrange("p (f c) -> p f c", c=NSTR), in1=b, op=ALU.add
                            ).then_inc(ch_sum, 1)

        for m in range(ADA_FIRST):
            chunk_lo(0, m, ada_lo[m % 2], ada_raw[m % ADA_RING], ada_hi[m % 2])
            add_square(m)
            if m > 1:
                chunk_sum(0, m - 2, m % 2)
        for m in (ADA_FIRST - 2, ADA_FIRST - 1):
            chunk_sum(0, m, m % 2)

        def norm_scale(row, scale):
            g = par[:, row:row + KD].unsqueeze(2).broadcast_to([P, KD, NSTR])
            v = modc[:, scale:scale + KD, :]
            return V.scalar_tensor_tensor(out=v, in0=v, scalar=1.0, in1=g, op0=ALU.add, op1=ALU.mult)

        def spread_gate(q, factor):
            v = modc[:, (3 * q + 2) * KD:(3 * q + 3) * KD, :]
            g = gate[:, q, :].rearrange("p (f g) -> p f g", f=KD)
            V.tensor_scalar(out=g[:, :, 0:GRP - DEC_BATCH],
                            in0=v[:, :, 0:1].broadcast_to([P, KD, GRP - DEC_BATCH]),
                            scalar1=factor, scalar2=None, op0=ALU.mult)
            st.done(V.tensor_scalar(out=g[:, :, GRP - DEC_BATCH:GRP], in0=v[:, :, 1:NSTR],
                                    scalar1=factor, scalar2=None, op0=ALU.mult))

        dve.wait_ge(ch_sum, ADA_FIRST)
        norm_scale(R_NORM, KD).then_inc(mod_ready, 1)

        def ffn(u0, q, t0, sq0):
            first_one = u0 == U_F0
            for part, kh in enumerate(PARTS):
                n = part_unit(u0, part)
                h0 = t0 + PART0[part]

                def pair(i, n=n, h0=h0, chunk=None):
                    if chunk is not None:
                        chunk_lo(i, chunk, slo, sraw, shi)
                    lo(n + 1, i)
                    lo(n + 2, i)
                    done(n + 1, i)
                    evacuated(dve, n, i)
                    wait(dve, hid_ready, i + h0)
                    V.tensor_tensor(out=split2(hidp[:, :]), in0=split2(silg[:, :]), in1=halves(acc[(n + 1) % 2]),
                                    op=ALU.mult).then_inc(acc_free[(n + 1) % 2], 1)
                    dve.wait_ge(hhi_ready, i + (h0 + 1))
                    V.tensor_tensor(out=tile(hid_lo, i), in0=hidp[:, :], in1=tile(hid_hi, i).bitcast(F32),
                                    op=ALU.subtract).then_inc(hid_ready, 1)
                    if chunk is not None:
                        chunk_sum(i, chunk, 0)
                have, chunk = chunks_of(u0, part)
                if have:
                    repeat_peeled(dve, min(have, kh - 1), lambda i: pair(i, chunk=chunk), n)
                if have < kh - 1:
                    repeat(dve, None, 0, have, kh - 1, pair)
                pair(kh - 1, chunk=chunk if have == kh else None)
                n += 2 * kh
                if first_one and part == 0:
                    dve.wait_ge(ch_sum, 3 * KD // 2)
                    spread_gate(0, 0.5)
                if first_one and part == 2:
                    dve.wait_ge(ch_sum, ADA_MAIN)
                    spread_gate(1, 1.0)
                    spread_gate(2, 0.5)
                    for row, scale in ((R_NORM + KD, 4 * KD), (R_NORM + 2 * KD, 7 * KD)):
                        ins = norm_scale(row, scale)
                    ins.then_inc(mod_ready, 1)
                if not first_one and part == 0:
                    dve.wait_ge(ch_sum, ADA_ALL)
                    norm_scale(R_FINAL, 10 * KD).then_inc(mod_ready, 1)
                last = part == 2

                def down(i, n=n, last=last, part=part):
                    chunk = CH_DOWN[part] if first_one and part < 2 else None
                    if chunk is not None:
                        chunk_lo(i, chunk, slo, sraw, shi)
                    for d in range(2):
                        lo(n + d + 1, i)
                        add_gated(n + d, i, i * 2 + d, q, last)
                        if last:
                            add_square(i * 2 + (sq0 + d))
                    if chunk is not None:
                        chunk_sum(i, chunk, 0)
                repeat(dve, st, 0 if last else 2, 0, KD // 2 - 1, down)
                down(KD // 2 - 1)

        lo(U_F0)
        r_of(0)
        dve.wait_ge(mod_ready, 1)
        norm(0, KD)
        ffn(U_F0, 0, 0, KD)
        r_of(1)
        norm(3 * KD, 4 * KD)

        lo(U_DT + 1)
        dve.wait_ge(st_done, 1)

        def xbc(n, i, j):
            b = j % 2
            lo(n + 1, i)
            V.tensor_copy(by_stream(xpad[b][:, PAD_P:PAD], PAD_S)[:, :, 0:3],
                          stT[:, bass.ds(i * 2 + j, 1), :].rearrange("p a (b k) -> p (a b) k", k=3))
            evacuated(dve, n, i)
            t = tails[:, bass.ds(i * 2 + j, 1), :].rearrange("p a r -> p (a r)")
            V.tensor_copy(t[:, 0:3], xpad[b][:, SEQ:PAD_P])
            st.done(V.tensor_copy(t[:, 3:TAIL].rearrange("p (b k) -> p b k", k=3),
                                  by_stream(xpad[b][:, PAD_P:PAD], PAD_S)[:, :, DEC_SEQ:PAD_S]))
            wait(dve, xcv_ready, i * 2 + j)
            w = [par[:, bass.ds(i * 2 + (R_CW + k * CT + j), 1)] for k in range(CONV_W)]
            st.done(V.tensor_scalar(out=cacc[:, 0:CONV_N], in0=xpad[b][:, 0:CONV_N], scalar1=w[0],
                                    scalar2=par[:, bass.ds(i * 2 + (R_CB + j), 1)], op0=ALU.mult, op1=ALU.add))
            for k in range(1, CONV_W):
                ins = V.scalar_tensor_tensor(out=cacc[:, 0:CONV_N], in0=xpad[b][:, k:k + CONV_N], scalar=w[k],
                                             in1=cacc[:, 0:CONV_N], op0=ALU.mult, op1=ALU.add)
                if k + 1 < CONV_W:
                    st.done(ins)
            ins.then_inc(conv_done, 1)

        def x_pair(i):
            xbc(U_X, i, 0)
            xbc(U_X + 1, i, 1)
        dve.wait_ge(pad0_ready, 2)
        st.done(V.memset(cacc[:, CONV_N:PAD], 0.0))
        x_pair(0)
        repeat(dve, st, 8, 1, XT_ // 2, x_pair)
        for j in range(XT_, CT):
            xbc(U_X + j, 0, j)
        dve.wait_ge(dt_tr, 1)
        per_head = [vecs[:, q, :].unsqueeze(1).broadcast_to([P, TT, HEADS]) for q in range(3)]
        by_tile = lambda t: t[:, :].rearrange("p (c h) -> p c h", h=HEADS)
        V.tensor_tensor(out=by_tile(dt_z), in0=pC[:, 0:TT * 32].rearrange("p (c h) -> p c h", h=32)[:, :, 16:32],
                        in1=per_head[0], op=ALU.add).then_inc(dt_z_ready, 1)
        st.done(V.tensor_scalar(out=vecs[:, 1, :], in0=vecs[:, 1, :], scalar1=-1.0, scalar2=None, op0=ALU.mult))
        dve.wait_ge(dt_e_ready, 1)
        st.done(V.scalar_tensor_tensor(out=dt_v[:, :], in0=dt_z[:, :], scalar=0.0, in1=dt_e[:, :],
                                       op0=ALU.max, op1=ALU.add))
        st.done(V.tensor_tensor(out=by_tile(dt_a), in0=by_tile(dt_v), in1=per_head[1], op=ALU.mult))

        heads = lambda ap: ap.rearrange("p (h x) -> p h x", x=HDIM)
        wide = lambda ap: ap.unsqueeze(2).broadcast_to([P, HG, HDIM])

        def parts(s):
            c, g = divmod(s, SSD_G)
            return c, g, c * HEADS + g * HG, ytm3[:, c, g * BANK:(g + 1) * BANK]

        def make_wd(s):
            c, g, h0, x = parts(s)
            wait(dve, seg_done, s)
            V.tensor_tensor(out=wd[:, :, :], in0=upto[:, int(c == ST), :].unsqueeze(1).broadcast_to([P, HG, P]),
                            in1=dt_a[:, h0:h0 + HG].unsqueeze(2).broadcast_to([P, HG, P]), op=ALU.mult
                            ).then_inc(wd_ready, 1)

        def make_xdt(s):
            c, g, h0, x = parts(s)
            wait(dve, y_mm, s)
            st.done(V.tensor_tensor(out=heads(xdt), in0=heads(x), in1=wide(dt_v[:, h0:h0 + HG]), op=ALU.mult))
            V.tensor_tensor(out=heads(xds), in0=heads(xdt), in1=wide(expo[:, 1, h0:h0 + HG]), op=ALU.mult)

        def make_g(s):
            c, g, h0, x = parts(s)
            dve.wait_ge(gexp_done, s + 1)
            V.tensor_tensor(out=gd[:, :, :], in0=gd[:, :, :], in1=cbm[:, s, :].unsqueeze(1).broadcast_to([P, HG, P]),
                            op=ALU.mult).then_inc(g_ready, 1)
            wait(dve, y_done, s)
            ins = V.tensor_tensor(out=heads(yt2), in0=heads(x), in1=wide(vecs[:, 2, g * HG:(g + 1) * HG]),
                                  op=ALU.mult)
            if c == 0:
                st.done(ins)

        def add_before(s):
            c, g, h0, x = parts(s)
            V.tensor_tensor(out=heads(yt1), in0=heads(pC[:, BANK:2 * BANK]), in1=wide(expo[:, 0, h0:h0 + HG]),
                            op=ALU.mult).then_inc(yo_used, 1)
            dve.wait_ge(yo_used, s + 1 - SSD_G)
            st.done(V.tensor_tensor(out=yt2, in0=yt2, in1=yt1, op=ALU.add))

        def add_within(s):
            c, g, h0, x = parts(s)
            dve.wait_ge(y_mm, s + 1)
            V.tensor_tensor(out=x, in0=yt2, in1=pC[:, 0:BANK], op=ALU.add).then_inc(y_done, 1)

        V.tensor_copy(wd[:, :, :].rearrange("p a (b x) -> p (a b) x", x=HDIM),
                      dt_a[:, ST * HEADS:TT * HEADS].unsqueeze(2).broadcast_to([P, HEADS, HDIM])
                      ).then_inc(wd_ready, 1)
        dve.wait_ge(cb_done, 1)
        n_p = ST * SSD_G
        for a, b, src in ((0, n_p, pB[:, :]), (n_p, TT * SSD_G, pC[:, BANK:BANK + SSD_G * P])):
            V.tensor_tensor(out=cbm[:, a:b, :], in0=src.rearrange("p (s n) -> p s n", n=P),
                            in1=upto[:, int(a > 0), :].unsqueeze(1).broadcast_to([P, b - a, P]), op=ALU.mult
                            ).then_inc(cbm_done, 1)
        dve.wait_ge(sums_mm, 1)
        make_wd(0)
        dve.wait_ge(expo_ready, 1)
        for s in range(ST * SSD_G):
            c, g, h0, x = parts(s)
            wait(dve, st_mm, s)
            make_xdt(s)
            make_wd(s + 1)
            make_g(s)
            if c:
                dve.wait_ge(yo_mm, s + 1 - SSD_G)
                add_before(s)
            lo(U_Z + s + 1)
            add_within(s)
            hs = hst[:, g * BANK:(g + 1) * BANK]
            if c:
                st.done(V.tensor_tensor(out=heads(hs), in0=heads(hs), in1=wide(expo[:, 2, h0:h0 + HG]), op=ALU.mult))
            elif s == 0:
                dve.wait_ge(tail_out, 32)
            dve.wait_ge(st_mm, s + 1)
            if c:
                V.tensor_tensor(out=hs, in0=hs, in1=pC[:, BANK:2 * BANK], op=ALU.add).then_inc(hst_ready, 1)
            else:
                V.tensor_copy(hs, pC[:, BANK:2 * BANK]).then_inc(hst_ready, 1)

        def make_bblk(g):
            V.tensor_tensor(out=bblk.rearrange("p (b n) -> p b n", n=NSTATE),
                            in0=btm[:, ST, g * P:(g + 1) * P].unsqueeze(1).broadcast_to([P, DEC_BATCH, NSTATE]),
                            in1=stream_of[:, :].unsqueeze(2).broadcast_to([P, DEC_BATCH, NSTATE]), op=ALU.mult
                            ).then_inc(bblk_ready, 1)

        def make_cblk(g):
            step = P + DEC_SEQ
            n = (DEC_BATCH - 1) * step
            C = bcf[:, SSD_G + g, SEQ:TOK]
            V.tensor_copy(hst[:, 0:n].rearrange("p (b t) -> p b t", t=step)[:, :, 0:DEC_SEQ],
                          by_stream(C)[:, 0:DEC_BATCH - 1, :])
            V.tensor_copy(hst[:, n:n + DEC_SEQ], C[:, P - DEC_SEQ:P]).then_inc(cblk_ready, 1)

        s = ST * SSD_G
        dve.wait_ge(st_mm, s)
        make_xdt(s)
        make_bblk(0)
        dve.wait_ge(hout_tr, 1)
        st.done(V.memset(hst[:, :], 0.0))
        make_cblk(0)
        make_g(s)
        make_wd(s + 1)
        for j in range(HP):
            g, jj = divmod(j, HP // SSD_G)
            h = h0s[j % H0_RING][:, :, :]
            dve.wait_ge(h0_tr, j + 1)
            st.done(V.tensor_tensor(out=h, in0=h, in1=decs[:, j, :].unsqueeze(2).broadcast_to([P, DEC_BATCH, NSTATE]),
                                    op=ALU.mult))
            dve.wait_ge(h1_mm, j + 1)
            last_of_first = j + 1 == HP // SSD_G
            if last_of_first:
                make_xdt(s + 1)
                make_bblk(1)
            V.tensor_tensor(out=h, in0=h, in1=acc_h1[:, :].rearrange("p (b n) -> p b n", n=NSTATE), op=ALU.add
                            ).then_inc(h1_ready, 1)
            if jj + 1 == HP // SSD_G:
                dve.wait_ge(ys_mm, j + 1)
                if last_of_first:
                    make_cblk(1)
                add_before(s + g)
                add_within(s + g)
                if last_of_first:
                    make_g(s + 1)
        dve.wait_ge(y_done, TT * SSD_G)
        dve.wait_ge(h1_ready, HP)
        V.memset(dt_e[:, 0:1], 0.0).then_inc(ssd_over, 1)
        V.memset(wsb[:, :, :], 0.0).then_inc(ws_zero, 1)

        lo(U_V + 1)
        dve.wait_ge(hout_out, 32)
        st.done(V.memset(ssum[:, :], 0.0))
        for j in range(KD):
            dve.wait_ge(yt_tr, j + 1)
            V.tensor_tensor(out=ytm3[:, :, j * P:(j + 1) * P],
                            in0=(pB, pC)[j % 2][:, 0:TOK].rearrange("p (c n) -> p c n", c=TT),
                            in1=zs3[:, j, :, :], op=ALU.mult).then_inc(yz_ready, 1)
            add_square(2 * KD + j)
        lo(U_V + 2)

        for i in range(H0_RING):
            dve.wait_ge(h1_out[i], 16 * (HP // H0_RING))
        dve.wait_ge(ws_tr, 1)
        for kind, src in enumerate((pB, pC)):
            V.tensor_tensor(out=wmT[:, kind, :].rearrange("p (h t) -> p h t", t=P),
                            in0=src[:, :].rearrange("p (h t) -> p h t", t=P),
                            in1=upto[:, kind, :].unsqueeze(1).broadcast_to([P, 8, P]), op=ALU.mult
                            ).then_inc(wm_ready, 1)
        dve.wait_ge(gm_vec_in, 32)

        def v_norm(h):
            pv = pB[:, 0:TOK].rearrange("p (c n) -> p c n", c=TT)
            vc = tmp[1][:, :].rearrange("p (c n) -> p c n", c=TT)
            vn = xadd[:, :].rearrange("p (c n) -> p c n", c=TT)
            dve.wait_ge(vt_tr, h + 1)
            st.done(V.tensor_reduce(out=stat[:, 0, :], in_=pv, axis=AX.X, op=ALU.add))
            st.done(V.tensor_scalar(out=stat[:, 1, :], in0=stat[:, 0, :], scalar1=-1.0 / P, scalar2=None, op0=ALU.mult))
            V.tensor_tensor(out=vc, in0=pv, in1=stat[:, 1, :].unsqueeze(2).broadcast_to([P, TT, P]), op=ALU.add
                            ).then_inc(vc_ready, 1)
            dve.wait_ge(vsq_ready, h + 1)
            V.tensor_reduce(out=stat[:, 2, :], in_=sq[:, :].rearrange("p (c n) -> p c n", c=TT), axis=AX.X, op=ALU.add
                            ).then_inc(vvar_ready, 1)
            dve.wait_ge(vstd_ready, h + 1)
            st.done(V.reciprocal(out=stat[:, 0, :], in_=stat[:, 3, :]))
            wait(dve, v_out, h * 16)
            wait(dve, mix_mm, h)
            st.done(V.tensor_tensor(out=vn, in0=vc, in1=stat[:, 0, :].unsqueeze(2).broadcast_to([P, TT, P]), op=ALU.mult))
            V.tensor_tensor(out=vn, in0=vn, in1=gm_g[:, bass.ds(h * P, P)].unsqueeze(1).broadcast_to([P, TT, P]),
                            op=ALU.mult).then_inc(vn_ready, 1)

        def gm_out(h):
            bias = gm_bias[:, bass.ds(h * P, P)]
            dve.wait_ge(mix_mm, h + 1)
            V.tensor_tensor(out=gmp[:, 0:SEQ].rearrange("p (c t) -> p c t", c=ST),
                            in0=pC[:, 0:SEQ].rearrange("p (c t) -> p c t", c=ST),
                            in1=bias.unsqueeze(1).broadcast_to([P, ST, P]), op=ALU.add)
            V.tensor_tensor(out=by_stream(gmp[:, SEQ:TOK]), in0=by_stream(pC[:, SEQ:TOK]),
                            in1=bias[:, 0:DEC_SEQ].unsqueeze(1).broadcast_to([P, DEC_BATCH, DEC_SEQ]), op=ALU.add
                            ).then_inc(mix_used, 1)
            dve.wait_ge(mix_used, h + 1)
            evacuated(dve, U_V + 1, h)
            V.tensor_tensor(out=gmp[:, :], in0=gmp[:, :], in1=gu[:, :], op=ALU.mult).then_inc(gmp_ready, 1)
            dve.wait_ge(gmhi_ready, h + 1)
            V.tensor_tensor(out=tile(gm_lo, h), in0=gmp[:, :], in1=tile(gm_hi, h).bitcast(F32), op=ALU.subtract
                            ).then_inc(gm_ready, 1)

        def vu(i):
            lo(U_V + 1, i)
            v_norm(i - 1)
            lo(U_V + 2, i)
            gm_out(i - 1)
        vu(1)
        repeat(dve, st, 4, 2, KD, vu)

        lo(U_OG + 1)
        v_norm(KD - 1)
        gm_out(KD - 1)
        lo(U_OG + 2)
        dve.wait_ge(v_out, 16 * KD)
        add_gated(U_OG, 0, 0, 1, False)
        lo(U_OG + 3)
        add_gated(U_OG + 1, 0, 1, 1, False)
        r_of(2)
        for f in range(KD):
            wait(dve, yfm_split, f - 1)
            v3 = tmp[f % 2][:, :].rearrange("p (c n) -> p c n", c=TT)
            V.scalar_tensor_tensor(out=v3, in0=ytm3[:, :, f * P:(f + 1) * P], scalar=par[:, R_SSDN + f:R_SSDN + f + 1],
                                   in1=rT[:, :].rearrange("p (c n) -> p c n", c=TT), op0=ALU.mult, op1=ALU.mult
                                   ).then_inc(yp_ready, 1)
            dve.wait_ge(yhi_ready, f + 1)
            V.tensor_tensor(out=tile(hn_lo, f), in0=tmp[f % 2][:, :], in1=tile(hn_hi, f).bitcast(F32), op=ALU.subtract
                            ).then_inc(yfm_split, 1)
            if f + 2 < KD:
                lo(U_OG + f + 4)
                add_gated(U_OG + f + 2, 0, f + 2, 1, False)
        for f in range(KD):
            if f:
                lo(U_OY + f + 1)
            add_gated(U_OY + f, 0, f, 1, True)
            add_square(3 * KD + f)
        r_of(3)
        norm(6 * KD, 7 * KD)
        ffn(U_F1, 2, FF_TILES, 4 * KD)
        r_of(4)
        dve.wait_ge(mod_ready, 3)

        def result(f):
            dve.wait_ge(of_tr, f + 1)
            V.tensor_copy(y_row[:, :, f * P:(f + 1) * P], acc[f % 2][:, 0:TOK].rearrange("p (c n) -> p c n", c=TT)
                          ).then_inc(of_done, 1)
        norm(9 * KD, 10 * KD, to_hn=False)
        result(KD - 1)

    top.close()


_INPUTS = ("x_prompt", "x_sample", "state_ssm", "state_conv", "c_prompt", "c_sample", "w_ada", "b_ada", "norm_g",
           "ffn_w1", "ffn_w2", "w_in", "gm_norm_g", "gm_ws", "gm_b", "conv_w", "conv_b", "dt_bias", "a_log",
           "d_skip", "ssd_norm_g", "w_out", "final_norm_g", "w_ada_final", "b_ada_final")
_OUTPUTS = (("y_prompt", (1, SEQ, D_MODEL)), ("y_sample", (DEC_BATCH, DEC_SEQ, D_MODEL)),
            ("ssm_prompt", (1, 1, HEADS, HDIM, NSTATE)), ("conv_prompt", (1, 1, CONV_W - 1, CONV_DIM)),
            ("ssm_sample", (1, DEC_BATCH, HEADS, HDIM, NSTATE)),
            ("conv_sample", (1, DEC_BATCH, CONV_W - 1, CONV_DIM)),
            ("gm_v_sample", (1, DEC_BATCH, DEC_SEQ, D_MODEL)))


def kernel(**inputs):
    import numpy as np
    import concourse.bacc as bacc
    from concourse.bass_utils import run_bass_kernel_spmd

    nc = bacc.Bacc("TRN2", target_bir_lowering=False, num_devices=1)
    arrays, args = {}, []
    for name in _INPUTS:
        a = np.ascontiguousarray(inputs[name])
        arrays[f"in_{name}"] = a
        args.append(nc.dram_tensor(f"in_{name}", a.shape, mybir.dt.from_np(a.dtype), kind="ExternalInput").ap())
    for name, shape in _OUTPUTS:
        args.append(nc.dram_tensor(f"out_{name}", shape, F32, kind="ExternalOutput").ap())
    trunk_program(nc, *args)
    r = run_bass_kernel_spmd(nc, [arrays], core_ids=[0])
    return tuple(r.results[0][f"out_{name}"] for name, _ in _OUTPUTS)
```

```python
from contextlib import ExitStack

import concourse.bass as bass
from concourse import mybir

F32 = mybir.dt.float32
F32R = mybir.dt.float32r
ACT = mybir.ActivationFunctionType
ALU = mybir.AluOpType
AX = mybir.AxisListType

P = 128
D_MODEL = 1024
SEQ = 512
DEC_BATCH = 8
DEC_SEQ = 16
TOK = SEQ + DEC_BATCH * DEC_SEQ
HALF = TOK // 2
BANK = 512
TT = TOK // P
ST = TT - 1
KD = D_MODEL // P
NSTR = 1 + DEC_BATCH
GRP = TOK // DEC_SEQ
D_FF = 2816
FF_TILES = D_FF // P
PARTS = (KD, KD, FF_TILES - 2 * KD)
PART0 = (0, KD, 2 * KD)
HEADS = 16
HDIM = 64
NSTATE = 128
SSD_G = 2
HG = HEADS // SSD_G
CONV_W = 4
CONV_DIM = D_MODEL + 2 * SSD_G * NSTATE
CT = CONV_DIM // P
DT_AT = CT - 2
XT_ = D_MODEL // P
D_IN = 4 * D_MODEL + 2 * SSD_G * NSTATE + HEADS
COL_U, COL_V, COL_Z, COL_X = 0, D_MODEL, 2 * D_MODEL, 3 * D_MODEL
COL_DT = D_IN - P
N_MOD = 9
MODT = (N_MOD + 2) * KD
EPS = 1e-6
HP = HEADS * HDIM // P
PAD_P = SEQ + CONV_W - 1
PAD_S = DEC_SEQ + CONV_W - 1
PAD = PAD_P + DEC_BATCH * PAD_S
CONV_N = PAD - (CONV_W - 1)
TAIL = NSTR * (CONV_W - 1)

R_NORM, R_FINAL, R_SSDN, R_CW, R_CB = 0, 24, 32, 40, 40 + CONV_W * CT
N_PAR = R_CB + CT

MIX_AT = 4
H0_RING = 4

ADA_COLS = 2 * P
ADA_FIRST = 2 * D_MODEL // ADA_COLS
ADA_RING = 4
ADA_MAIN = N_MOD * D_MODEL // ADA_COLS
ADA_ALL = (N_MOD + 2) * D_MODEL // ADA_COLS
CH_PAIR = (ADA_FIRST, ADA_FIRST + PARTS[0] + KD // 2, ADA_FIRST + PARTS[0] + PARTS[1] + KD)
CH_DOWN = (CH_PAIR[0] + PARTS[0], CH_PAIR[1] + PARTS[1])
CH_LAST = ADA_MAIN - CH_PAIR[2]


def trunk_program(nc, x_prompt, x_sample, state_ssm, state_conv, c_prompt, c_sample, w_ada, b_ada, norm_g,
                  ffn_w1, ffn_w2, w_in, gm_norm_g, gm_ws, gm_b, conv_w, conv_b, dt_bias, a_log, d_skip,
                  ssd_norm_g, w_out, final_norm_g, w_ada_final, b_ada_final,
                  y_prompt, y_sample, ssm_prompt, conv_prompt, ssm_sample, conv_sample, gm_v_sample):
    top = ExitStack()

    def sb(name, shape, dt=F32, stack=None):
        return (stack or top).enter_context(nc.sbuf_tensor(name, shape, dt))

    def ps(name, cols):
        return top.enter_context(nc.psum_tensor(name, [P, cols], F32))

    def sem(name):
        return top.enter_context(nc.semaphore(name))

    xT = sb("xT", [P, KD * TOK])
    hn_hi = sb("hn_hi", [P, KD * TOK], F32R)
    hn_lo = sb("hn_lo", [P, KD * TOK], F32R)
    wraw = [sb(f"wraw{i}", [P, KD * P]) for i in range(2)]
    whi = [sb(f"whi{i}", [P, KD * P], F32R) for i in range(2)]
    wlo = [sb(f"wlo{i}", [P, KD * P], F32R) for i in range(2)]
    modc = sb("modc", [P, MODT, NSTR])
    gate = sb("gate", [P, 3, KD * GRP])
    par = sb("par", [P, N_PAR])
    ident = sb("ident", [P, P])
    ones_mean = sb("ones_mean", [P, P])
    ones = sb("ones", [P, P])
    upto = sb("upto", [P, 2, P])
    after = sb("after", [P, 2, P])
    stream_of = sb("stream_of", [P, DEC_BATCH])
    rT = sb("rT", [P, TOK])
    ssum = sb("ssum", [P, TOK])
    sq = sb("sq", [P, TOK])
    tmp = [sb(f"tmp{i}", [P, TOK]) for i in range(2)]
    tms = [sb(f"tms{i}", [P, P]) for i in range(2)]
    xadd = sb("xadd", [P, TOK])
    eps_t = sb("eps_t", [P, 1])
    rcol = sb("rcol", [P, TT])
    c_hl = sb("c_hl", [P, KD, 2 * NSTR], F32R)
    b_col = sb("b_col", [P, MODT])
    c_f32 = sb("c_f32", [P, KD, 2 * NSTR])
    pairsum = sb("pairsum", [2 * NSTR, NSTR])
    vecs = sb("vecs", [P, 3, HEADS])

    reg = ExitStack()
    ada_raw = [sb(f"ada_raw{i}", [P, KD * ADA_COLS], stack=reg) for i in range(ADA_RING)]
    ada_hi = [sb(f"ada_hi{i}", [P, KD * ADA_COLS], F32R, reg) for i in range(2)]
    ada_lo = [sb(f"ada_lo{i}", [P, KD * ADA_COLS], F32R, reg) for i in range(2)]
    ada_row = [sb(f"ada_row{i}", [2 * NSTR, ADA_COLS], stack=reg) for i in range(2)]
    c_row = sb("c_row", [NSTR, D_MODEL], stack=reg)
    c_sil = sb("c_sil", [NSTR, D_MODEL], stack=reg)
    b_row = sb("b_row", [MODT, P], stack=reg)
    p_row = sb("p_row", [N_PAR, P], stack=reg)
    x_row = [sb(f"x_row{i}", [P, D_MODEL], stack=reg) for i in range(TT)]
    reg.close()
    reg = ExitStack()
    hid_hi = sb("hid_hi", [P, KD * TOK], F32R, reg)
    hid_lo = sb("hid_lo", [P, KD * TOK], F32R, reg)
    silg = sb("silg", [P, TOK], stack=reg)
    hidp = sb("hidp", [P, TOK], stack=reg)
    sraw = sb("sraw", [P, KD * ADA_COLS], stack=reg)
    shi = sb("shi", [P, KD * ADA_COLS], F32R, reg)
    slo = sb("slo", [P, KD * ADA_COLS], F32R, reg)
    srow = sb("srow", [2 * NSTR, ADA_COLS], stack=reg)
    reg.close()
    reg = ExitStack()
    ytm = sb("ytm", [P, TT * D_MODEL], stack=reg)
    sub = ExitStack()
    bcf = sb("bcf", [P, 4, TOK], stack=sub)
    btm = sb("btm", [P, TT, SSD_G * NSTATE], stack=sub)
    dt_z = sb("dt_z", [P, TT * HEADS], stack=sub)
    dt_e = sb("dt_e", [P, TT * HEADS], stack=sub)
    dt_v = sb("dt_v", [P, TT * HEADS], stack=sub)
    dt_a = sb("dt_a", [P, TT * HEADS], stack=sub)
    expo = sb("expo", [P, 3, TT * HEADS], stack=sub)
    decs = sb("decs", [P, HP, DEC_BATCH], stack=sub)
    conv_mem = ExitStack()
    tails = sb("tails", [P, CT, TAIL], stack=conv_mem)
    stT = sb("stT", [P, CT, TAIL - 3], stack=conv_mem)
    st_row = sb("st_row", [TAIL - 3, CONV_DIM], stack=conv_mem)
    tail_row = sb("tail_row", [TAIL, CONV_DIM], stack=conv_mem)
    xpad = [sb(f"xpad{i}", [P, PAD], stack=conv_mem) for i in range(2)]
    cacc = sb("cacc", [P, PAD], stack=conv_mem)
    conv_mem.close()
    h0s = [sb(f"h0s{i}", [P, DEC_BATCH, NSTATE], stack=sub) for i in range(H0_RING)]
    h0T = sb("h0T", [P, DEC_BATCH, P], stack=sub)
    hst = sb("hst", [P, HEADS * HDIM], stack=sub)
    wd = sb("wd", [P, HG, P], stack=sub)
    gd = sb("gd", [P, HG, P], stack=sub)
    cbm = sb("cbm", [P, TT * SSD_G, P], stack=sub)
    zs = sb("zs", [P, KD * TOK], stack=sub)
    sub.close()
    sub = ExitStack()
    wst = sb("wst", [P, 8, P], stack=sub)
    wsb = sb("wsb", [P, 8, P], stack=sub)
    gm_g = sb("gm_g", [P, D_MODEL], stack=sub)
    gm_bias = sb("gm_bias", [P, 8 * P], stack=sub)
    wmT = sb("wmT", [P, 2, 8 * P], stack=sub)
    stat = sb("stat", [P, 4, TT], stack=sub)
    gu = sb("gu", [P, TOK], stack=sub)
    gmp = sb("gmp", [P, TOK], stack=sub)
    gm_hi = sb("gm_hi", [P, KD * TOK], F32R, sub)
    gm_lo = sb("gm_lo", [P, KD * TOK], F32R, sub)
    sub.close()
    reg.close()
    reg = ExitStack()
    y_row = sb("y_row", [P, TT, D_MODEL], stack=reg)
    y_fm = [sb(f"y_fm{i}", [P, TOK], stack=reg) for i in range(2)]
    reg.close()

    acc = [ps("acc0", 2 * BANK), ps("acc1", 2 * BANK)]
    pB = ps("pB", 2 * BANK)
    pC = ps("pC", 2 * BANK)

    setup_in = sem("setup_in")
    vecs_in = sem("vecs_in")
    x_in = [sem(f"x_in{i}") for i in range(TT)]
    masks_done = sem("masks_done")
    pool_step, act_step, dve_step = sem("pool_step"), sem("act_step"), sem("dve_step")
    c_silu = sem("c_silu")
    c_tr, c_used, c_split = sem("c_tr"), sem("c_used"), sem("c_split")
    par_tr = sem("par_tr")
    xt_tr, xt_done = sem("xt_tr"), sem("xt_done")
    ada_in = [sem(f"ada_in{i}") for i in range(ADA_RING)]
    s_in = sem("s_in")
    ada_hi_done, ada_lo_done = sem("ada_hi_done"), sem("ada_lo_done")
    ch_hi, ch_lo = sem("ch_hi"), sem("ch_lo")
    ch_mm, ch_row, ch_tr, ch_sum = (
        sem("ch_mm"), sem("ch_row"), sem("ch_tr"), sem("ch_sum"))
    mod_ready = sem("mod_ready")
    w_in_sb = [sem(f"w_in_sb{i}") for i in range(2)]
    whi_done, wlo_done = sem("whi_done"), sem("wlo_done")
    unit_done = sem("unit_done")
    acc_free = [sem(f"acc_free{i}") for i in range(2)]
    x_ready = sem("x_ready")
    hhi_ready, hid_ready = sem("hhi_ready"), sem("hid_ready")
    sq_ready, sq_added = sem("sq_ready"), sem("sq_added")
    rms_mm, rms_sqrt, diag_ready, r_mm, rinv_ready = (
        sem("rms_mm"), sem("rms_sqrt"), sem("diag_ready"), sem("r_mm"), sem("rinv_ready"))
    prod_ready, tms_ready = sem("prod_ready"), sem("tms_ready")
    nhi_ready, hn_ready = sem("nhi_ready"), sem("hn_ready")
    st_in, st_tr, st_done = sem("st_in"), sem("st_tr"), sem("st_done")
    dt_tr, dt_z_ready, dt_e_ready = sem("dt_tr"), sem("dt_z_ready"), sem("dt_e_ready")
    pad0_ready = sem("pad0_ready")
    conv_done, xcv_ready = sem("conv_done"), sem("xcv_ready")
    conv_tr, conv_tr_used = sem("conv_tr"), sem("conv_tr_used")
    tail_tr, tail_done, tail_out = sem("tail_tr"), sem("tail_done"), sem("tail_out")
    sums_mm, expo_ready = sem("sums_mm"), sem("expo_ready")
    wd_ready, seg_done, gexp_done = sem("wd_ready"), sem("seg_done"), sem("gexp_done")
    cb_done, cbm_done = sem("cb_done"), sem("cbm_done")
    g_ready, y_mm, y_done = sem("g_ready"), sem("y_mm"), sem("y_done")
    yo_mm, yo_used = sem("yo_mm"), sem("yo_used")
    st_mm, hst_ready = sem("st_mm"), sem("hst_ready")
    hout_tr, hout_ready, hout_out = sem("hout_tr"), sem("hout_ready"), sem("hout_out")
    h0_in = [sem(f"h0_in{i}") for i in range(H0_RING)]
    h0_tr, h0T_ready, ys_mm = sem("h0_tr"), sem("h0T_ready"), sem("ys_mm")
    h1_mm, h1_ready = sem("h1_mm"), sem("h1_ready")
    h1_out = [sem(f"h1_out{i}") for i in range(H0_RING)]
    bblk_ready, cblk_ready = sem("bblk_ready"), sem("cblk_ready")
    ssd_over = sem("ssd_over")
    yt_tr, yz_ready = sem("yt_tr"), sem("yz_ready")
    ws_zero, ws_in, ws_blk_in, gm_vec_in = sem("ws_zero"), sem("ws_in"), sem("ws_blk_in"), sem("gm_vec_in")
    ws_tr, wm_ready = sem("ws_tr"), sem("wm_ready")
    vt_tr, vc_ready, vsq_ready, vvar_ready, vstd_ready, vn_ready, v_out = (
        sem("vt_tr"), sem("vc_ready"), sem("vsq_ready"), sem("vvar_ready"), sem("vstd_ready"),
        sem("vn_ready"), sem("v_out"))
    mix_mm, mix_used = sem("mix_mm"), sem("mix_used")
    gmp_ready, gmhi_ready, gm_ready = sem("gmp_ready"), sem("gmhi_ready"), sem("gm_ready")
    yp_ready, yhi_ready, yfm_split = sem("yp_ready"), sem("yhi_ready"), sem("yfm_split")
    of_ready, of_tr, of_done, y_out = sem("of_ready"), sem("of_tr"), sem("of_done"), sem("y_out")

    def halves(t):
        return t[:, :].rearrange("p (h x) -> p h x", h=2)[:, :, 0:HALF]

    def split2(ap):
        return ap.rearrange("p (h x) -> p h x", h=2)

    def tile(t, f):
        return t[:, bass.ds(f * TOK, TOK)]

    def kxn(w, k, n):
        return w[:, 0:k * n].rearrange("p (k n) -> p k n", n=n)

    def mod40(q, f):
        g = gate[:, q, bass.ds(f * GRP, GRP)]
        return g.rearrange("p (h g) -> p h g", h=2).unsqueeze(3).broadcast_to([P, 2, GRP // 2, DEC_SEQ])

    def by_group(ap3):
        return ap3.rearrange("p h (g t) -> p h g t", t=DEC_SEQ)

    def by_stream(ap, n=DEC_SEQ):
        return ap.rearrange("p (b t) -> p b t", t=n)

    ch_rows = [pC[0:2 * NSTR, i * BANK:i * BANK + ADA_COLS] for i in range(2)]
    ch_cols = [pB[:, i * BANK:i * BANK + 2 * NSTR] for i in range(2)]

    xdt, xds = sq[:, 0:HG * HDIM], xadd[:, 0:HG * HDIM]
    yt1, yt2 = tmp[0][:, 0:HG * HDIM], tmp[1][:, 0:HG * HDIM]
    hout = [rT[:, 0:BANK], ssum[:, 0:BANK]]
    bblk = btm[:, 0:ST, :].rearrange("p c n -> p (c n)")
    zs3 = zs[:, :].rearrange("p (f c n) -> p f c n", c=TT, n=P)
    ytm3 = ytm[:, :].rearrange("p (c n) -> p c n", c=TT)
    w1 = ffn_w1[0].rearrange("a (k p) n -> a p k n", p=P)
    w2 = ffn_w2[0].rearrange("a (k p) n -> a p k n", p=P)
    win = w_in[0].rearrange("(k p) n -> p k n", p=P)
    wout = w_out[0].rearrange("(k p) n -> p k n", p=P)
    wada = w_ada[0].rearrange("(k p) n -> p k n", p=P)
    wadaf = w_ada_final.rearrange("(k p) n -> p k n", p=P)
    ws_t = gm_ws[0].rearrange("h t s -> t h s")
    h0_d = state_ssm[0].rearrange("b (j h) p n -> j (h p) b n", h=2)
    h1_d = ssm_sample[0].rearrange("b (j h) p n -> j (h p) b n", h=2)
    hp_d = ssm_prompt[0, 0].rearrange("(j h) p n -> (h p) j n", h=2)

    ffn_units = sum(2 * kh + KD for kh in PARTS)
    U_F0 = 0
    U_DT = ffn_units
    U_X = U_DT + 1
    U_Z = U_X + CT
    U_V = U_Z + KD
    U_OG = U_V + 2 * KD
    U_OY = U_OG + KD
    U_F1 = U_OY + KD
    U_END = U_F1 + ffn_units

    acc_h0, acc_h1 = acc[U_V % 2], acc[(U_V + 1) % 2]

    def unit_tiles(n, i=0):
        n += 2 * i if isinstance(i, int) else 0
        for base in (U_F0, U_F1):
            for kh in PARTS:
                base += 2 * kh
                if base <= n < base + KD:
                    return kh
                base += KD
        return KD

    def part_unit(u0, part):
        return u0 + sum(2 * kh + KD for kh in PARTS[:part])

    def chunks_of(u0, part):
        if u0 == U_F0:
            return (CH_LAST if part == 2 else PARTS[part]), CH_PAIR[part]
        return (PARTS[0], ADA_MAIN) if part == 0 else (0, None)

    class Steps:

        def __init__(self, eng, s):
            self.eng, self.s, self.n, self.i, self.start, self.per = eng, s, 0, None, 0, 0

        def done(self, ins):
            ins.then_inc(self.s, 1)
            self.n += 1
            v = self.n if self.i is None else self.i * self.per + (self.n - self.start * self.per)
            self.eng.wait_ge(self.s, v)

    def repeat(eng, steps, per, start, stop, body):
        if stop - start == 1:
            body(start)
            return
        with eng.Fori(start, stop) as i:
            n0 = steps.n if steps else 0
            if steps:
                steps.i, steps.start, steps.per = i, start, per
            body(i)
            if steps:
                assert steps.n - n0 == per, (steps.n - n0, per)
                steps.n = n0 + per * (stop - start)
                steps.i = None

    def after_first(i):
        return not isinstance(i, int) or i > 0

    def repeat_peeled(eng, stop, body, n):
        peel = n in (U_F0, U_F1)
        if peel:
            body(0)
        repeat(eng, None, 0, int(peel), stop, body)

    def evacuated(eng, n, i=0):
        eng.wait_ge(acc_free[n % 2], i + (n // 2 + 1))

    def all_evacuated(eng, p, n):
        eng.wait_ge(acc_free[p], (n + 1 - p) // 2)

    def wait(eng, s, v):
        if not isinstance(v, int) or v > 0:
            eng.wait_ge(s, v)

    block = top.enter_context(nc.Block())

    @block.sync
    def _(sp):
        def first_col(col):
            return col if isinstance(col, int) else sp.snap(col)

        def load_unit(n, i, rows, col):
            col = first_col(col)
            wait(sp, wlo_done, n - 1 + i * 2)
            k = unit_tiles(n, i)
            sp.dma_start(kxn(wraw[n % 2], k, P), rows[:, :, bass.ds(col, P)]).then_inc(w_in_sb[n % 2], 16)

        def load_chunk(i, m, src, m0):
            col = first_col(i * ADA_COLS + (m - m0) * ADA_COLS)
            wait(sp, ch_lo, i + (m - ADA_FIRST))
            sp.dma_start(kxn(sraw, KD, ADA_COLS), src[:, :, bass.ds(col, ADA_COLS)]).then_inc(s_in, 16)

        def load_ffn(u0, a):
            for part, kh in enumerate(PARTS):
                n, h0 = part_unit(u0, part), PART0[part]

                def pair(i, n=n, h0=h0, part=part, chunk=None, src=wada, m0=0):
                    if not isinstance(i, int) or n + i > U_F0:
                        load_unit(n, i, w1[a], i * P + h0 * P)
                        load_unit(n + 1, i, w1[a], i * P + (D_FF + h0 * P))
                    if chunk is not None:
                        load_chunk(i, chunk, src, m0)
                have = 0
                if u0 == U_F0:
                    have = CH_LAST if part == 2 else kh
                    if part == 0:
                        pair(0, chunk=CH_PAIR[0])
                    repeat(sp, None, 0, int(part == 0), have, lambda i: pair(i, chunk=CH_PAIR[part]))
                elif part == 0:
                    have = kh
                    repeat(sp, None, 0, 0, kh, lambda i: pair(i, chunk=ADA_MAIN, src=wadaf, m0=ADA_MAIN))
                if have < kh:
                    repeat(sp, None, 0, have, kh, pair)
                n += 2 * kh

                def down(i, n=n, h0=h0, kh=kh, part=part):
                    for d in range(2):
                        load_unit(n + d, i, w2[a, :, h0:h0 + kh, :], i * (2 * P) + d * P)
                    if u0 == U_F0 and part < 2:
                        load_chunk(i, CH_DOWN[part], wada, 0)
                repeat(sp, None, 0, 0, KD // 2, down)

        def load_two(n, src, col):
            def two(i):
                for d in range(2):
                    load_unit(n + d, i, src, i * (2 * P) + (col + d * P))
            return two

        def load_first(m):
            sp.dma_start(kxn(ada_raw[m % ADA_RING], KD, ADA_COLS),
                         wada[:, :, m * ADA_COLS:(m + 1) * ADA_COLS]).then_inc(ada_in[m % ADA_RING], 16)
        sp.dma_start(c_row[0:1, :], c_prompt).then_inc(setup_in, 16)
        sp.dma_start(c_row[1:NSTR, :], c_sample).then_inc(setup_in, 16)
        sp.dma_start(b_row[0:N_MOD * KD, :], b_ada[0].rearrange("(r c) -> r c", c=P)).then_inc(setup_in, 16)
        sp.dma_start(b_row[N_MOD * KD:MODT, :], b_ada_final.rearrange("(r c) -> r c", c=P)).then_inc(setup_in, 16)
        for r, src in ((R_NORM, norm_g[0].rearrange("a (r c) -> (a r) c", c=P)),
                       (R_FINAL, final_norm_g.rearrange("(r c) -> r c", c=P)),
                       (R_SSDN, ssd_norm_g[0].rearrange("(r c) -> r c", c=P)),
                       (R_CW, conv_w[0].rearrange("a (r c) -> (a r) c", c=P)),
                       (R_CB, conv_b[0].rearrange("(r c) -> r c", c=P))):
            sp.dma_start(p_row[r:r + src.shape[0], :], src).then_inc(setup_in, 16)
        for q, src in enumerate((dt_bias, a_log, d_skip)):
            sp.dma_start(vecs[:, q, :], src[0].partition_broadcast(P)).then_inc(vecs_in, 16)
        for c in range(TT):
            src = x_prompt[0, c * P:(c + 1) * P, :] if c < ST else x_sample.rearrange("b t d -> (b t) d")
            sp.dma_start(x_row[c][:, :], src).then_inc(x_in[c], 16)
        for m in range(ADA_RING):
            load_first(m)
        for m in range(ADA_RING, ADA_FIRST):
            if m % 2:
                sp.wait_ge(ada_lo_done, (m - ADA_RING) // 2 + 1)
            else:
                sp.wait_ge(ch_mm, m + 1 - ADA_RING)
            load_first(m)
        load_unit(U_F0, 0, w1[0], 0)
        load_unit(U_F0 + 1, 0, w1[0], D_FF)
        sp.wait_ge(ch_tr, ADA_FIRST)
        sp.wait_ge(xt_tr, TT)
        load_ffn(U_F0, 0)
        load_unit(U_DT, 0, win, COL_DT)
        load_unit(U_X, 0, win, COL_X)
        sp.wait_ge(unit_done, U_DT)
        sp.dma_start(st_row[:, :], state_conv[0].rearrange("b k c -> (b k) c")).then_inc(st_in, 16)
        load_unit(U_X + 1, 0, win, COL_X + P)
        repeat(sp, None, 0, 1, CT // 2, load_two(U_X, win, COL_X))
        load_two(U_Z, win, COL_Z)(0)
        sp.wait_ge(tail_out, 32)
        for j in range(H0_RING):
            sp.dma_start(h0s[j][:, :, :], h0_d[j]).then_inc(h0_in[j], 16)
        repeat(sp, None, 0, 1, KD // 2, load_two(U_Z, win, COL_Z))
        for d, col in ((0, COL_V), (1, COL_U)):
            load_unit(U_V + d, 0, win, col)
        for j in range(H0_RING, HP):
            sp.wait_ge(h1_out[j % H0_RING], 16 * (j // H0_RING))
            sp.dma_start(h0s[j % H0_RING][:, :, :], h0_d[j]).then_inc(h0_in[j % H0_RING], 16)

        sp.wait_ge(ssd_over, 1)
        sp.dma_start(wst[:, :, :], ws_t).then_inc(ws_in, 16)
        sp.wait_ge(ws_zero, 1)
        for b in range(DEC_BATCH):
            r = slice(b * DEC_SEQ, (b + 1) * DEC_SEQ)
            sp.dma_start(wsb[r, :, r], ws_t[0:DEC_SEQ, :, 0:DEC_SEQ]).then_inc(ws_blk_in, 16)
        sp.dma_start(gm_g[:, :], gm_norm_g[0].partition_broadcast(P)).then_inc(gm_vec_in, 16)
        sp.dma_start(gm_bias[:, :], gm_b[0].rearrange("h t -> (h t)").partition_broadcast(P)).then_inc(gm_vec_in, 16)

        def vu(i):
            load_unit(U_V + 2, i, win, i * P + (COL_V + P))
            load_unit(U_V + 3, i, win, i * P + (COL_U + P))
        repeat(sp, None, 0, 0, KD - 1, vu)
        repeat(sp, None, 0, 0, KD // 2, load_two(U_OG, wout[:, 0:KD, :], 0))
        repeat(sp, None, 0, 0, KD // 2, load_two(U_OY, wout[:, KD:2 * KD, :], 0))
        load_ffn(U_F1, 1)
        for f in range(KD):
            sp.wait_ge(of_done, f + 1)
            cols = slice(f * P, (f + 1) * P)
            sp.dma_start(y_prompt[0].rearrange("(c p) d -> p c d", p=P)[:, :, cols],
                         y_row[:, 0:ST, cols]).then_inc(y_out, 16)
            sp.dma_start(y_sample.rearrange("b t d -> (b t) d")[:, cols], y_row[:, ST, cols]).then_inc(y_out, 16)
        sp.wait_ge(y_out, 2 * 16 * KD)

    @block.gpsimd
    def _(pool):
        st = Steps(pool, pool_step)

        def select(t, pattern, mult, base):
            st.done(nc.gpsimd.affine_select(out=t, in_=t, pattern=pattern, compare_op=ALU.is_ge, fill=0.0,
                                            base=base, channel_multiplier=mult))
        st.done(nc.gpsimd.memset(ident[:, :], 0.0))
        st.done(nc.gpsimd.affine_select(out=ident[:, :], in_=ident[:, :], pattern=[[-1, P]],
                                        compare_op=ALU.not_equal, fill=1.0, base=0, channel_multiplier=1))
        nc.gpsimd.memset(ones[:, :], 1.0)
        nc.gpsimd.memset(c_f32[:, :, :], 0.0)
        nc.gpsimd.memset(ones_mean[:, :], 1.0 / D_MODEL)
        nc.gpsimd.memset(eps_t[:, :], EPS)
        nc.gpsimd.memset(upto[:, :, :], 1.0)
        nc.gpsimd.memset(after[:, :, :], 1.0)
        st.done(nc.gpsimd.memset(stream_of[:, :], 1.0))
        select(upto[:, :, :], [[0, 2], [1, P]], -1, 0)
        select(after[:, :, :], [[0, 2], [-1, P]], 1, -1)
        for t in (upto, after):
            v = t[:, 1, :].rearrange("p (b t) -> p b t", t=DEC_SEQ)
            select(v, [[-DEC_SEQ, DEC_BATCH], [0, DEC_SEQ]], 1, 0)
            select(v, [[DEC_SEQ, DEC_BATCH], [0, DEC_SEQ]], -1, DEC_SEQ - 1)
        select(stream_of[:, :], [[-DEC_SEQ, DEC_BATCH]], 1, 0)
        select(stream_of[:, :], [[DEC_SEQ, DEC_BATCH]], -1, DEC_SEQ - 1)
        nc.gpsimd.tensor_tensor(out=pairsum[:, :], in0=ident[0:2 * NSTR, 0:NSTR],
                                in1=ident[0:2 * NSTR, NSTR:2 * NSTR], op=ALU.add).then_inc(masks_done, 1)

        def norm_samples(m, used0, shift, scale):
            pool.wait_ge(rinv_ready, m + 1)
            pool.wait_ge(mod_ready, (1, 2, 2, 2, 3)[m])
            for f in range(KD):
                t = tms[f % 2]
                if f >= 2:
                    used0(f - 2)
                tv = by_stream(t[:, :])
                st.done(nc.gpsimd.tensor_tensor(out=t[:, :], in0=xT[:, f * TOK + SEQ:(f + 1) * TOK],
                                                in1=rT[:, SEQ:TOK], op=ALU.mult))
                for op, q in ((ALU.mult, scale), (ALU.add, shift)):
                    v = modc[:, q + f, 1:NSTR].unsqueeze(2).broadcast_to([P, DEC_BATCH, DEC_SEQ])
                    ins = nc.gpsimd.tensor_tensor(out=tv, in0=tv, in1=v, op=op)
                    if op == ALU.mult:
                        st.done(ins)
                ins.then_inc(tms_ready, 1)

        norm_samples(0, lambda f: pool.wait_ge(hn_ready, f + 1), 0, KD)
        pool.wait_ge(unit_done, U_DT)
        for i in range(2):
            nc.gpsimd.memset(xpad[i][:, 0:CONV_W - 1], 0.0).then_inc(pad0_ready, 1)
        norm_samples(1, lambda f: pool.wait_ge(hn_ready, KD + f + 1), 3 * KD, 4 * KD)

        pool.wait_ge(tail_done, 1)
        pool.dma_start(conv_prompt[0, 0], tail_row[0:CONV_W - 1, :]).then_inc(tail_out, 16)
        pool.dma_start(conv_sample[0].rearrange("b k c -> (b k) c"), tail_row[CONV_W - 1:TAIL, :]).then_inc(tail_out, 16)
        for q in range(2):
            pool.wait_ge(hout_ready, q + 1)
            pool.dma_start(hp_d[:, q * HP // 2:(q + 1) * HP // 2, :], hout[q].rearrange("p (j n) -> p j n", n=NSTATE)
                           ).then_inc(hout_out, 16)
        for j in range(HP):
            pool.wait_ge(h1_ready, j + 1)
            pool.dma_start(h1_d[j], h0s[j % H0_RING][:, :, :]).then_inc(h1_out[j % H0_RING], 16)
        def v_store(i):
            pool.wait_ge(vn_ready, i + 1)
            pool.dma_start(gm_v_sample[0].rearrange("b t d -> (b t) d")[:, bass.ds(i * P, P)],
                           xadd[:, ST * P:TT * P]).then_inc(v_out, 16)
        repeat(pool, None, 0, 0, KD, v_store)
        pool.wait_ge(v_out, 16 * KD)
        norm_samples(3, lambda f: pool.wait_ge(hn_ready, 2 * KD + f + 1), 6 * KD, 7 * KD)
        norm_samples(4, lambda f: pool.wait_ge(of_ready, f + 1), 9 * KD, 10 * KD)

    @block.tensor
    def _(pe):
        mm = nc.tensor.matmul

        def unit(n, i, hi, lo, k_ready, ks=None):
            p, kt = n % 2, unit_tiles(n, i)
            wh, wl = kxn(whi[p], kt, P), kxn(wlo[p], kt, P)
            ks = range(kt) if ks is None else ks
            if ks[0] == 0:
                pe.wait_ge(wlo_done, i * 2 + (n + 1))
                wait(pe, acc_free[p], i + n // 2)
            for k in ks:
                k_ready(k)
                for t, (w, a) in enumerate(((wh, hi), (wh, lo), (wl, hi))):
                    for h in range(2):
                        last = mm(acc[p][:, h * BANK:h * BANK + HALF], w[:, k, :],
                                  a[:, k * TOK + h * HALF:k * TOK + (h + 1) * HALF],
                                  start=(k == 0 and t == 0), stop=(k == kt - 1 and t == 2))
            if ks[-1] == kt - 1:
                last.then_inc(unit_done, 1)

        def two_units(n, k_ready):
            for k in range(KD):
                for d in range(2):
                    unit(n + d, 0, hn_hi, hn_lo, k_ready, ks=(k,))

        def hn_wait(m):
            return lambda k: pe.wait_ge(hn_ready, m * KD + k + 1)

        def mean_square(m):
            pe.wait_ge(sq_added, (m + 1) * KD)
            out = acc[0] if m == 0 else pC
            for c in range(TT):
                last = mm(out[:, c:c + 1], ssum[:, c * P:(c + 1) * P], ones_mean[:, 0:1], start=True, stop=True)
            last.then_inc(rms_mm, 1)

        def spread_r(m):
            pe.wait_ge(diag_ready, m + 1)
            for h in range(2):
                last = mm(pC[:, h * BANK:h * BANK + HALF], ones[:, :], sq[:, h * HALF:(h + 1) * HALF],
                          start=True, stop=True)
            last.then_inc(r_mm, 1)

        def to_tokens(out, src, used, v):
            wait(pe, used, v)
            for c in range(TT):
                last = nc.tensor.transpose(out[:, c * P:(c + 1) * P], src[:, c * P:(c + 1) * P], ident[:, :])
            return last

        pe.wait_ge(masks_done, 1)
        pe.wait_ge(c_silu, 1)
        for k in range(KD):
            last = mm(pB[:, k * NSTR:(k + 1) * NSTR], c_sil[0:NSTR, k * P:(k + 1) * P], ident[0:NSTR, 0:NSTR],
                      start=True, stop=True)
        last.then_inc(c_tr, 1)
        mm(pB[:, BANK:BANK + MODT], b_row[0:MODT, :], ident[0:MODT, 0:MODT], start=True, stop=True)
        mm(pB[:, BANK + P:BANK + P + N_PAR], p_row[0:N_PAR, :], ident[0:N_PAR, 0:N_PAR],
           start=True, stop=True).then_inc(par_tr, 1)
        for c in range(TT):
            pe.wait_ge(x_in[c], 16)
            wait(pe, xt_done, c - 1)
            for f in range(KD):
                last = nc.tensor.transpose(acc[c % 2][:, f * P:(f + 1) * P], x_row[c][:, f * P:(f + 1) * P],
                                           ident[:, :])
            last.then_inc(xt_tr, 1)

        pe.wait_ge(c_split, 1)

        def chunk_rows(i, m, bank, wh, wl):
            pe.wait_ge(ch_lo, i + (m + 1 - ADA_FIRST))
            for k in range(KD):
                for t, w in enumerate((wh, wl)):
                    last = mm(ch_rows[bank], c_hl[:, k, :], kxn(w, KD, ADA_COLS)[:, k, :],
                              start=(k == 0 and t == 0), stop=(k == KD - 1 and t == 1))
            last.then_inc(ch_mm, 1)

        def chunk_cols(i, m, bank, row):
            pe.wait_ge(ch_row, i + (m + 1))
            for f in range(2):
                last = mm(ch_cols[bank][:, f * NSTR:(f + 1) * NSTR], row[:, f * P:(f + 1) * P], pairsum[:, :],
                          start=True, stop=True)
            last.then_inc(ch_tr, 1)

        def first_rows(m):
            if m % 2 == 0:
                pe.wait_ge(ada_in[m % ADA_RING], 16 * (m // ADA_RING + 1))
                parts = [(c_f32, ada_raw[m % ADA_RING])]
            else:
                pe.wait_ge(ada_lo_done, m // 2 + 1)
                parts = [(c_hl, ada_hi[m // 2 % 2]), (c_hl, ada_lo[m // 2 % 2])]
            for k in range(KD):
                for t, (c, w) in enumerate(parts):
                    last = mm(ch_rows[m % 2], c[:, k, :], kxn(w, KD, ADA_COLS)[:, k, :],
                              start=(k == 0 and t == 0), stop=(k == KD - 1 and t == len(parts) - 1))
            last.then_inc(ch_mm, 1)

        for m in range(ADA_FIRST + 1):
            if m == ADA_FIRST:
                mean_square(0)
            if m < ADA_FIRST:
                wait(pe, ch_row, m - 1)
                first_rows(m)
            if m:
                wait(pe, ch_sum, m - 2)
                chunk_cols(0, m - 1, (m - 1) % 2, ada_row[(m - 1) % 2])

        def ffn(u0, m, t0):
            first_one = u0 == U_F0
            for part, kh in enumerate(PARTS):
                n = part_unit(u0, part)

                def pair(i, n=n, chunk=None):
                    first_pair = not after_first(i) and n == u0
                    if first_pair:
                        two_units(n, hn_wait(m))
                    else:
                        unit(n, i, hn_hi, hn_lo, lambda k: None)
                    if chunk is not None:
                        chunk_rows(i, chunk, 0, shi, slo)
                    if not first_pair:
                        unit(n + 1, i, hn_hi, hn_lo, lambda k: None)
                    if chunk is not None:
                        pe.wait_ge(ch_sum, i + chunk)
                        chunk_cols(i, chunk, 0, srow)
                have, chunk = chunks_of(u0, part)
                if have:
                    repeat_peeled(pe, have, lambda i: pair(i, chunk=chunk), n)
                if have < kh:
                    repeat(pe, None, 0, have, kh, pair)

                def hid_wait(k, have=t0 + PART0[part], kh=kh):
                    if k in (0, kh - 1):
                        pe.wait_ge(hid_ready, have + (kh if k else kh - 1))

                def down(i, n=n + 2 * kh, part=part):
                    chunk = CH_DOWN[part] if first_one and part < 2 else None
                    unit(n, i, hid_hi, hid_lo, hid_wait)
                    if chunk is not None:
                        chunk_rows(i, chunk, 0, shi, slo)
                    unit(n + 1, i, hid_hi, hid_lo, hid_wait)
                    if chunk is not None:
                        pe.wait_ge(ch_sum, i + chunk)
                        chunk_cols(i, chunk, 0, srow)
                repeat(pe, None, 0, 0, KD // 2, down)

        spread_r(0)
        ffn(U_F0, 0, 0)
        mean_square(1)
        spread_r(1)

        two_units(U_DT, hn_wait(1))
        pe.wait_ge(st_in, 16)
        for j in range(CT):
            last = mm(pB[:, j * 24:(j + 1) * 24], st_row[0:24, j * P:(j + 1) * P], ident[0:24, 0:24],
                      start=True, stop=True)
        last.then_inc(st_tr, 1)
        pe.wait_ge(st_done, 1)

        def conv_tr_tile(p, i, j, src=None):
            pe.wait_ge(xcv_ready, i * 2 + (j + 1))
            to_tokens(pB, tmp[p] if src is None else src, conv_tr_used, i * 2 + j).then_inc(conv_tr, 1)

        def x_pair(i):
            if after_first(i):
                unit(U_X, i, hn_hi, hn_lo, lambda k: None)
                conv_tr_tile(1, i, -1)
            unit(U_X + 1, i, hn_hi, hn_lo, lambda k: None)
            conv_tr_tile(0, i, 0)
        x_pair(0)
        evacuated(pe, U_DT)
        for c in range(TT):
            last = mm(pC[:, c * 32:(c + 1) * 32], sq[96:P, c * P:(c + 1) * P], ident[96:P, 96:P],
                      start=True, stop=True)
        last.then_inc(dt_tr, 1)
        repeat(pe, None, 0, 1, XT_ // 2, x_pair)
        for j in range(XT_, CT):
            unit(U_X + j, 0, hn_hi, hn_lo, lambda k: None)
            if j - 1 < XT_:
                conv_tr_tile((j - 1) % 2, 0, j - 1)
            elif j - 1 < XT_ + SSD_G:
                conv_tr_tile(0, 0, j - 1, bcf[:, j - 1 - XT_, :])
        unit(U_Z, 0, hn_hi, hn_lo, lambda k: None)
        pe.wait_ge(conv_done, CT)
        all_evacuated(pe, (U_Z + 1) % 2, U_Z)
        pe.wait_ge(dt_z_ready, 1)
        for j in range(CT):
            dst = (acc[(U_Z + 1) % 2][0:TAIL, j * P:(j + 1) * P] if j < 8 else pC[0:TAIL, (j - 8) * P:(j - 7) * P])
            last = mm(dst, tails[:, j, :], ident[:, :], start=True, stop=True)
        last.then_inc(tail_tr, 1)
        pe.wait_ge(xcv_ready, CT)
        pe.wait_ge(conv_tr_used, XT_ + SSD_G)
        for s in range(TT * SSD_G):
            c, g = divmod(s, SSD_G)
            tok = slice(c * P, (c + 1) * P)
            dst = pB[:, s * P:(s + 1) * P] if c < ST else pC[:, BANK + g * P:BANK + (g + 1) * P]
            last = mm(dst, bcf[:, g, tok], bcf[:, SSD_G + g, tok], start=True, stop=True)
        last.then_inc(cb_done, 1)

        pe.wait_ge(wd_ready, 1)
        pe.wait_ge(tail_done, 1)
        nh = TT * HEADS
        np_ = ST * HEADS
        for q, mask in enumerate((upto, after)):
            mm(pC[:, q * nh:q * nh + np_], mask[:, 0, :], dt_a[:, 0:np_], start=True, stop=True)
            mm(pC[:, q * nh + np_:(q + 1) * nh], mask[:, 1, :], dt_a[:, np_:nh], start=True, stop=True)
        mm(pC[:, 2 * nh:3 * nh], ones[:, :], dt_a[:, :], start=True, stop=True)
        for j in range(HP):
            last = mm(pC[:, 3 * nh + j * DEC_BATCH:3 * nh + (j + 1) * DEC_BATCH],
                      gd[:, :, :].rearrange("p a b -> p (a b)")[:, j * P:(j + 1) * P], stream_of[:, :],
                      start=True, stop=True)
        last.then_inc(sums_mm, 1)

        def seg(s):
            pe.wait_ge(wd_ready, s + 2)
            wait(pe, gexp_done, s)
            for q in range(2):
                last = mm(pB[:, q * BANK:(q + 1) * BANK], after[:, int(s >= ST * SSD_G), :],
                          wd[:, 4 * q:4 * q + 4, :].rearrange("p a b -> p (a b)"), start=True, stop=True)
            last.then_inc(seg_done, 1)

        def within(s):
            pe.wait_ge(g_ready, s + 1)
            wait(pe, y_done, s)
            for h in range(HG):
                last = mm(pC[:, h * HDIM:(h + 1) * HDIM], gd[:, h, :], xdt[:, h * HDIM:(h + 1) * HDIM],
                          start=True, stop=True)
            last.then_inc(y_mm, 1)

        pe.wait_ge(cbm_done, 2)
        for s in range(ST * SSD_G):
            c, g = divmod(s, SSD_G)
            seg(s)
            if c:
                pe.wait_ge(hst_ready, s)
                mm(pC[:, BANK:2 * BANK], bcf[:, SSD_G + g, c * P:(c + 1) * P], hst[:, g * BANK:(g + 1) * BANK],
                   start=True, stop=True).then_inc(yo_mm, 1)

            def inner(k, s=s, c=c, g=g):
                if k == KD // 2:
                    within(s)
                    if c:
                        pe.wait_ge(yo_used, s + 1 - SSD_G)
                    else:
                        wait(pe, hst_ready, s)
                    mm(pC[:, BANK:2 * BANK], btm[:, c, g * P:(g + 1) * P], xds, start=True, stop=True
                       ).then_inc(st_mm, 1)
            if s + 1 < KD:
                unit(U_Z + s + 1, 0, hn_hi, hn_lo, inner)
            else:
                inner(KD // 2)

        pe.wait_ge(hst_ready, ST * SSD_G)
        pe.wait_ge(gexp_done, ST * SSD_G)
        for j in range(HP):
            last = nc.tensor.transpose(pB[:, j * P:(j + 1) * P], hst[:, j * P:(j + 1) * P], ident[:, :])
        last.then_inc(hout_tr, 1)

        def state_tr(j):
            pe.wait_ge(h0_in[j % H0_RING], 16 * (j // H0_RING + 1))
            wait(pe, h0T_ready, j)
            for b in range(DEC_BATCH):
                last = nc.tensor.transpose(acc_h0[:, b * P:(b + 1) * P], h0s[j % H0_RING][:, b, :], ident[:, :])
            last.then_inc(h0_tr, 1)

        all_evacuated(pe, U_V % 2, U_V)
        state_tr(0)
        pe.wait_ge(hout_ready, 2)
        seg(ST * SSD_G)
        all_evacuated(pe, (U_V + 1) % 2, U_V)
        for j in range(HP):
            g, jj = divmod(j, HP // SSD_G)
            pe.wait_ge(bblk_ready, g + 1)
            wait(pe, h1_ready, j)
            for q in range(2):
                last = mm(acc_h1[:, q * BANK:(q + 1) * BANK], xds[:, jj * P:(jj + 1) * P],
                          bblk[:, q * BANK:(q + 1) * BANK], start=True, stop=True)
            last.then_inc(h1_mm, 1)
            if j + 1 < HP:
                state_tr(j + 1)
            pe.wait_ge(h0T_ready, j + 1)
            pe.wait_ge(cblk_ready, g + 1)
            if jj == 0 and g:
                pe.wait_ge(y_done, ST * SSD_G + g)
            for b in range(DEC_BATCH):
                last = mm(pC[:, BANK + jj * P:BANK + (jj + 1) * P], hst[:, b * P:(b + 1) * P], h0T[:, b, :],
                          start=(b == 0), stop=(b == DEC_BATCH - 1))
            last.then_inc(ys_mm, 1)
            if jj == 0:
                within(ST * SSD_G + g)
                if g == 0:
                    seg(ST * SSD_G + 1)

        def y_tile(k):
            if k == 0:
                pe.wait_ge(y_done, TT * SSD_G)
                pe.wait_ge(gexp_done, TT * SSD_G)
            dst = (pB, pC)[k % 2]
            wait(pe, yz_ready, k - 1)
            for c in range(TT):
                last = nc.tensor.transpose(dst[:, c * P:(c + 1) * P], ytm3[:, c, k * P:(k + 1) * P], ident[:, :])
            last.then_inc(yt_tr, 1)

        def ws_tile(h):
            if h == 0:
                pe.wait_ge(yz_ready, KD)
                pe.wait_ge(ws_in, 16)
                pe.wait_ge(ws_blk_in, 16 * DEC_BATCH)
            for dst, src in ((pB, wst), (pC, wsb)):
                last = nc.tensor.transpose(dst[:, h * P:(h + 1) * P], src[:, h, :], ident[:, :])
            if h == 7:
                last.then_inc(ws_tr, 1)

        def mix(h):
            pe.wait_ge(vn_ready, h + 1)
            wait(pe, mix_used, h)
            for c in range(TT):
                last = mm(pC[:, c * P:(c + 1) * P], xadd[:, c * P:(c + 1) * P],
                          wmT[:, int(c == ST), bass.ds(h * P, P)], start=True, stop=True)
            last.then_inc(mix_mm, 1)

        def vu(i):
            unit(U_V, i, hn_hi, hn_lo, lambda k: None)
            unit(U_V + 1, i, hn_hi, hn_lo, lambda k: mix(i - 1) if k == MIX_AT else None)
            evacuated(pe, U_V, i)
            to_tokens(pB, tmp[0], vc_ready, i).then_inc(vt_tr, 1)
        pe.wait_ge(h0T_ready, HP)
        unit(U_V, 0, hn_hi, hn_lo, lambda k: y_tile(k - 1) if k else None)
        y_tile(KD - 1)
        pe.wait_ge(h1_ready, HP)
        unit(U_V + 1, 0, hn_hi, hn_lo, lambda k: ws_tile(k - 1) if k else None)
        ws_tile(KD - 1)
        evacuated(pe, U_V)
        pe.wait_ge(wm_ready, 1)
        to_tokens(pB, tmp[0], vc_ready, 0).then_inc(vt_tr, 1)
        vu(1)
        repeat(pe, None, 0, 2, KD, vu)

        for d in range(2):
            unit(U_OG + d, 0, gm_hi, gm_lo, lambda k: pe.wait_ge(gm_ready, KD - 1), ks=range(KD - 1))
            if d == 0:
                mix(KD - 1)
        pe.wait_ge(gm_ready, KD)
        for d in range(2):
            unit(U_OG + d, 0, gm_hi, gm_lo, lambda k: None, ks=(KD - 1,))
        mean_square(2)

        def og(i):
            for d in range(2):
                unit(U_OG + d, i, gm_hi, gm_lo, lambda k: None)
        unit(U_OG + 2, 0, gm_hi, gm_lo, lambda k: spread_r(2) if k == 6 else None)
        unit(U_OG + 3, 0, gm_hi, gm_lo, lambda k: None)
        repeat(pe, None, 0, 2, KD // 2, og)

        def oy(i):
            for d in range(2):
                unit(U_OY + d, i, hn_hi, hn_lo, lambda k: pe.wait_ge(yfm_split, k + 1))
        repeat(pe, None, 0, 0, KD // 2, oy)

        mean_square(3)
        spread_r(3)
        ffn(U_F1, 2, FF_TILES)
        mean_square(4)
        spread_r(4)
        for f in range(KD):
            if f < 2:
                all_evacuated(pe, f, U_END)
            pe.wait_ge(of_ready, f + 1)
            to_tokens(acc[f % 2], y_fm[f % 2], of_done, f - 1).then_inc(of_tr, 1)

    @block.scalar
    def _(act):
        st = Steps(act, act_step)
        A = nc.scalar.activation

        def hi(n, i=0):
            if isinstance(i, int) and n + 2 * i >= U_END:
                return
            p, w = n % 2, unit_tiles(n, i) * P
            act.wait_ge(w_in_sb[p], i * 16 + 16 * (n // 2 + 1))
            wait(act, unit_done, i * 2 + (n - 1))
            A(whi[p][:, 0:w], wraw[p][:, 0:w], ACT.Copy).then_inc(whi_done, 1)

        def done(n, i=0):
            act.wait_ge(unit_done, i * 2 + (n + 1))

        def rms_root(m):
            act.wait_ge(rms_mm, m + 1)
            A(rcol[:, :], (acc[0] if m == 0 else pC)[:, 0:TT], ACT.Sqrt, bias=eps_t[:, 0:1]).then_inc(rms_sqrt, 1)

        def copy_r(m):
            act.wait_ge(r_mm, m + 1)
            A(split2(rT[:, :]), halves(pC), ACT.Copy).then_inc(rinv_ready, 1)

        def norm(m, hn0, shift, dst=None):
            for f in range(KD):
                b = modc[:, shift + f, 0:1]
                if dst is None:
                    act.wait_ge(prod_ready, prod0[0] + f + 1)
                    A(hn_hi[:, f * TOK:f * TOK + SEQ], tmp[f % 2][:, 0:SEQ], ACT.Identity, bias=b)
                    act.wait_ge(tms_ready, tms0[0] + f + 1)
                    A(hn_hi[:, f * TOK + SEQ:(f + 1) * TOK], tms[f % 2][:, :], ACT.Copy).then_inc(nhi_ready, 1)
                else:
                    act.wait_ge(prod_ready, prod0[0] + f + 1)
                    wait(act, of_tr, f - 1)
                    A(dst[f % 2][:, 0:SEQ], tmp[f % 2][:, 0:SEQ], ACT.Identity, bias=b)
                    act.wait_ge(tms_ready, tms0[0] + f + 1)
                    A(dst[f % 2][:, SEQ:TOK], tms[f % 2][:, :], ACT.Copy).then_inc(of_ready, 1)
            prod0[0] += KD
            tms0[0] += KD
        prod0, tms0 = [0], [0]

        act.wait_ge(setup_in, 16 * 9)
        A(c_sil[:, :], c_row[:, :], ACT.Silu).then_inc(c_silu, 1)
        act.wait_ge(vecs_in, 48)
        st.done(A(vecs[:, 1, :], vecs[:, 1, :], ACT.Exp))
        act.wait_ge(c_tr, 1)
        c_cols = pB[:, 0:KD * NSTR].rearrange("p (k c) -> p k c", c=NSTR)
        A(c_f32[:, :, 0:NSTR], c_cols, ACT.Copy)
        A(c_hl[:, :, 0:NSTR], c_cols, ACT.Copy).then_inc(c_used, 1)
        def copy_x(c):
            act.wait_ge(xt_tr, c + 1)
            A(xT[:, :].rearrange("p (f t) -> p f t", t=TOK)[:, :, c * P:(c + 1) * P],
              acc[c % 2][:, :].rearrange("p (f t) -> p f t", t=P), ACT.Copy).then_inc(xt_done, 1)

        def chunk_hi(i, m, dst, src):
            A(dst[:, :], src[:, :], ACT.Copy).then_inc(ch_hi, 1)

        def chunk_row(i, m, bank, row):
            act.wait_ge(ch_mm, i + (m + 1))
            A(row[:, :], ch_rows[bank], ACT.Copy).then_inc(ch_row, 1)

        for c in range(TT):
            copy_x(c)
        act.wait_ge(xt_done, TT)
        def first_hi(m):
            act.wait_ge(ada_in[m % ADA_RING], 16 * (m // ADA_RING + 1))
            wait(act, ch_mm, m - 3)
            A(ada_hi[m // 2 % 2][:, :], ada_raw[m % ADA_RING][:, :], ACT.Copy).then_inc(ada_hi_done, 1)

        def first_square(f):
            wait(act, sq_added, f - 1)
            A(tmp[f % 2][:, :], tile(xT, f), ACT.Square).then_inc(sq_ready, 1)

        def first_row(m):
            wait(act, ch_tr, m - 1)
            chunk_row(0, m, m % 2, ada_row[m % 2])

        for m in range(1, ADA_FIRST, 2):
            first_hi(m)
            if m > 1:
                first_row(m - 2)
            for f in (m - 1, m):
                first_square(f)
            first_row(m - 1)
        hi(U_F0)
        rms_root(0)
        hi(U_F0 + 1)
        first_row(ADA_FIRST - 1)
        copy_r(0)

        def stream_hi(i, m):
            act.wait_ge(s_in, i * 16 + 16 * (m - ADA_FIRST + 1))
            if not (isinstance(i, int) and m == ADA_FIRST):
                act.wait_ge(ch_mm, i + m)
            chunk_hi(i, m, shi, sraw)

        def stream_row(i, m):
            if not (isinstance(i, int) and m == ADA_FIRST):
                act.wait_ge(ch_tr, i + m)
            chunk_row(i, m, 0, srow)

        def ffn(u0, t0, squares):
            first_one = u0 == U_F0
            for part, kh in enumerate(PARTS):
                n = part_unit(u0, part)
                h0 = t0 + PART0[part]

                def pair(i, n=n, h0=h0, chunk=None):
                    if chunk is not None:
                        stream_hi(i, chunk)
                    if after_first(i) or n != u0:
                        hi(n + 1, i)
                    done(n, i)
                    wait(act, hid_ready, i + h0)
                    A(split2(silg[:, :]), halves(acc[n % 2]), ACT.Silu).then_inc(acc_free[n % 2], 1)
                    hi(n + 2, i)
                    if chunk is not None:
                        stream_row(i, chunk)
                    evacuated(act, n + 1, i)
                    A(tile(hid_hi, i), hidp[:, :], ACT.Copy).then_inc(hhi_ready, 1)
                have, chunk = chunks_of(u0, part)
                if have:
                    repeat_peeled(act, min(have, kh - 1), lambda i: pair(i, chunk=chunk), n)
                if have < kh - 1:
                    repeat(act, None, 0, have, kh - 1, pair)
                pair(kh - 1, chunk=chunk if have == kh else None)
                n += 2 * kh

                def down(i, n=n, last=(part == 2), part=part):
                    chunk = CH_DOWN[part] if first_one and part < 2 else None
                    if chunk is not None:
                        stream_hi(i, chunk)
                    for d in range(2):
                        hi(n + d + 1, i)
                        if d == 0 and chunk is not None:
                            stream_row(i, chunk)
                        if last and d and isinstance(i, int):
                            hi(n + 3, i)
                        if last:
                            act.wait_ge(x_ready, i * 2 + (x0[0] + d + 1))
                            act.wait_ge(sq_added, i * 2 + (squares + d))
                            A(sq[:, :], tile(xT, i * 2 + d), ACT.Square).then_inc(sq_ready, 1)
                repeat(act, None, 0, 0, KD // 2 - 1, down)
                down(KD // 2 - 1)
            x0[0] += KD
        x0 = [0]

        act.wait_ge(mod_ready, 1)
        norm(0, 0, 0)
        ffn(U_F0, 0, KD)
        rms_root(1)
        copy_r(1)
        act.wait_ge(mod_ready, 2)
        norm(1, 0, 3 * KD)

        done(U_DT)
        A(sq[96:P, :].rearrange("p (h x) -> p h x", h=2), halves(acc[U_DT % 2])[96:P], ACT.Copy
          ).then_inc(acc_free[U_DT % 2], 1)
        act.wait_ge(st_tr, 1)
        A(stT[:, :, :], pB[:, 0:CT * 24].rearrange("p (j r) -> p j r", r=24), ACT.Copy).then_inc(st_done, 1)

        def softplus():
            act.wait_ge(dt_z_ready, 1)
            st.done(A(dt_e[:, :], dt_z[:, :], ACT.Abs))
            st.done(A(dt_e[:, :], dt_e[:, :], ACT.Exp, scale=-1.0))
            A(dt_e[:, :], dt_e[:, :], ACT.Ln, bias=1.0).then_inc(dt_e_ready, 1)

        def xbc(n, i, j):
            p = n % 2
            b = j % 2
            done(n, i)
            wait(act, conv_done, i * 2 + (j - 1))
            A(xpad[b][:, 3:3 + HALF], acc[p][:, 0:HALF], ACT.Copy)
            A(xpad[b][:, 3 + HALF:PAD_P], acc[p][:, BANK:BANK + SEQ - HALF], ACT.Copy)
            A(by_stream(xpad[b][:, PAD_P:PAD], PAD_S)[:, :, 3:PAD_S],
              by_stream(acc[p][:, BANK + SEQ - HALF:BANK + HALF]), ACT.Copy).then_inc(acc_free[p], 1)
            hi(n + 2, i)
            if isinstance(i, int) and j == DT_AT:
                softplus()
            act.wait_ge(conv_done, i * 2 + (j + 1))
            if j < XT_:
                dst = tmp[b]
                wait(act, conv_tr, i * 2 + (j - 1))
            else:
                dst = bcf[:, j - XT_, :]
            A(dst[:, 0:SEQ], cacc[:, 0:SEQ], ACT.Silu)
            A(by_stream(dst[:, SEQ:TOK]), by_stream(cacc[:, PAD_P:PAD], PAD_S)[:, :, 0:DEC_SEQ],
              ACT.Silu).then_inc(xcv_ready, 1)

        def conv_out(i, j):
            act.wait_ge(conv_tr, i * 2 + (j + 1))
            if j < XT_:
                dst = ytm3[:, :, bass.ds(i * 2 * P + j * P, P)]
            else:
                dst = btm[:, :, (j - XT_) * P:(j - XT_ + 1) * P]
            A(dst, pB[:, 0:TOK].rearrange("p (c n) -> p c n", c=TT), ACT.Copy).then_inc(conv_tr_used, 1)

        def x_pair(i):
            xbc(U_X, i, 0)
            if after_first(i):
                conv_out(i, -1)
            xbc(U_X + 1, i, 1)
            conv_out(i, 0)
        hi(U_X + 1)
        x_pair(0)
        repeat(act, None, 0, 1, XT_ // 2, x_pair)
        for j in range(XT_, CT):
            xbc(U_X + j, 0, j)
            if j - 1 < XT_ + SSD_G:
                conv_out(0, j - 1)
        act.wait_ge(tail_tr, 1)
        A(tail_row[:, 0:2 * BANK], acc[(U_Z + 1) % 2][0:TAIL, :], ACT.Copy)
        A(tail_row[:, 2 * BANK:CONV_DIM], pC[0:TAIL, 0:CONV_DIM - 2 * BANK], ACT.Copy).then_inc(tail_done, 1)

        nh = TT * HEADS
        act.wait_ge(sums_mm, 1)
        A(expo[:, :, :].rearrange("p a b -> p (a b)"), pC[:, 0:3 * nh], ACT.Exp)
        A(decs[:, :, :].rearrange("p a b -> p (a b)"), pC[:, 3 * nh:3 * nh + HP * DEC_BATCH], ACT.Exp
          ).then_inc(expo_ready, 1)

        def decay(s):
            act.wait_ge(seg_done, s + 1)
            wait(act, y_mm, s)
            A(gd[:, :, :].rearrange("p a b -> p (a b)"), pB[:, :], ACT.Exp).then_inc(gexp_done, 1)

        def silu_z(j):
            n = U_Z + j
            done(n)
            A(split2(tile(zs, j)), halves(acc[n % 2]), ACT.Silu).then_inc(acc_free[n % 2], 1)
        for s in range(ST * SSD_G):
            decay(s)
            silu_z(s)
            if s + 2 < KD:
                hi(U_Z + s + 2)
        hi(U_V)
        act.wait_ge(hout_tr, 1)
        for q in range(2):
            A(hout[q], pB[:, q * BANK:(q + 1) * BANK], ACT.Copy).then_inc(hout_ready, 1)
        for j in range(HP):
            act.wait_ge(h0_tr, j + 1)
            wait(act, ys_mm, j)
            A(h0T[:, :, :].rearrange("p a b -> p (a b)"), acc_h0[:, :], ACT.Copy).then_inc(h0T_ready, 1)
            if j < SSD_G:
                decay(ST * SSD_G + j)

        def v_stats(h):
            act.wait_ge(vc_ready, h + 1)
            A(sq[:, :], tmp[1][:, :], ACT.Square).then_inc(vsq_ready, 1)
            act.wait_ge(vvar_ready, h + 1)
            A(stat[:, 3, :], stat[:, 2, :], ACT.Sqrt, bias=eps_t[:, 0:1], scale=1.0 / P).then_inc(vstd_ready, 1)

        def gm_hi_part(h):
            act.wait_ge(gmp_ready, h + 1)
            A(tile(gm_hi, h), gmp[:, :], ACT.Copy).then_inc(gmhi_ready, 1)

        def vu(i):
            first = not after_first(i)
            hi(U_V + 1, i)
            if first:
                for j in range(KD):
                    act.wait_ge(yz_ready, j + 1)
                    wait(act, sq_added, 2 * KD + j)
                    A(sq[:, :].rearrange("p (c n) -> p c n", c=TT), ytm3[:, :, j * P:(j + 1) * P], ACT.Square
                      ).then_inc(sq_ready, 1)
            else:
                v_stats(i - 1)
            done(U_V, i)
            wait(act, vt_tr, i)
            A(split2(tmp[0][:, :]), halves(acc[U_V % 2]), ACT.Gelu_apprx_tanh).then_inc(acc_free[U_V % 2], 1)
            hi(U_V + 2, i)
            if not first:
                gm_hi_part(i - 1)
            if first:
                for j in range(H0_RING):
                    act.wait_ge(h1_out[j], 16 * (HP // H0_RING))
            done(U_V + 1, i)
            A(split2(gu[:, :]), halves(acc[(U_V + 1) % 2]), ACT.Gelu_apprx_tanh).then_inc(acc_free[(U_V + 1) % 2], 1)
        vu(0)
        vu(1)
        repeat(act, None, 0, 2, KD, vu)

        hi(U_OG + 1)
        v_stats(KD - 1)
        gm_hi_part(KD - 1)
        hi(U_OG + 2)
        hi(U_OG + 3)
        rms_root(2)
        copy_r(2)
        for f in range(KD):
            act.wait_ge(yp_ready, f + 1)
            A(tile(hn_hi, f), tmp[f % 2][:, :], ACT.Copy).then_inc(yhi_ready, 1)
            if f % 2:
                hi(U_OG + f // 2 + 4)
        for u in (8, 9):
            hi(U_OG + u)
        for f in range(KD):
            if f:
                hi(U_OY + f + 1)
            if f == KD - 1:
                hi(U_F1 + 1)
            act.wait_ge(x_ready, x0[0] + f + 1)
            wait(act, sq_added, 3 * KD + f)
            A(sq[:, :], tile(xT, f), ACT.Square).then_inc(sq_ready, 1)
        x0[0] += KD
        rms_root(3)
        copy_r(3)
        norm(3, 0, 6 * KD)
        ffn(U_F1, FF_TILES, 4 * KD)
        rms_root(4)
        copy_r(4)
        act.wait_ge(mod_ready, 3)
        norm(4, 0, 9 * KD, y_fm)

    @block.vector
    def _(dve):
        V = nc.vector
        st = Steps(dve, dve_step)

        def lo(n, i=0):
            if isinstance(i, int) and n + 2 * i >= U_END:
                return
            p, w = n % 2, unit_tiles(n, i) * P
            dve.wait_ge(whi_done, i * 2 + (n + 1))
            V.tensor_tensor(out=wlo[p][:, 0:w], in0=wraw[p][:, 0:w], in1=whi[p][:, 0:w].bitcast(F32),
                            op=ALU.subtract).then_inc(wlo_done, 1)

        def done(n, i=0):
            dve.wait_ge(unit_done, i * 2 + (n + 1))

        def add_gated(n, i, f, q, count_x):
            done(n, i)
            g = by_group(split2(xadd[:, :]))
            V.tensor_tensor(out=g, in0=by_group(halves(acc[n % 2])), in1=mod40(q, f), op=ALU.mult
                            ).then_inc(acc_free[n % 2], 1)
            evacuated(dve, n, i)
            x = tile(xT, f)
            ins = V.tensor_tensor(out=x, in0=x, in1=xadd[:, :], op=ALU.add)
            if count_x:
                ins.then_inc(x_ready, 1)
            else:
                st.done(ins)

        def add_square(k, square=sq):
            dve.wait_ge(sq_ready, k + 1)
            V.tensor_tensor(out=ssum[:, :], in0=ssum[:, :], in1=square[:, :], op=ALU.add).then_inc(sq_added, 1)

        def r_of(m):
            dve.wait_ge(rms_sqrt, m + 1)
            st.done(V.reciprocal(out=rcol[:, :], in_=rcol[:, :]))
            V.tensor_tensor(out=sq[:, :].rearrange("p (c n) -> p c n", c=TT),
                            in0=ident[:, :].unsqueeze(1).broadcast_to([P, TT, P]),
                            in1=rcol[:, :].unsqueeze(2).broadcast_to([P, TT, P]), op=ALU.mult
                            ).then_inc(diag_ready, 1)

        def norm(m, shift, scale, to_hn=True):
            dve.wait_ge(rinv_ready, m + 1)

            def prod(f):
                V.scalar_tensor_tensor(out=tmp[f % 2][:, 0:SEQ], in0=xT[:, f * TOK:f * TOK + SEQ],
                                       scalar=modc[:, scale + f, 0:1], in1=rT[:, 0:SEQ],
                                       op0=ALU.mult, op1=ALU.mult).then_inc(prod_ready, 1)
            prod(0)
            for f in range(KD):
                if f == 1 and to_hn:
                    st.done(V.memset(ssum[:, :], 0.0))
                if f + 1 < KD:
                    if f >= 1:
                        dve.wait_ge(*((hn_ready, nhi0[0] + f) if to_hn else (of_ready, f)))
                    prod(f + 1)
                if not to_hn and f:
                    result(f - 1)
                if not to_hn:
                    continue
                dve.wait_ge(nhi_ready, nhi0[0] + f + 1)
                a, b, c = f * TOK, f * TOK + SEQ, (f + 1) * TOK
                V.scalar_tensor_tensor(out=hn_lo[:, a:b], in0=tmp[f % 2][:, 0:SEQ], scalar=modc[:, shift + f, 0:1],
                                       in1=hn_hi[:, a:b].bitcast(F32), op0=ALU.add, op1=ALU.subtract)
                V.tensor_tensor(out=hn_lo[:, b:c], in0=tms[f % 2][:, :], in1=hn_hi[:, b:c].bitcast(F32),
                                op=ALU.subtract).then_inc(hn_ready, 1)
            nhi0[0] += KD
        nhi0 = [0]

        dve.wait_ge(c_used, 1)
        V.tensor_tensor(out=c_hl[:, :, NSTR:2 * NSTR], in0=pB[:, 0:KD * NSTR].rearrange("p (k c) -> p k c", c=NSTR),
                        in1=c_hl[:, :, 0:NSTR].bitcast(F32), op=ALU.subtract).then_inc(c_split, 1)
        dve.wait_ge(par_tr, 1)
        V.tensor_copy(b_col[:, :], pB[:, BANK:BANK + MODT])
        st.done(V.tensor_copy(par[:, :], pB[:, BANK + P:BANK + P + N_PAR]))
        st.done(V.memset(ssum[:, :], 0.0))

        def chunk_lo(i, m, dst, raw, hi_half):
            dve.wait_ge(ch_hi, i + (m + 1 - ADA_FIRST))
            V.tensor_tensor(out=dst[:, :], in0=raw[:, :], in1=hi_half[:, :].bitcast(F32), op=ALU.subtract
                            ).then_inc(ch_lo, 1)

        def chunk_sum(i, m, bank):
            dve.wait_ge(ch_tr, i + (m + 1))
            b = b_col[:, bass.ds(i * 2 + 2 * m, 2)].unsqueeze(2).broadcast_to([P, 2, NSTR])
            V.tensor_tensor(out=modc[:, bass.ds(i * 2 + 2 * m, 2), :],
                            in0=ch_cols[bank].rearrange("p (f c) -> p f c", c=NSTR), in1=b, op=ALU.add
                            ).then_inc(ch_sum, 1)

        for m in range(1, ADA_FIRST, 2):
            dve.wait_ge(ada_hi_done, m // 2 + 1)
            V.tensor_tensor(out=ada_lo[m // 2 % 2][:, :], in0=ada_raw[m % ADA_RING][:, :],
                            in1=ada_hi[m // 2 % 2][:, :].bitcast(F32), op=ALU.subtract).then_inc(ada_lo_done, 1)
            if m > 1:
                chunk_sum(0, m - 3, (m - 3) % 2)
                chunk_sum(0, m - 2, (m - 2) % 2)
            for f in (m - 1, m):
                if f:
                    dve.wait_ge(sq_added, f)
                add_square(f, tmp[f % 2])
        lo(U_F0)
        chunk_sum(0, ADA_FIRST - 2, 0)
        r_of(0)
        lo(U_F0 + 1)
        chunk_sum(0, ADA_FIRST - 1, 1)

        def norm_scale(row, scale):
            g = par[:, row:row + KD].unsqueeze(2).broadcast_to([P, KD, NSTR])
            v = modc[:, scale:scale + KD, :]
            return V.scalar_tensor_tensor(out=v, in0=v, scalar=1.0, in1=g, op0=ALU.add, op1=ALU.mult)

        def spread_gate(q, factor):
            v = modc[:, (3 * q + 2) * KD:(3 * q + 3) * KD, :]
            g = gate[:, q, :].rearrange("p (f g) -> p f g", f=KD)
            V.tensor_scalar(out=g[:, :, 0:GRP - DEC_BATCH],
                            in0=v[:, :, 0:1].broadcast_to([P, KD, GRP - DEC_BATCH]),
                            scalar1=factor, scalar2=None, op0=ALU.mult)
            st.done(V.tensor_scalar(out=g[:, :, GRP - DEC_BATCH:GRP], in0=v[:, :, 1:NSTR],
                                    scalar1=factor, scalar2=None, op0=ALU.mult))

        dve.wait_ge(ch_sum, ADA_FIRST)
        norm_scale(R_NORM, KD).then_inc(mod_ready, 1)

        def ffn(u0, q, t0, sq0):
            first_one = u0 == U_F0
            for part, kh in enumerate(PARTS):
                n = part_unit(u0, part)
                h0 = t0 + PART0[part]

                def pair(i, n=n, h0=h0, chunk=None):
                    if chunk is not None:
                        chunk_lo(i, chunk, slo, sraw, shi)
                    if after_first(i) or n != u0:
                        lo(n + 1, i)
                    lo(n + 2, i)
                    done(n + 1, i)
                    evacuated(dve, n, i)
                    wait(dve, hid_ready, i + h0)
                    V.tensor_tensor(out=split2(hidp[:, :]), in0=split2(silg[:, :]), in1=halves(acc[(n + 1) % 2]),
                                    op=ALU.mult).then_inc(acc_free[(n + 1) % 2], 1)
                    dve.wait_ge(hhi_ready, i + (h0 + 1))
                    V.tensor_tensor(out=tile(hid_lo, i), in0=hidp[:, :], in1=tile(hid_hi, i).bitcast(F32),
                                    op=ALU.subtract).then_inc(hid_ready, 1)
                    if chunk is not None:
                        chunk_sum(i, chunk, 0)
                have, chunk = chunks_of(u0, part)
                if have:
                    repeat_peeled(dve, min(have, kh - 1), lambda i: pair(i, chunk=chunk), n)
                if have < kh - 1:
                    repeat(dve, None, 0, have, kh - 1, pair)
                pair(kh - 1, chunk=chunk if have == kh else None)
                n += 2 * kh
                if first_one and part == 0:
                    dve.wait_ge(ch_sum, 3 * KD // 2)
                    spread_gate(0, 0.5)
                if first_one and part == 2:
                    dve.wait_ge(ch_sum, ADA_MAIN)
                    spread_gate(1, 1.0)
                    spread_gate(2, 0.5)
                    for row, scale in ((R_NORM + KD, 4 * KD), (R_NORM + 2 * KD, 7 * KD)):
                        ins = norm_scale(row, scale)
                    ins.then_inc(mod_ready, 1)
                if not first_one and part == 0:
                    dve.wait_ge(ch_sum, ADA_ALL)
                    norm_scale(R_FINAL, 10 * KD).then_inc(mod_ready, 1)
                last = part == 2

                def down(i, n=n, last=last, part=part):
                    chunk = CH_DOWN[part] if first_one and part < 2 else None
                    if chunk is not None:
                        chunk_lo(i, chunk, slo, sraw, shi)
                    for d in range(2):
                        lo(n + d + 1, i)
                        add_gated(n + d, i, i * 2 + d, q, last)
                        if last:
                            add_square(i * 2 + (sq0 + d))
                    if chunk is not None:
                        chunk_sum(i, chunk, 0)
                repeat(dve, st, 0 if last else 2, 0, KD // 2 - 1, down)
                down(KD // 2 - 1)

        dve.wait_ge(mod_ready, 1)
        norm(0, 0, KD)
        ffn(U_F0, 0, 0, KD)
        r_of(1)
        lo(U_DT + 1)
        norm(1, 3 * KD, 4 * KD)

        dve.wait_ge(st_done, 1)

        def xbc(n, i, j):
            b = j % 2
            V.tensor_copy(by_stream(xpad[b][:, PAD_P:PAD], PAD_S)[:, :, 0:3],
                          stT[:, bass.ds(i * 2 + j, 1), :].rearrange("p a (b k) -> p (a b) k", k=3))
            evacuated(dve, n, i)
            t = tails[:, bass.ds(i * 2 + j, 1), :].rearrange("p a r -> p (a r)")
            V.tensor_copy(t[:, 0:3], xpad[b][:, SEQ:PAD_P])
            st.done(V.tensor_copy(t[:, 3:TAIL].rearrange("p (b k) -> p b k", k=3),
                                  by_stream(xpad[b][:, PAD_P:PAD], PAD_S)[:, :, DEC_SEQ:PAD_S]))
            wait(dve, xcv_ready, i * 2 + j)
            w = [par[:, bass.ds(i * 2 + (R_CW + k * CT + j), 1)] for k in range(CONV_W)]
            st.done(V.tensor_scalar(out=cacc[:, 0:CONV_N], in0=xpad[b][:, 0:CONV_N], scalar1=w[0],
                                    scalar2=par[:, bass.ds(i * 2 + (R_CB + j), 1)], op0=ALU.mult, op1=ALU.add))
            for k in range(1, CONV_W):
                ins = V.scalar_tensor_tensor(out=cacc[:, 0:CONV_N], in0=xpad[b][:, k:k + CONV_N], scalar=w[k],
                                             in1=cacc[:, 0:CONV_N], op0=ALU.mult, op1=ALU.add)
                if k + 1 < CONV_W:
                    st.done(ins)
            ins.then_inc(conv_done, 1)
            lo(n + 2, i)

        def x_pair(i):
            xbc(U_X, i, 0)
            xbc(U_X + 1, i, 1)
        dve.wait_ge(pad0_ready, 2)
        st.done(V.memset(cacc[:, CONV_N:PAD], 0.0))
        lo(U_X + 1)
        x_pair(0)
        repeat(dve, st, 8, 1, XT_ // 2, x_pair)
        per_head = [vecs[:, q, :].unsqueeze(1).broadcast_to([P, TT, HEADS]) for q in range(3)]
        by_tile = lambda t: t[:, :].rearrange("p (c h) -> p c h", h=HEADS)
        for j in range(XT_, CT):
            if j == DT_AT:
                dve.wait_ge(dt_tr, 1)
                V.tensor_tensor(out=by_tile(dt_z),
                                in0=pC[:, 0:TT * 32].rearrange("p (c h) -> p c h", h=32)[:, :, 16:32],
                                in1=per_head[0], op=ALU.add).then_inc(dt_z_ready, 1)
                st.done(V.tensor_scalar(out=vecs[:, 1, :], in0=vecs[:, 1, :], scalar1=-1.0, scalar2=None,
                                        op0=ALU.mult))
            if j == DT_AT + 1:
                dve.wait_ge(dt_e_ready, 1)
                st.done(V.scalar_tensor_tensor(out=dt_v[:, :], in0=dt_z[:, :], scalar=0.0, in1=dt_e[:, :],
                                               op0=ALU.max, op1=ALU.add))
                st.done(V.tensor_tensor(out=by_tile(dt_a), in0=by_tile(dt_v), in1=per_head[1], op=ALU.mult))
            xbc(U_X + j, 0, j)
        heads = lambda ap: ap.rearrange("p (h x) -> p h x", x=HDIM)
        wide = lambda ap: ap.unsqueeze(2).broadcast_to([P, HG, HDIM])

        def parts(s):
            c, g = divmod(s, SSD_G)
            return c, g, c * HEADS + g * HG, ytm3[:, c, g * BANK:(g + 1) * BANK]

        def make_wd(s):
            c, g, h0, x = parts(s)
            wait(dve, seg_done, s)
            V.tensor_tensor(out=wd[:, :, :], in0=upto[:, int(c == ST), :].unsqueeze(1).broadcast_to([P, HG, P]),
                            in1=dt_a[:, h0:h0 + HG].unsqueeze(2).broadcast_to([P, HG, P]), op=ALU.mult
                            ).then_inc(wd_ready, 1)

        def make_xdt(s):
            c, g, h0, x = parts(s)
            wait(dve, y_mm, s)
            st.done(V.tensor_tensor(out=heads(xdt), in0=heads(x), in1=wide(dt_v[:, h0:h0 + HG]), op=ALU.mult))
            V.tensor_tensor(out=heads(xds), in0=heads(xdt), in1=wide(expo[:, 1, h0:h0 + HG]), op=ALU.mult)

        def make_g(s):
            c, g, h0, x = parts(s)
            dve.wait_ge(gexp_done, s + 1)
            V.tensor_tensor(out=gd[:, :, :], in0=gd[:, :, :], in1=cbm[:, s, :].unsqueeze(1).broadcast_to([P, HG, P]),
                            op=ALU.mult).then_inc(g_ready, 1)
            wait(dve, y_done, s)
            ins = V.tensor_tensor(out=heads(yt2), in0=heads(x), in1=wide(vecs[:, 2, g * HG:(g + 1) * HG]),
                                  op=ALU.mult)
            if c == 0:
                st.done(ins)

        def add_before(s):
            c, g, h0, x = parts(s)
            V.tensor_tensor(out=heads(yt1), in0=heads(pC[:, BANK:2 * BANK]), in1=wide(expo[:, 0, h0:h0 + HG]),
                            op=ALU.mult).then_inc(yo_used, 1)
            dve.wait_ge(yo_used, s + 1 - SSD_G)
            st.done(V.tensor_tensor(out=yt2, in0=yt2, in1=yt1, op=ALU.add))

        def add_within(s):
            c, g, h0, x = parts(s)
            dve.wait_ge(y_mm, s + 1)
            V.tensor_tensor(out=x, in0=yt2, in1=pC[:, 0:BANK], op=ALU.add).then_inc(y_done, 1)

        V.tensor_copy(gd[:, :, :].rearrange("p a (b x) -> p (a b) x", x=HDIM),
                      dt_a[:, ST * HEADS:TT * HEADS].unsqueeze(2).broadcast_to([P, HEADS, HDIM])
                      ).then_inc(wd_ready, 1)
        make_wd(0)
        dve.wait_ge(cb_done, 1)
        n_p = ST * SSD_G
        for a, b, src in ((0, n_p, pB[:, :]), (n_p, TT * SSD_G, pC[:, BANK:BANK + SSD_G * P])):
            V.tensor_tensor(out=cbm[:, a:b, :], in0=src.rearrange("p (s n) -> p s n", n=P),
                            in1=upto[:, int(a > 0), :].unsqueeze(1).broadcast_to([P, b - a, P]), op=ALU.mult
                            ).then_inc(cbm_done, 1)
        dve.wait_ge(expo_ready, 1)
        for s in range(ST * SSD_G):
            c, g, h0, x = parts(s)
            wait(dve, st_mm, s)
            make_xdt(s)
            make_wd(s + 1)
            make_g(s)
            if c:
                dve.wait_ge(yo_mm, s + 1 - SSD_G)
                add_before(s)
            if s + 2 < KD:
                lo(U_Z + s + 2)
            add_within(s)
            hs = hst[:, g * BANK:(g + 1) * BANK]
            if c:
                st.done(V.tensor_tensor(out=heads(hs), in0=heads(hs), in1=wide(expo[:, 2, h0:h0 + HG]), op=ALU.mult))
            elif s == 0:
                dve.wait_ge(tail_out, 32)
            dve.wait_ge(st_mm, s + 1)
            if c:
                V.tensor_tensor(out=hs, in0=hs, in1=pC[:, BANK:2 * BANK], op=ALU.add).then_inc(hst_ready, 1)
            else:
                V.tensor_copy(hs, pC[:, BANK:2 * BANK]).then_inc(hst_ready, 1)

        lo(U_V)

        def make_bblk(g):
            V.tensor_tensor(out=bblk.rearrange("p (b n) -> p b n", n=NSTATE),
                            in0=btm[:, ST, g * P:(g + 1) * P].unsqueeze(1).broadcast_to([P, DEC_BATCH, NSTATE]),
                            in1=stream_of[:, :].unsqueeze(2).broadcast_to([P, DEC_BATCH, NSTATE]), op=ALU.mult
                            ).then_inc(bblk_ready, 1)

        def make_cblk(g):
            step = P + DEC_SEQ
            n = (DEC_BATCH - 1) * step
            C = bcf[:, SSD_G + g, SEQ:TOK]
            V.tensor_copy(hst[:, 0:n].rearrange("p (b t) -> p b t", t=step)[:, :, 0:DEC_SEQ],
                          by_stream(C)[:, 0:DEC_BATCH - 1, :])
            V.tensor_copy(hst[:, n:n + DEC_SEQ], C[:, P - DEC_SEQ:P]).then_inc(cblk_ready, 1)

        s = ST * SSD_G
        dve.wait_ge(st_mm, s)
        make_xdt(s)
        make_bblk(0)
        dve.wait_ge(hout_tr, 1)
        st.done(V.memset(hst[:, :], 0.0))
        make_cblk(0)
        make_g(s)
        make_wd(s + 1)
        for j in range(HP):
            g, jj = divmod(j, HP // SSD_G)
            h = h0s[j % H0_RING][:, :, :]
            dve.wait_ge(h0_tr, j + 1)
            st.done(V.tensor_tensor(out=h, in0=h, in1=decs[:, j, :].unsqueeze(2).broadcast_to([P, DEC_BATCH, NSTATE]),
                                    op=ALU.mult))
            dve.wait_ge(h1_mm, j + 1)
            last_of_first = j + 1 == HP // SSD_G
            if last_of_first:
                make_xdt(s + 1)
                make_bblk(1)
            V.tensor_tensor(out=h, in0=h, in1=acc_h1[:, :].rearrange("p (b n) -> p b n", n=NSTATE), op=ALU.add
                            ).then_inc(h1_ready, 1)
            if jj + 1 == HP // SSD_G:
                dve.wait_ge(ys_mm, j + 1)
                if last_of_first:
                    make_cblk(1)
                add_before(s + g)
                add_within(s + g)
                if last_of_first:
                    make_g(s + 1)
        dve.wait_ge(y_done, TT * SSD_G)
        dve.wait_ge(h1_ready, HP)
        V.memset(dt_e[:, 0:1], 0.0).then_inc(ssd_over, 1)
        V.memset(wsb[:, :, :], 0.0).then_inc(ws_zero, 1)

        lo(U_V + 1)
        dve.wait_ge(hout_out, 32)
        st.done(V.memset(ssum[:, :], 0.0))
        for j in range(KD):
            dve.wait_ge(yt_tr, j + 1)
            V.tensor_tensor(out=ytm3[:, :, j * P:(j + 1) * P],
                            in0=(pB, pC)[j % 2][:, 0:TOK].rearrange("p (c n) -> p c n", c=TT),
                            in1=zs3[:, j, :, :], op=ALU.mult).then_inc(yz_ready, 1)
            if j:
                add_square(2 * KD + j - 1)
        add_square(3 * KD - 1)
        lo(U_V + 2)

        for i in range(H0_RING):
            dve.wait_ge(h1_out[i], 16 * (HP // H0_RING))
        dve.wait_ge(ws_tr, 1)
        for kind, src in enumerate((pB, pC)):
            V.tensor_tensor(out=wmT[:, kind, :].rearrange("p (h t) -> p h t", t=P),
                            in0=src[:, :].rearrange("p (h t) -> p h t", t=P),
                            in1=upto[:, kind, :].unsqueeze(1).broadcast_to([P, 8, P]), op=ALU.mult
                            ).then_inc(wm_ready, 1)
        dve.wait_ge(gm_vec_in, 32)

        def v_norm(h, between=None):
            pv = pB[:, 0:TOK].rearrange("p (c n) -> p c n", c=TT)
            vc = tmp[1][:, :].rearrange("p (c n) -> p c n", c=TT)
            vn = xadd[:, :].rearrange("p (c n) -> p c n", c=TT)
            dve.wait_ge(vt_tr, h + 1)
            st.done(V.tensor_reduce(out=stat[:, 0, :], in_=pv, axis=AX.X, op=ALU.add))
            st.done(V.tensor_scalar(out=stat[:, 1, :], in0=stat[:, 0, :], scalar1=-1.0 / P, scalar2=None, op0=ALU.mult))
            V.tensor_tensor(out=vc, in0=pv, in1=stat[:, 1, :].unsqueeze(2).broadcast_to([P, TT, P]), op=ALU.add
                            ).then_inc(vc_ready, 1)
            if between:
                between()
            dve.wait_ge(vsq_ready, h + 1)
            V.tensor_reduce(out=stat[:, 2, :], in_=sq[:, :].rearrange("p (c n) -> p c n", c=TT), axis=AX.X, op=ALU.add
                            ).then_inc(vvar_ready, 1)
            dve.wait_ge(vstd_ready, h + 1)
            st.done(V.reciprocal(out=stat[:, 0, :], in_=stat[:, 3, :]))
            wait(dve, v_out, h * 16)
            wait(dve, mix_mm, h)
            st.done(V.tensor_tensor(out=vn, in0=vc, in1=stat[:, 0, :].unsqueeze(2).broadcast_to([P, TT, P]), op=ALU.mult))
            V.tensor_tensor(out=vn, in0=vn, in1=gm_g[:, bass.ds(h * P, P)].unsqueeze(1).broadcast_to([P, TT, P]),
                            op=ALU.mult).then_inc(vn_ready, 1)

        def gm_out(h):
            bias = gm_bias[:, bass.ds(h * P, P)]
            dve.wait_ge(mix_mm, h + 1)
            V.tensor_tensor(out=gmp[:, 0:SEQ].rearrange("p (c t) -> p c t", c=ST),
                            in0=pC[:, 0:SEQ].rearrange("p (c t) -> p c t", c=ST),
                            in1=bias.unsqueeze(1).broadcast_to([P, ST, P]), op=ALU.add)
            V.tensor_tensor(out=by_stream(gmp[:, SEQ:TOK]), in0=by_stream(pC[:, SEQ:TOK]),
                            in1=bias[:, 0:DEC_SEQ].unsqueeze(1).broadcast_to([P, DEC_BATCH, DEC_SEQ]), op=ALU.add
                            ).then_inc(mix_used, 1)
            dve.wait_ge(mix_used, h + 1)
            evacuated(dve, U_V + 1, h)
            V.tensor_tensor(out=gmp[:, :], in0=gmp[:, :], in1=gu[:, :], op=ALU.mult).then_inc(gmp_ready, 1)
            dve.wait_ge(gmhi_ready, h + 1)
            V.tensor_tensor(out=tile(gm_lo, h), in0=gmp[:, :], in1=tile(gm_hi, h).bitcast(F32), op=ALU.subtract
                            ).then_inc(gm_ready, 1)

        def vu(i):
            v_norm(i - 1, lambda: lo(U_V + 1, i))
            lo(U_V + 2, i)
            gm_out(i - 1)
        vu(1)
        repeat(dve, st, 4, 2, KD, vu)

        v_norm(KD - 1, lambda: lo(U_OG + 1))
        gm_out(KD - 1)
        lo(U_OG + 2)
        dve.wait_ge(v_out, 16 * KD)
        add_gated(U_OG, 0, 0, 1, False)
        lo(U_OG + 3)
        add_gated(U_OG + 1, 0, 1, 1, False)
        r_of(2)
        dve.wait_ge(rinv_ready, 3)
        for f in range(KD):
            wait(dve, yfm_split, f - 1)
            if f == 1:
                st.done(V.memset(ssum[:, :], 0.0))
            v3 = tmp[f % 2][:, :].rearrange("p (c n) -> p c n", c=TT)
            V.scalar_tensor_tensor(out=v3, in0=ytm3[:, :, f * P:(f + 1) * P], scalar=par[:, R_SSDN + f:R_SSDN + f + 1],
                                   in1=rT[:, :].rearrange("p (c n) -> p c n", c=TT), op0=ALU.mult, op1=ALU.mult
                                   ).then_inc(yp_ready, 1)
            dve.wait_ge(yhi_ready, f + 1)
            V.tensor_tensor(out=tile(hn_lo, f), in0=tmp[f % 2][:, :], in1=tile(hn_hi, f).bitcast(F32), op=ALU.subtract
                            ).then_inc(yfm_split, 1)
            if f % 2:
                u = f // 2 + 2
                lo(U_OG + u + 2)
                add_gated(U_OG + u, 0, u, 1, False)
        for u in (6, 7):
            lo(U_OG + u + 2)
            add_gated(U_OG + u, 0, u, 1, False)
        for f in range(KD):
            if f:
                lo(U_OY + f + 1)
            add_gated(U_OY + f, 0, f, 1, True)
            add_square(3 * KD + f)
        r_of(3)
        lo(U_F1 + 1)
        norm(3, 6 * KD, 7 * KD)
        ffn(U_F1, 2, FF_TILES, 4 * KD)
        r_of(4)
        dve.wait_ge(mod_ready, 3)

        def result(f):
            dve.wait_ge(of_tr, f + 1)
            V.tensor_copy(y_row[:, :, f * P:(f + 1) * P], acc[f % 2][:, 0:TOK].rearrange("p (c n) -> p c n", c=TT)
                          ).then_inc(of_done, 1)
        norm(4, 9 * KD, 10 * KD, to_hn=False)
        result(KD - 1)

    top.close()


_INPUTS = ("x_prompt", "x_sample", "state_ssm", "state_conv", "c_prompt", "c_sample", "w_ada", "b_ada", "norm_g",
           "ffn_w1", "ffn_w2", "w_in", "gm_norm_g", "gm_ws", "gm_b", "conv_w", "conv_b", "dt_bias", "a_log",
           "d_skip", "ssd_norm_g", "w_out", "final_norm_g", "w_ada_final", "b_ada_final")
_OUTPUTS = (("y_prompt", (1, SEQ, D_MODEL)), ("y_sample", (DEC_BATCH, DEC_SEQ, D_MODEL)),
            ("ssm_prompt", (1, 1, HEADS, HDIM, NSTATE)), ("conv_prompt", (1, 1, CONV_W - 1, CONV_DIM)),
            ("ssm_sample", (1, DEC_BATCH, HEADS, HDIM, NSTATE)),
            ("conv_sample", (1, DEC_BATCH, CONV_W - 1, CONV_DIM)),
            ("gm_v_sample", (1, DEC_BATCH, DEC_SEQ, D_MODEL)))


def kernel(**inputs):
    import numpy as np
    import concourse.bacc as bacc
    from concourse.bass_utils import run_bass_kernel_spmd

    nc = bacc.Bacc("TRN2", target_bir_lowering=False, num_devices=1)
    arrays, args = {}, []
    for name in _INPUTS:
        a = np.ascontiguousarray(inputs[name])
        arrays[f"in_{name}"] = a
        args.append(nc.dram_tensor(f"in_{name}", a.shape, mybir.dt.from_np(a.dtype), kind="ExternalInput").ap())
    for name, shape in _OUTPUTS:
        args.append(nc.dram_tensor(f"out_{name}", shape, F32, kind="ExternalOutput").ap())
    trunk_program(nc, *args)
    r = run_bass_kernel_spmd(nc, [arrays], core_ids=[0])
    return tuple(r.results[0][f"out_{name}"] for name, _ in _OUTPUTS)
```
